# Optimizing a Trainium2 kernel written in Bass

```python
import math
import jax, jax.numpy as jnp
from jax import lax
import numpy as np

D_MODEL = 1024
BATCH = 1
SEQ = 256
DEPTH = 2

N_HEADS_MLA = 8
MLA_QK_NOPE = 64
MLA_QK_ROPE = 32
MLA_V = 64
MLA_Q_RANK = 768
MLA_KV_RANK = 256
MLA_QK = MLA_QK_NOPE + MLA_QK_ROPE

N_HEADS_SB = 8
SB_HEAD = 64

N_HEADS_MOBA = 8
MOBA_HEAD = 64
MOBA_BLOCK = 256
MOBA_TOPK = 3
MOBA_Q_CHUNK = 32

Q_BLOCK = 128
ROPE_THETA = 500000.0
PARTIAL_ROPE_DIM = MOBA_HEAD // 4
D_FF = 4 * D_MODEL
N_BRANCH = 3
EPS = 1e-6
NEG_INF = -1e30

W_MLA = N_HEADS_MLA * MLA_V
W_SB = N_HEADS_SB * SB_HEAD
W_MOBA = N_HEADS_MOBA * MOBA_HEAD

IN_SPLITS = (MLA_Q_RANK, MLA_KV_RANK, MLA_QK_ROPE, 3 * W_SB, 3 * W_MOBA, N_BRANCH * D_MODEL)
D_IN = sum(IN_SPLITS)
SPLIT_POINTS = [int(v) for v in np.cumsum(IN_SPLITS)[:-1]]


def rmsnorm(x, g):
    xf = x.astype(jnp.float32)
    y = xf * lax.rsqrt(jnp.mean(xf * xf, axis=-1, keepdims=True) + EPS)
    return y.astype(x.dtype) * g

def modulate(h, shift, scale):
    return h * (1.0 + scale[:, None, :]) + shift[:, None, :]

def rope_tables(positions, rot_dim, dtype):
    inv = ROPE_THETA ** (-jnp.arange(0, rot_dim, 2, dtype=jnp.float32) / rot_dim)
    ang = positions.astype(jnp.float32)[..., None] * inv
    return jnp.cos(ang)[:, None].astype(dtype), jnp.sin(ang)[:, None].astype(dtype)

def apply_rope(x, cos, sin):
    rd = 2 * cos.shape[-1]
    xr, xp = x[..., :rd], x[..., rd:]
    x1, x2 = xr[..., : rd // 2], xr[..., rd // 2:]
    rot = jnp.concatenate([x1 * cos - x2 * sin, x1 * sin + x2 * cos], axis=-1)
    return jnp.concatenate([rot, xp], axis=-1)

def to_heads(t, n_heads):
    b, s, w = t.shape
    return t.reshape(b, s, n_heads, w // n_heads).transpose(0, 2, 1, 3)

def from_heads(t):
    b, h, s, d = t.shape
    return t.transpose(0, 2, 1, 3).reshape(b, s, h * d)

def causal_softmax_attention(q, k, v, scale):
    b, h, s, dq = q.shape
    nq = s // Q_BLOCK
    qb = jnp.moveaxis(q.reshape(b, h, nq, Q_BLOCK, dq), 2, 0)
    kpos = jnp.arange(s)

    def body(args):
        qi, i = args
        sc = jnp.einsum('bhqd,bhkd->bhqk', qi, k).astype(jnp.float32) * scale
        qpos = i * Q_BLOCK + jnp.arange(Q_BLOCK)
        sc = jnp.where(kpos[None, :] <= qpos[:, None], sc, NEG_INF)
        p = jax.nn.softmax(sc, axis=-1).astype(v.dtype)
        return jnp.einsum('bhqk,bhkd->bhqd', p, v)

    o = lax.map(body, (qb, jnp.arange(nq)))
    return jnp.moveaxis(o, 0, 2).reshape(b, h, s, v.shape[-1])

def stick_breaking_attention(q, k, v):
    b, h, s, d = q.shape
    scale = 1.0 / math.sqrt(d)
    nq = s // Q_BLOCK
    qb = jnp.moveaxis(q.reshape(b, h, nq, Q_BLOCK, d), 2, 0)
    kpos = jnp.arange(s)

    def body(args):
        qi, i = args
        z = jnp.einsum('bhqd,bhkd->bhqk', qi, k).astype(jnp.float32) * scale
        qpos = i * Q_BLOCK + jnp.arange(Q_BLOCK)
        past = kpos[None, :] < qpos[:, None]
        log_beta = jax.nn.log_sigmoid(z)
        log_keep = jnp.where(past, jax.nn.log_sigmoid(-z), 0.0)
        later = lax.cumsum(log_keep, axis=3, reverse=True) - log_keep
        a = jnp.where(past, jnp.exp(log_beta + later), 0.0).astype(v.dtype)
        return jnp.einsum('bhqk,bhkd->bhqd', a, v)

    o = lax.map(body, (qb, jnp.arange(nq)))
    return jnp.moveaxis(o, 0, 2).reshape(b, h, s, d)

def moba_attention(q, k, v):
    b, h, s, d = q.shape
    scale = 1.0 / math.sqrt(d)
    nb = -(-s // MOBA_BLOCK)
    pad = nb * MOBA_BLOCK - s
    kb = jnp.pad(k, ((0, 0), (0, 0), (0, pad), (0, 0))).reshape(b, h, nb, MOBA_BLOCK, d)
    vb = jnp.pad(v, ((0, 0), (0, 0), (0, pad), (0, 0))).reshape(b, h, nb, MOBA_BLOCK, d)
    kmean = jnp.mean(kb.astype(jnp.float32), axis=3)

    cur = jnp.arange(s) // MOBA_BLOCK
    gate = jnp.einsum('bhsd,bhnd->bhsn', q.astype(jnp.float32), kmean)
    past_blk = jnp.arange(nb)[None, :] < cur[:, None]
    gate = jnp.where(past_blk, gate, NEG_INF)
    topk = min(MOBA_TOPK, nb)
    _, idx = lax.top_k(gate, topk)
    valid = jnp.arange(topk)[None, :] < cur[:, None]

    nc = s // MOBA_Q_CHUNK
    qc = jnp.moveaxis(q.reshape(b, h, nc, MOBA_Q_CHUNK, d), 2, 0)
    ic = jnp.moveaxis(idx.reshape(b, h, nc, MOBA_Q_CHUNK, topk), 2, 0)
    vc = valid.reshape(nc, MOBA_Q_CHUNK, topk)
    gather = jax.vmap(jax.vmap(lambda blocks, ids: blocks[ids]))

    def body(args):
        qi, ii, vi, ci = args
        kg = gather(kb, ii)
        vg = gather(vb, ii)
        qpos = ci * MOBA_Q_CHUNK + jnp.arange(MOBA_Q_CHUNK)
        s_sel = jnp.einsum('bhqd,bhqnjd->bhqnj', qi, kg).astype(jnp.float32) * scale
        s_sel = jnp.where(vi[:, :, None], s_sel, NEG_INF).reshape(b, h, MOBA_Q_CHUNK, topk * MOBA_BLOCK)
        ob = (ci * MOBA_Q_CHUNK) // MOBA_BLOCK
        k_own = lax.dynamic_index_in_dim(kb, ob, axis=2, keepdims=False)
        v_own = lax.dynamic_index_in_dim(vb, ob, axis=2, keepdims=False)
        s_own = jnp.einsum('bhqd,bhjd->bhqj', qi, k_own).astype(jnp.float32) * scale
        kpos = ob * MOBA_BLOCK + jnp.arange(MOBA_BLOCK)
        s_own = jnp.where(kpos[None, :] <= qpos[:, None], s_own, NEG_INF)
        p = jax.nn.softmax(jnp.concatenate([s_sel, s_own], axis=-1), axis=-1).astype(v.dtype)
        p_sel = p[..., : topk * MOBA_BLOCK].reshape(b, h, MOBA_Q_CHUNK, topk, MOBA_BLOCK)
        p_own = p[..., topk * MOBA_BLOCK:]
        return (jnp.einsum('bhqnj,bhqnjd->bhqd', p_sel, vg)
                + jnp.einsum('bhqj,bhjd->bhqd', p_own, v_own))

    o = lax.map(body, (qc, ic, vc, jnp.arange(nc)))
    return jnp.moveaxis(o, 0, 2).reshape(b, h, s, d)

def first_inputs(seed: int = 0) -> dict:
    key = jax.random.key(seed)
    ks = jax.random.split(key, 24)
    f32 = jnp.float32

    def nrm(k, shape, fan_in):
        return jax.random.normal(k, shape, f32) * (fan_in ** -0.5)

    def gain(k, shape):
        return 1.0 + 0.02 * jax.random.normal(k, shape, f32)

    L = DEPTH
    return {
        "x": jax.random.normal(ks[0], (BATCH, SEQ, D_MODEL), f32),
        "c": jax.random.normal(ks[1], (BATCH, D_MODEL), f32),
        "positions": jnp.broadcast_to(jnp.arange(SEQ, dtype=jnp.int32)[None, :], (BATCH, SEQ)),
        "w_ada": nrm(ks[2], (L, D_MODEL, 6 * D_MODEL), D_MODEL),
        "b_ada": 0.02 * jax.random.normal(ks[3], (L, 6 * D_MODEL), f32),
        "norm1_g": gain(ks[4], (L, D_MODEL)),
        "norm2_g": gain(ks[5], (L, D_MODEL)),
        "w_in": nrm(ks[6], (L, D_MODEL, D_IN), D_MODEL),
        "q_norm_g": gain(ks[7], (L, MLA_Q_RANK)),
        "w_uq": nrm(ks[8], (L, MLA_Q_RANK, N_HEADS_MLA * MLA_QK), MLA_Q_RANK),
        "kv_norm_g": gain(ks[9], (L, MLA_KV_RANK)),
        "w_ukv": nrm(ks[10], (L, MLA_KV_RANK, N_HEADS_MLA * (MLA_QK_NOPE + MLA_V)), MLA_KV_RANK),
        "w_o_mla": nrm(ks[11], (L, W_MLA, D_MODEL), W_MLA),
        "w_o_sb": nrm(ks[12], (L, W_SB, D_MODEL), W_SB),
        "w_o_moba": nrm(ks[13], (L, W_MOBA, D_MODEL), W_MOBA),
        "w_out": nrm(ks[14], (L, D_MODEL, D_MODEL), D_MODEL),
        "w_ff1": nrm(ks[15], (L, D_MODEL, D_FF), D_MODEL),
        "w_ff2": nrm(ks[16], (L, D_FF, D_MODEL), D_FF),
        "final_norm_g": gain(ks[17], (D_MODEL,)),
    }

def first_block(x, c, positions, w_ada, b_ada, norm1_g, norm2_g, w_in, q_norm_g, w_uq,
              kv_norm_g, w_ukv, w_o_mla, w_o_sb, w_o_moba, w_out, w_ff1, w_ff2, final_norm_g):
    b, s, _ = x.shape
    cos_mla, sin_mla = rope_tables(positions, MLA_QK_ROPE, x.dtype)
    cos_mb, sin_mb = rope_tables(positions, PARTIAL_ROPE_DIM, x.dtype)
    c_act = jax.nn.silu(c)
    mla_scale = 1.0 / math.sqrt(MLA_QK)

    for l in range(DEPTH):
        mod = c_act @ w_ada[l] + b_ada[l]
        shift1, scale1, gate1, shift2, scale2, gate2 = jnp.split(mod, 6, axis=-1)

        hdn = modulate(rmsnorm(x, norm1_g[l]), shift1, scale1)
        proj = hdn @ w_in[l]
        q_lat, c_kv, k_pe, sb_qkv, mb_qkv, gates = jnp.split(proj, SPLIT_POINTS, axis=-1)

        q = to_heads(rmsnorm(q_lat, q_norm_g[l]) @ w_uq[l], N_HEADS_MLA)
        q_nope, q_pe = q[..., :MLA_QK_NOPE], q[..., MLA_QK_NOPE:]
        kv = to_heads(rmsnorm(c_kv, kv_norm_g[l]) @ w_ukv[l], N_HEADS_MLA)
        k_nope, v_mla = kv[..., :MLA_QK_NOPE], kv[..., MLA_QK_NOPE:]
        q_pe = apply_rope(q_pe, cos_mla, sin_mla)
        k_pe = apply_rope(k_pe[:, None], cos_mla, sin_mla)
        q_mla = jnp.concatenate([q_nope, q_pe], axis=-1)
        k_mla = jnp.concatenate([k_nope, jnp.broadcast_to(k_pe, k_nope.shape[:3] + (MLA_QK_ROPE,))], axis=-1)
        o_mla = from_heads(causal_softmax_attention(q_mla, k_mla, v_mla, mla_scale))

        q_sb, k_sb, v_sb = [to_heads(t, N_HEADS_SB) for t in jnp.split(sb_qkv, 3, axis=-1)]
        o_sb = from_heads(stick_breaking_attention(q_sb, k_sb, v_sb))

        q_mb, k_mb, v_mb = [to_heads(t, N_HEADS_MOBA) for t in jnp.split(mb_qkv, 3, axis=-1)]
        q_mb = apply_rope(q_mb, cos_mb, sin_mb)
        k_mb = apply_rope(k_mb, cos_mb, sin_mb)
        o_mb = from_heads(moba_attention(q_mb, k_mb, v_mb))

        g_a, g_b, g_c = jnp.split(jax.nn.sigmoid(gates), N_BRANCH, axis=-1)
        merged = (g_a * (o_mla @ w_o_mla[l]) + g_b * (o_sb @ w_o_sb[l])
                  + g_c * (o_mb @ w_o_moba[l]))
        x = x + gate1[:, None, :] * (merged @ w_out[l])

        hdn = modulate(rmsnorm(x, norm2_g[l]), shift2, scale2)
        ff = jnp.square(jax.nn.relu(hdn @ w_ff1[l])) @ w_ff2[l]
        x = x + gate2[:, None, :] * ff

    return rmsnorm(x, final_norm_g)


HEAD_DIM = 64
FOX_HEADS = 4
NSA_HEADS = 8
NSA_KV_GROUPS = 2
DIL_HEADS = 4
MIX_WIDTH = (FOX_HEADS + NSA_HEADS + DIL_HEADS) * HEAD_DIM
DIL_PATTERNS = ((128, 1), (512, 4), (2048, 16))
ROPE_DIM = HEAD_DIM // 4
CMP_BLOCK = 32
CMP_STRIDE = 16
CMP_HIDDEN = 4 * HEAD_DIM
SEL_BLOCK = 64
SEL_TOPK = 16
NSA_WINDOW = 512
D_FF_2 = 2816
CONV_WIDTH = 3
RMS_EPS = 1e-6
NEG_INF_2 = -1e30
FORCE_SCORE = 1e9
ATTN_SCALE = HEAD_DIM ** -0.5
KV_W = NSA_KV_GROUPS * HEAD_DIM
IN_SPLITS_2 = (FOX_HEADS * HEAD_DIM,) * 3 + (FOX_HEADS,) + (NSA_HEADS * HEAD_DIM,) + (KV_W,) * 6 + (3 * NSA_HEADS,) + (DIL_HEADS * HEAD_DIM,) * 3
N_IN = sum(IN_SPLITS_2)


def rms_norm(x, g):
    xf = x.astype(jnp.float32)
    y = xf * lax.rsqrt(jnp.mean(xf * xf, axis=-1, keepdims=True) + RMS_EPS)
    return (y * g.astype(jnp.float32)).astype(x.dtype)

def rope_tables_2(positions):
    half = ROPE_DIM // 2
    inv_freq = ROPE_THETA ** (-2.0 * jnp.arange(half, dtype=jnp.float32) / ROPE_DIM)
    ang = positions.astype(jnp.float32)[..., None] * inv_freq
    return jnp.cos(ang)[:, :, None, :], jnp.sin(ang)[:, :, None, :]

def partial_rope(x, cos, sin):
    half = ROPE_DIM // 2
    cos = cos.astype(x.dtype)
    sin = sin.astype(x.dtype)
    x1 = x[..., :half]
    x2 = x[..., half:ROPE_DIM]
    return jnp.concatenate([x1 * cos - x2 * sin, x2 * cos + x1 * sin, x[..., ROPE_DIM:]], axis=-1)

def masked_softmax(scores, mask):
    s = jnp.where(mask, scores, NEG_INF_2)
    m = jnp.max(s, axis=-1, keepdims=True)
    e = jnp.where(mask, jnp.exp(s - m), 0.0)
    den = jnp.maximum(jnp.sum(e, axis=-1, keepdims=True), 1e-30)
    return e / den, m + jnp.log(den)

def sweep_query_blocks(fn, seq):
    out = lax.map(fn, jnp.arange(seq // Q_BLOCK, dtype=jnp.int32) * Q_BLOCK)
    out = jnp.moveaxis(out, 0, 1)
    return out.reshape((out.shape[0], seq) + out.shape[3:])

def fox_attention(q, k, v, log_f):
    S = q.shape[1]
    c = jnp.cumsum(log_f, axis=1)
    c_k = jnp.transpose(c, (0, 2, 1))[:, :, None, :]
    kpos = jnp.arange(S)

    def block(start):
        qb = lax.dynamic_slice_in_dim(q, start, Q_BLOCK, axis=1)
        cb = lax.dynamic_slice_in_dim(c, start, Q_BLOCK, axis=1)
        qpos = start + jnp.arange(Q_BLOCK)
        s = jnp.einsum('bqhd,bkhd->bhqk', qb, k, preferred_element_type=jnp.float32) * ATTN_SCALE
        s = s + jnp.transpose(cb, (0, 2, 1))[..., None] - c_k
        p, _ = masked_softmax(s, kpos[None, :] <= qpos[:, None])
        return jnp.einsum('bhqk,bkhd->bqhd', p.astype(v.dtype), v)

    return sweep_query_blocks(block, S)

def dilated_attention(q, k, v):
    S = q.shape[1]

    def block(start):
        qb = lax.dynamic_slice_in_dim(q, start, Q_BLOCK, axis=1)
        qpos = start + jnp.arange(Q_BLOCK)
        outs, lses = [], []
        for window, dilation in DIL_PATTERNS:
            offs = jnp.arange(window // dilation + 1) * dilation
            idx = qpos[:, None] - offs[None, :]
            valid = idx >= 0
            idx = jnp.maximum(idx, 0)
            kg = jnp.take(k, idx, axis=1)
            vg = jnp.take(v, idx, axis=1)
            s = jnp.einsum('bqhd,bqjhd->bhqj', qb, kg, preferred_element_type=jnp.float32) * ATTN_SCALE
            p, lse = masked_softmax(s, valid[None, None])
            outs.append(jnp.einsum('bhqj,bqjhd->bqhd', p.astype(v.dtype), vg))
            lses.append(lse[..., 0])
        w = jax.nn.softmax(jnp.stack(lses, 0), axis=0)
        w = jnp.transpose(w, (0, 1, 3, 2))[..., None].astype(v.dtype)
        return jnp.sum(w * jnp.stack(outs, 0), axis=0)

    return sweep_query_blocks(block, S)

def nsa_compress(kv, pos_emb, w1, w2):
    S = kv.shape[1]
    n_cmp = (S - CMP_BLOCK) // CMP_STRIDE + 1
    idx = jnp.arange(n_cmp)[:, None] * CMP_STRIDE + jnp.arange(CMP_BLOCK)[None, :]
    win = jnp.take(kv, idx, axis=1) + pos_emb[None, None, :, None, :]
    B, N, L, G, hd = win.shape
    win = jnp.transpose(win, (0, 1, 3, 2, 4)).reshape(B, N, G, L * hd)
    return jax.nn.gelu(win @ w1) @ w2

def nsa_attention(q, kc, vc, ks, vs, kw, vw, gates, cmp_pos_k, cmp_w1_k, cmp_w2_k, cmp_pos_v, cmp_w1_v, cmp_w2_v):
    B, S, H, hd = q.shape
    G = NSA_KV_GROUPS
    R = H // G
    k_cmp = nsa_compress(kc, cmp_pos_k, cmp_w1_k, cmp_w2_k)
    v_cmp = nsa_compress(vc, cmp_pos_v, cmp_w1_v, cmp_w2_v)
    n_cmp = k_cmp.shape[1]
    cmp_start = jnp.arange(n_cmp) * CMP_STRIDE
    cmp_end = cmp_start + CMP_BLOCK - 1
    n_sel = S // SEL_BLOCK
    top_k = min(SEL_TOPK, n_sel)
    sel_start = jnp.arange(n_sel) * SEL_BLOCK
    overlap = ((cmp_start[:, None] < sel_start[None, :] + SEL_BLOCK) & (cmp_start[:, None] + CMP_BLOCK > sel_start[None, :])).astype(jnp.float32)
    ks_blk = jnp.transpose(ks.reshape(B, n_sel, SEL_BLOCK, G, hd), (0, 3, 1, 2, 4))
    vs_blk = jnp.transpose(vs.reshape(B, n_sel, SEL_BLOCK, G, hd), (0, 3, 1, 2, 4))
    pad = ((0, 0), (NSA_WINDOW, 0), (0, 0), (0, 0))
    kw_pad = jnp.pad(kw, pad)
    vw_pad = jnp.pad(vw, pad)
    gather_blocks = jax.vmap(jax.vmap(lambda blocks, idx: blocks[idx]))
    blk_id = jnp.arange(n_sel)[None, :]

    def block(start):
        qb = lax.dynamic_slice_in_dim(q, start, Q_BLOCK, axis=1).reshape(B, Q_BLOCK, G, R, hd)
        gb = lax.dynamic_slice_in_dim(gates, start, Q_BLOCK, axis=1).reshape(B, Q_BLOCK, G, R, 3)
        qpos = start + jnp.arange(Q_BLOCK)
        s_c = jnp.einsum('bqgrd,bngd->bgrqn', qb, k_cmp, preferred_element_type=jnp.float32) * ATTN_SCALE
        p_c, _ = masked_softmax(s_c, cmp_end[None, :] <= qpos[:, None])
        o_c = jnp.einsum('bgrqn,bngd->bqgrd', p_c.astype(v_cmp.dtype), v_cmp)
        imp = jnp.einsum('bgrqn,nj->bgqj', p_c, overlap)
        cur = (qpos // SEL_BLOCK)[:, None]
        forced = (blk_id == 0) | (blk_id == cur) | (blk_id == cur - 1)
        future = sel_start[None, :] > qpos[:, None]
        imp = jnp.where(future, NEG_INF_2, jnp.where(forced, FORCE_SCORE, imp))
        _, sel = lax.top_k(imp, top_k)
        k_sel = gather_blocks(ks_blk, sel).reshape(B, G, Q_BLOCK, top_k * SEL_BLOCK, hd)
        v_sel = gather_blocks(vs_blk, sel).reshape(B, G, Q_BLOCK, top_k * SEL_BLOCK, hd)
        kpos_sel = (sel[..., None] * SEL_BLOCK + jnp.arange(SEL_BLOCK)).reshape(B, G, Q_BLOCK, top_k * SEL_BLOCK)
        mask_s = (kpos_sel <= qpos[None, None, :, None])[:, :, None]
        s_s = jnp.einsum('bqgrd,bgqkd->bgrqk', qb, k_sel, preferred_element_type=jnp.float32) * ATTN_SCALE
        p_s, _ = masked_softmax(s_s, mask_s)
        o_s = jnp.einsum('bgrqk,bgqkd->bqgrd', p_s.astype(v_sel.dtype), v_sel)
        kwb = lax.dynamic_slice_in_dim(kw_pad, start, Q_BLOCK + NSA_WINDOW, axis=1)
        vwb = lax.dynamic_slice_in_dim(vw_pad, start, Q_BLOCK + NSA_WINDOW, axis=1)
        kpos_w = (start - NSA_WINDOW + jnp.arange(Q_BLOCK + NSA_WINDOW))[None, :]
        mask_w = (kpos_w <= qpos[:, None]) & (kpos_w > qpos[:, None] - NSA_WINDOW) & (kpos_w >= 0)
        s_w = jnp.einsum('bqgrd,bkgd->bgrqk', qb, kwb, preferred_element_type=jnp.float32) * ATTN_SCALE
        p_w, _ = masked_softmax(s_w, mask_w)
        o_w = jnp.einsum('bgrqk,bkgd->bqgrd', p_w.astype(vwb.dtype), vwb)
        o = gb[..., 0:1] * o_c + gb[..., 1:2] * o_s + gb[..., 2:3] * o_w
        return o.reshape(B, Q_BLOCK, H, hd)

    return sweep_query_blocks(block, S)

def hybrid_mixer(h, cos, sin, w_in, b_forget, b_nsa_gate, cmp_pos_k, cmp_w1_k, cmp_w2_k, cmp_pos_v, cmp_w1_v, cmp_w2_v, w_out):
    B, S, _ = h.shape
    proj = h @ w_in
    splits = np.cumsum(IN_SPLITS_2)[:-1].tolist()
    (fq, fk, fv, ff, nq, kc, vc, ks, vs, kw, vw, ng, dq, dk, dv) = jnp.split(proj, splits, axis=-1)

    def heads(t, n):
        return t.reshape(B, S, n, HEAD_DIM)

    log_f = jax.nn.log_sigmoid(ff.astype(jnp.float32) + b_forget.astype(jnp.float32))
    o_fox = fox_attention(heads(fq, FOX_HEADS), heads(fk, FOX_HEADS), heads(fv, FOX_HEADS), log_f)
    rope = lambda t, n: partial_rope(heads(t, n), cos, sin)
    gates = jax.nn.sigmoid(ng + b_nsa_gate).reshape(B, S, NSA_HEADS, 3)
    o_nsa = nsa_attention(rope(nq, NSA_HEADS), rope(kc, NSA_KV_GROUPS), heads(vc, NSA_KV_GROUPS),
                          rope(ks, NSA_KV_GROUPS), heads(vs, NSA_KV_GROUPS),
                          rope(kw, NSA_KV_GROUPS), heads(vw, NSA_KV_GROUPS), gates,
                          cmp_pos_k, cmp_w1_k, cmp_w2_k, cmp_pos_v, cmp_w1_v, cmp_w2_v)
    o_dil = dilated_attention(rope(dq, DIL_HEADS), rope(dk, DIL_HEADS), heads(dv, DIL_HEADS))
    mix = jnp.concatenate([o_fox.reshape(B, S, -1), o_nsa.reshape(B, S, -1), o_dil.reshape(B, S, -1)], axis=-1)
    return mix @ w_out

def conv_ffn(h, w_up, conv_w, conv_b, w_down):
    S = h.shape[1]
    u = h @ w_up
    u_pad = jnp.pad(u, ((0, 0), (CONV_WIDTH - 1, 0), (0, 0)))
    c = conv_b + u_pad[:, 0:S] * conv_w[0]
    for j in range(1, CONV_WIDTH):
        c = c + u_pad[:, j:j + S] * conv_w[j]
    a, b = jnp.split(c, 2, axis=-1)
    return (jax.nn.silu(a) * b) @ w_down

def second_inputs(seed: int = 0) -> dict:
    key = jax.random.key(seed)
    k = jax.random.split(key, 24)
    nrm = lambda kk, shape, scale: jax.random.normal(kk, shape, jnp.float32) * scale
    x = nrm(k[0], (BATCH, SEQ, D_MODEL), 1.0)
    offset = jax.random.randint(k[1], (BATCH, 1), 0, 1024, dtype=jnp.int32)
    positions = offset + jnp.arange(SEQ, dtype=jnp.int32)[None, :]
    return {
        'x': x,
        'positions': positions,
        'attn_pre_norm': 1.0 + nrm(k[2], (DEPTH, D_MODEL), 0.05),
        'attn_post_norm': 1.0 + nrm(k[3], (DEPTH, D_MODEL), 0.05),
        'ffn_pre_norm': 1.0 + nrm(k[4], (DEPTH, D_MODEL), 0.05),
        'ffn_post_norm': 1.0 + nrm(k[5], (DEPTH, D_MODEL), 0.05),
        'w_in': nrm(k[6], (DEPTH, D_MODEL, N_IN), D_MODEL ** -0.5),
        'b_forget': jax.random.uniform(k[7], (DEPTH, FOX_HEADS), jnp.float32, 1.0, 5.0),
        'b_nsa_gate': nrm(k[8], (DEPTH, 3 * NSA_HEADS), 0.01),
        'cmp_pos_k': nrm(k[9], (DEPTH, CMP_BLOCK, HEAD_DIM), 0.1),
        'cmp_w1_k': nrm(k[10], (DEPTH, CMP_BLOCK * HEAD_DIM, CMP_HIDDEN), (CMP_BLOCK * HEAD_DIM) ** -0.5),
        'cmp_w2_k': nrm(k[11], (DEPTH, CMP_HIDDEN, HEAD_DIM), CMP_HIDDEN ** -0.5),
        'cmp_pos_v': nrm(k[12], (DEPTH, CMP_BLOCK, HEAD_DIM), 0.1),
        'cmp_w1_v': nrm(k[13], (DEPTH, CMP_BLOCK * HEAD_DIM, CMP_HIDDEN), (CMP_BLOCK * HEAD_DIM) ** -0.5),
        'cmp_w2_v': nrm(k[14], (DEPTH, CMP_HIDDEN, HEAD_DIM), CMP_HIDDEN ** -0.5),
        'w_out': nrm(k[15], (DEPTH, MIX_WIDTH, D_MODEL), MIX_WIDTH ** -0.5),
        'w_up': nrm(k[16], (DEPTH, D_MODEL, 2 * D_FF_2), D_MODEL ** -0.5),
        'conv_w': nrm(k[17], (DEPTH, CONV_WIDTH, 2 * D_FF_2), CONV_WIDTH ** -0.5),
        'conv_b': nrm(k[18], (DEPTH, 2 * D_FF_2), 0.01),
        'w_down': nrm(k[19], (DEPTH, D_FF_2, D_MODEL), D_FF_2 ** -0.5),
    }

def second_block(x, positions, attn_pre_norm, attn_post_norm, ffn_pre_norm, ffn_post_norm, w_in, b_forget, b_nsa_gate,
              cmp_pos_k, cmp_w1_k, cmp_w2_k, cmp_pos_v, cmp_w1_v, cmp_w2_v, w_out, w_up, conv_w, conv_b, w_down):
    cos, sin = rope_tables_2(positions)
    for l in range(DEPTH):
        h = rms_norm(x, attn_pre_norm[l])
        mix = hybrid_mixer(h, cos, sin, w_in[l], b_forget[l], b_nsa_gate[l], cmp_pos_k[l], cmp_w1_k[l], cmp_w2_k[l],
                           cmp_pos_v[l], cmp_w1_v[l], cmp_w2_v[l], w_out[l])
        x = x + rms_norm(mix, attn_post_norm[l])
        h = rms_norm(x, ffn_pre_norm[l])
        x = x + rms_norm(conv_ffn(h, w_up[l], conv_w[l], conv_b[l], w_down[l]), ffn_post_norm[l])
    return x


def setup_inputs(seed=0):
    out = dict(first_inputs(seed))
    for name, value in second_inputs(seed + 1).items():
        if name != "x":
            out[name + "_2"] = value
    return out


def reference(
    x, c, positions, w_ada, b_ada, norm1_g, norm2_g, w_in, q_norm_g, w_uq, kv_norm_g, w_ukv,
    w_o_mla, w_o_sb, w_o_moba, w_out, w_ff1, w_ff2, final_norm_g, positions_2, attn_pre_norm_2,
    attn_post_norm_2, ffn_pre_norm_2, ffn_post_norm_2, w_in_2, b_forget_2, b_nsa_gate_2,
    cmp_pos_k_2, cmp_w1_k_2, cmp_w2_k_2, cmp_pos_v_2, cmp_w1_v_2, cmp_w2_v_2, w_out_2, w_up_2,
    conv_w_2, conv_b_2, w_down_2,
):
    x = first_block(
        x, c, positions, w_ada, b_ada, norm1_g, norm2_g, w_in, q_norm_g, w_uq, kv_norm_g, w_ukv,
        w_o_mla, w_o_sb, w_o_moba, w_out, w_ff1, w_ff2, final_norm_g,
    )
    return second_block(
        x, positions_2, attn_pre_norm_2, attn_post_norm_2, ffn_pre_norm_2, ffn_post_norm_2,
        w_in_2, b_forget_2, b_nsa_gate_2, cmp_pos_k_2, cmp_w1_k_2, cmp_w2_k_2, cmp_pos_v_2,
        cmp_w1_v_2, cmp_w2_v_2, w_out_2, w_up_2, conv_w_2, conv_b_2, w_down_2,
    )


_drawn_inputs = setup_inputs


def setup_inputs(seed=0):
    import zlib

    import numpy as np

    out = dict(_drawn_inputs(seed))
    spreads = {}
    factors = {'norm1_g': 4.941,
     'norm2_g': 2.817,
     'q_norm_g': 8.0,
     'kv_norm_g': 8.0,
     'b_nsa_gate_2': 22.605,
     'cmp_pos_k_2': 8.0,
     'conv_b_2': 5.143}
    for name, (base, spread) in spreads.items():
        noise = np.random.default_rng([zlib.crc32(name.encode()), seed]).standard_normal(out[name].shape)
        drawn = base * np.exp(spread * noise) if base else spread * noise
        out[name] = __import__('jax').numpy.asarray(drawn.astype(out[name].dtype))
    for name, factor in factors.items():
        out[name] = (out[name] * factor).astype(out[name].dtype)
    return out
```

```python
import contextlib
import math

import numpy as np
import concourse.bass as bass
from concourse import mybir

F32 = mybir.dt.float32
I32 = mybir.dt.int32
ACT = mybir.ActivationFunctionType
ALU = mybir.AluOpType
AX = mybir.AxisListType

P = 128
S, D, DEPTH = 256, 1024, 2
T = S // P
KD = D // P
EPS = 1e-6
NEG = -1e30
THETA = 500000.0
HD = 64

NH = 8
NOPE, ROPE = 64, 32
QK = NOPE + ROPE
QR, KVR = 768, 256
ATT = QR + KVR + ROPE + 6 * NH * HD
SB0 = QR + KVR + ROPE
MB0 = SB0 + 3 * NH * HD
D_IN = ATT + 3 * D
FF1 = 4 * D
ATT_W = 464
UQ_W = NH * QK // 2

FOX, NSA, GRP, DIL = 4, 8, 2, 4
FQ, FK, FV, FG = 0, FOX * HD, 2 * FOX * HD, 3 * FOX * HD
NQ = FG + FOX
KC = NQ + NSA * HD
VC, KS, VS, KW, VW = (KC + n * GRP * HD for n in range(1, 6))
NG = KC + 6 * GRP * HD
DQ = NG + 3 * NSA
DK, DV = DQ + DIL * HD, DQ + 2 * DIL * HD
N_IN = DV + DIL * HD
IN2_W = N_IN // 6
CMP_L, CMP_ST, CMP_H = 32, 16, 256
NCMP = (S - CMP_L) // CMP_ST + 1
FF2 = 2816
CH = FF2 // P
WU = 4096
SLOTS = 4
AUG = HD + 2

C_ID, C_ONE, C_TRI, C_NTRI, C_NONE = (n * P for n in range(5))
C_CAUS = 5 * P
C_DMASK = C_CAUS + 3 * P
C_DW = C_DMASK + 3 * P
C_CMASK = C_DW + 3 * P
C_CADD = C_CMASK + T * NCMP
C_SMASK = C_CADD + T * NCMP
C_INV = C_SMASK + 3 * P
C_N = C_INV + 32

TWO_PI = 2 * math.pi
PI_A = 6.28125
PI_B = float(np.float32(np.floor((TWO_PI - PI_A) * 2**20) / 2**20))
PI_C = float(np.float32(TWO_PI - PI_A - PI_B))
ROUNDER = 12582912.0
PI_SAFE = 3.1415925


def constants():
    c = np.zeros((P, C_N), np.float32)
    i = np.arange(P)
    c[:, C_ID:C_ID + P] = np.eye(P)
    c[:, C_ONE:C_ONE + P] = 1.0
    c[:, C_TRI:C_TRI + P] = i[:, None] <= i[None, :]
    c[:, C_NTRI:C_NTRI + P] = -(i[:, None] >= i[None, :]).astype(np.float32)
    c[:, C_NONE:C_NONE + P] = -1.0
    q = np.concatenate([np.broadcast_to(i[:, None], (P, P)), np.broadcast_to(P + i[:, None], (P, S))], 1)
    k = np.concatenate([np.broadcast_to(i[None], (P, P)), np.broadcast_to(np.arange(S)[None], (P, S))], 1)
    back = q - k
    c[:, C_CAUS:C_CAUS + 3 * P] = np.where(back >= 0, 0.0, NEG)
    times = sum(((back >= 0) & (back % d == 0) & (back <= w)).astype(np.float32)
                for w, d in ((128, 1), (512, 4), (2048, 16)))
    c[:, C_DMASK:C_DMASK + 3 * P] = np.where(times > 0, 0.0, NEG)
    c[:, C_DW:C_DW + 3 * P] = times
    after = np.where(i[None, :] > i[:, None], 0.0, NEG)
    c[:, C_SMASK:C_SMASK + P] = after
    c[:, C_SMASK + 2 * P:C_SMASK + 3 * P] = after
    ends = np.arange(NCMP) * CMP_ST + CMP_L - 1
    for t in range(T):
        seen = ends[None, :] <= t * P + i[:, None]
        c[:, C_CMASK + t * NCMP:C_CMASK + (t + 1) * NCMP] = seen
        c[:, C_CADD + t * NCMP:C_CADD + (t + 1) * NCMP] = np.where(seen, 0.0, NEG)
    for at, rot in ((0, ROPE), (16, HD // 4), (24, HD // 4)):
        inv = np.float32(THETA) ** (-np.arange(0, rot, 2, dtype=np.float32) / np.float32(rot))
        c[:, C_INV + at:C_INV + at + rot // 2] = inv
    return c


def jobs_first(q, k_mla, v_mla, proj):
    mla = [dict(kind="mla", head=h, rows=QK, base=0, q=h, k=h, v=v_mla[:, :, h * HD:(h + 1) * HD],
                scale=1 / math.sqrt(QK)) for h in range(NH)]
    v0 = MB0 + 2 * NH * HD
    moba = [dict(kind="moba", head=h, rows=HD, base=HD * (h % 2), q=h // 2, k=NH // 2 + h // 2,
                 v=proj[:, :, v0 + h * HD:v0 + (h + 1) * HD], scale=1 / math.sqrt(HD)) for h in range(NH)]
    return mla, moba


def two_blocks(nc, x_in, c_in, positions, w_ada, b_ada, norm1_g, norm2_g, w_in, q_norm_g, w_uq,
               kv_norm_g, w_ukv, w_o_mla, w_o_sb, w_o_moba, w_out, w_ff1, w_ff2, final_norm_g,
               positions_2, attn_pre, attn_post, ffn_pre, ffn_post, w_in_2, b_forget, b_nsa,
               pos_k, cw1_k, cw2_k, pos_v, cw1_v, cw2_v, w_out_2, w_up, conv_w, conv_b, w_down,
               table, out, LAYERS1=DEPTH, LAYERS2=DEPTH):
    ctx = contextlib.ExitStack()
    with ctx:
        def sb(name, shape, dt=F32):
            return ctx.enter_context(nc.sbuf_tensor(name, shape, dt))

        def sem(name):
            return ctx.enter_context(nc.semaphore(name))

        cst = sb("cst", [P, C_N])
        x = sb("x", [P, T, D])
        wide = sb("wide", [P, T, D])
        featT = sb("featT", [P, KD, S])
        big = sb("big", [P, 33 * S])
        gates = sb("gates", [P, T, 3 * D])
        kvm = sb("kvm", [P, T, NH * (QK + HD)])
        oT = sb("oT", [P, 12, S])
        NB = 3
        sm = sb("sm", [P, NB, 3 * P])
        pr = sb("pr", [P, NB, 3 * P])
        pT = sb("pT", [P, NB, 3 * P])
        rowbc = sb("rowbc", [P, 2, D])
        pcol = sb("pcol", [P, 6, P])
        mod = sb("mod", [P, 32])
        small = sb("small", [P, DEPTH, FOX + 3 * NSA])
        cw2 = sb("cw2", [P, DEPTH, 2, 2, HD])
        posi = sb("posi", [4, P], I32)
        posf = sb("posf", [4, P])
        cs = sb("cs", [P, 2, T, 32])
        trig = sb("trig", [P, 3, T * 32])
        posc = sb("posc", [P, 4])
        tiny = sb("tiny", [P, 64])
        stat = sb("stat", [P, 16])
        mx = sb("mx", [P, NB, T])
        rs = sb("rs", [P, NB, T])
        half = sb("half", [P, T])
        fox = sb("fox", [P, 3, T * FOX])
        gn = sb("gn", [P, 2, T * 3 * NSA])
        ring = sb("ring", [P, SLOTS, WU])

        proj = big[:, 0:T * ATT].rearrange("p (t n) -> p t n", t=T)
        proj2 = big[:, 0:T * N_IN].rearrange("p (t n) -> p t n", t=T)
        hidT = big[:, 0:32 * S].rearrange("p (c s) -> p c s", s=S)
        qmla = proj[:, :, 0:QR]
        k_mla = kvm[:, :, 0:NH * QK].rearrange("p t (h e) -> p t h e", e=QK)
        v_mla = kvm[:, :, NH * QK:]
        c_act = tiny[:, 0:8]
        c_tmp = tiny[:, 8:16]
        cbc = featT[:, 0:4, :].rearrange("p a b -> p (a b)").rearrange("p (k m) -> p k m", m=P)
        prow = big[:, 0:6 * P].rearrange("p (m n) -> p m n", m=6)
        rope_t = sm[:, :, :].rearrange("p b n -> p (b n)")[:, 0:4 * 256].rearrange("p (a n) -> p a n", a=4)
        wideT = wide[:, :, :].rearrange("p t n -> p (t n)").rearrange("p (c s) -> p c s", s=S)
        ident = cst[:, C_ID:C_ID + P]
        gf = gates[:, :, :].rearrange("p t n -> p (t n)")
        faug = gf[:, 0:T * 2 * FOX * AUG].rearrange("p (t a h e) -> p t a h e", t=T, a=2, h=FOX)
        UOFF = T * 2 * FOX * AUG
        U = gf[:, UOFF:UOFF + 2 * GRP * S].rearrange("p (a g s) -> p a g s", a=2, g=GRP)
        AOFF = UOFF + 2 * GRP * S
        awin = gf[:, AOFF:AOFF + 2 * 16 * GRP * NCMP].rearrange("p (a c n) -> p a c n", a=2, c=16)
        GOFF = AOFF + 2 * 16 * GRP * NCMP
        gel = gf[0:GRP * NCMP, GOFF:GOFF + 3 * 512].rearrange("p (a n) -> p a n", a=3)
        HOFF = GOFF + 3 * 512
        hT = gf[:, HOFF:HOFF + 4 * GRP * NCMP].rearrange("p (a n) -> p a n", a=4)
        KOFF = HOFF + 4 * GRP * NCMP
        kcT = gf[:, KOFF:KOFF + NCMP]
        vcm = gf[0:NCMP, KOFF + 16:KOFF + 16 + GRP * HD].rearrange("p (g d) -> p g d", g=GRP)
        nq = gf[:, KOFF + 16 + GRP * HD:KOFF + 16 + GRP * HD + T * NSA * HD].rearrange(
            "p (t j g d) -> p t j g d", t=T, j=4, g=GRP)
        kf = kvm[:, :, :].rearrange("p t n -> p (t n)")
        pc = kf[:, 0:T * NSA * NCMP].rearrange("p (t h n) -> p t h n", t=T, h=NSA)
        pc2 = kf[:, 240:240 + T * NSA * NCMP].rearrange("p (t h n) -> p t h n", t=T, h=NSA)
        pcs = kf[:, 480:480 + T * NSA].rearrange("p (t h) -> p t h", t=T)
        pcT = kf[0:NCMP, 496:496 + NSA * S].rearrange("p (h s) -> p h s", s=S)
        cv = gf[:, 0:2 * 3 * 512].rearrange("p (b a n) -> p b a n", b=2, a=3)

        banks = [ctx.enter_context(nc.psum_tensor(f"bank{n}", [P, 512], F32)) for n in range(8)]

        class Tiles:

            def __init__(self, name, own):
                self.banks = own
                self.full = sem(f"{name}_full")
                self.read = sem(f"{name}_read")

        for_act = Tiles("for_act", banks[0:3])
        for_dve = Tiles("for_dve", banks[3:6])
        outputs = Tiles("outputs", banks[6:8])

        w_used = sem("w_used")
        w_loaded = [sem(f"w_loaded{n}") for n in range(SLOTS)]
        const_loaded = sem("const_loaded")
        rows_loaded = sem("rows_loaded")
        small_loaded = sem("small_loaded")
        x_loaded = sem("x_loaded")
        bc_loaded = sem("bc_loaded")
        out_stored = sem("out_stored")
        act_chain, dve_chain, pool_chain = sem("act_chain"), sem("dve_chain"), sem("pool_chain")
        pos_cast = sem("pos_cast")
        angles = sem("angles")
        sines = sem("sines")
        c_exp, cbc_ready = sem("c_exp"), sem("cbc_ready")
        squares = sem("squares")
        rstd_ready = sem("rstd_ready")
        scaled = sem("scaled")
        x_ready = sem("x_ready")
        evac_act = sem("evac_act")
        ready_dve = sem("ready_dve")
        gate_exp = sem("gate_exp")
        merged = sem("merged")
        s_masked = sem("s_masked")
        s_exp = sem("s_exp")
        p_ready = sem("p_ready")
        sb_log, sb_raw, sb_keep = sem("sb_log"), sem("sb_raw"), sem("sb_keep")
        sb_total, sb_masked, sb_ready = sem("sb_total"), sem("sb_masked"), sem("sb_ready")
        evac_dve = sem("evac_dve")
        conv_done = sem("conv_done")
        stick_tile0, conv_tile0 = [], []
        fox_in, fox_log, fox_lf = sem("fox_in"), sem("fox_log"), sem("fox_lf")
        nsa_in, nsa_exp = sem("nsa_in"), sem("nsa_exp")
        gelu_in, gelu_exp, gelu_out = sem("gelu_in"), sem("gelu_exp"), sem("gelu_out")
        win_ready = sem("win_ready")
        pc_in, pc_exp, pc_out = sem("pc_in"), sem("pc_exp"), sem("pc_out")
        conv_base, silu_in, silu_exp = sem("conv_base"), sem("silu_in"), sem("silu_exp")

        def rows_of(w, n0, n1, c0, c1):
            return w[n0 * P:n1 * P, c0:c1].rearrange("(k p) n -> p k n", p=P)

        def slot_view(u, k, n):
            return ring[:, u % SLOTS, 0:k * n].rearrange("p (k n) -> p k n", k=k)

        units = []

        def unit(k, n, *parts):
            units.append((k, n, parts or None))

        def plain(w, k0, k1, c0, c1):
            k, n = k1 - k0, c1 - c0
            units.append((k, n, [(slice(0, P), slice(0, k), slice(0, n), rows_of(w, k0, k1, c0, c1))]))

        for l in range(LAYERS1):
            for u in range(12):
                plain(w_ada[l], 0, KD, 512 * u, 512 * u + 512)
            for c0 in range(0, ATT, ATT_W):
                plain(w_in[l], 0, KD, c0, min(c0 + ATT_W, ATT))
            for u in range(6):
                plain(w_in[l], 0, KD, ATT + 512 * u, ATT + 512 * u + 512)
            for u in range(2):
                plain(w_uq[l], 0, QR // P, UQ_W * u, UQ_W * u + UQ_W)
            plain(w_ukv[l], 0, KVR // P, 0, 2 * NH * HD)
            for w in (w_o_mla, w_o_sb, w_o_moba):
                plain(w[l], 0, 4, 0, D)
            for u in range(2):
                plain(w_out[l], 0, KD, 512 * u, 512 * u + 512)
            for u in range(8):
                plain(w_ff1[l], 0, KD, 512 * u, 512 * u + 512)
            for u in range(8):
                plain(w_ff2[l], 4 * u, 4 * u + 4, 0, D)
        for l in range(LAYERS2):
            for u in range(6):
                plain(w_in_2[l], 0, KD, IN2_W * u, IN2_W * u + IN2_W)
            for w in (cw1_k, cw1_v):
                plain(w[l], 0, 16, 0, CMP_H)
            for u in range(2):
                cols = slice(512 * u, 512 * u + 512)
                w = w_out_2[l]
                lo = FOX * HD
                lower = w[lo:lo + 4 * HD, cols].rearrange("(j p) n -> p j n", p=HD)
                upper = w[lo + 4 * HD:lo + 8 * HD, cols].rearrange("(j p) n -> p j n", p=HD)
                units.append((KD, 512, [
                    (slice(0, P), slice(0, 2), slice(0, 512), rows_of(w, 0, 2, cols.start, cols.stop)),
                    (slice(0, HD), slice(2, 6), slice(0, 512), lower),
                    (slice(HD, P), slice(2, 6), slice(0, 512), upper),
                    (slice(0, P), slice(6, 8), slice(0, 512), rows_of(w, 6, 8, cols.start, cols.stop))]))
            for j in range(CH // 2):
                a0, b0 = 256 * j, FF2 + 256 * j
                units.append((KD, 512, [
                    (slice(0, P), slice(0, KD), slice(0, 256), rows_of(w_up[l], 0, KD, a0, a0 + 256)),
                    (slice(0, P), slice(0, KD), slice(256, 512), rows_of(w_up[l], 0, KD, b0, b0 + 256))]))
            for k0 in range(0, CH, 4):
                plain(w_down[l], k0, min(k0 + 4, CH), 0, D)
        loads = [0] * SLOTS
        arrival = []
        for u, (_, _, parts) in enumerate(units):
            loads[u % SLOTS] += 16 * len(parts)
            arrival.append(loads[u % SLOTS])

        mla_jobs, moba_jobs = jobs_first(qmla, k_mla, v_mla, proj)
        for n, j in enumerate(mla_jobs):
            j.update(chunk=n // 2, obase=HD * (n % 2), first=True, last=True, done=n % 2 == 1, mask=C_CAUS, weight=False, gate=None, dst=0)
        for n, j in enumerate(moba_jobs):
            j.update(chunk=8 + n // 2, obase=HD * (n % 2), first=True, last=True, done=n % 2 == 1, mask=C_CAUS, weight=False, gate=None, dst=0)
        second_jobs = []
        for h in range(FOX):
            second_jobs.append(dict(kind="fox", rows=AUG, base=0, q=h, k=FOX + h, v=proj2[:, :, FV + h * HD:FV + (h + 1) * HD],
                                    scale=1.0, chunk=h // 2, obase=HD * (h % 2), first=True, last=True, done=h % 2 == 1,
                                    mask=C_CAUS, weight=False, gate=None, cmp=None))
        for j in range(NSA // 2):
            for g in range(GRP):
                h = j + g * NSA // 2
                for br, (v0, kt) in enumerate(((VS, 12), (VW, 13))):
                    second_jobs.append(dict(kind="nsa", rows=HD, base=HD * g, q=8 + j, k=kt,
                                            v=proj2[:, :, v0 + g * HD:v0 + (g + 1) * HD], scale=1 / math.sqrt(HD),
                                            chunk=2 + j, obase=HD * g, first=False, last=br == 1, done=g == 1 and br == 1,
                                            mask=C_CAUS, weight=False, gate=3 * h + 1 + br, cmp=(h, g) if br == 0 else None))
        for h in range(DIL):
            second_jobs.append(dict(kind="dil", rows=HD, base=HD * (h % 2), q=14 + h // 2, k=h // 2 + 100,
                                    v=proj2[:, :, DV + h * HD:DV + (h + 1) * HD], scale=1 / math.sqrt(HD),
                                    chunk=6 + h // 2, obase=HD * (h % 2), first=True, last=True, done=h % 2 == 1,
                                    mask=C_DMASK, weight=True, gate=None, cmp=None))
        for j in mla_jobs + moba_jobs:
            j["cmp"] = None

        def turn(dst, src, rows, scale=None):
            return dict(dst=dst, src=src, rows=rows, scale=scale)

        def cols_of(src, c0, n):
            return [src[:, t, c0:c0 + n] for t in range(T)]

        mla_turns = [turn(h, cols_of(qmla, h * QK, QK), QK) for h in range(NH)] + \
                    [turn(NH + h, [k_mla[:, t, h, :] for t in range(T)], QK) for h in range(NH)]
        for j in mla_jobs:
            j["k"] += NH
        for j in moba_jobs:
            j["q"], j["k"] = j["q"], j["k"]
        sb_turns = [turn(j, cols_of(proj, SB0 + j * P, P), P, 1 / math.sqrt(HD)) for j in range(4)] + \
                   [turn(4 + j, cols_of(proj, SB0 + NH * HD + j * P, P), P) for j in range(4)]
        moba_turns = [turn(j, cols_of(proj, MB0 + j * P, P), P) for j in range(8)]
        fox_turns = [turn(h, [faug[:, t, 0, h, :] for t in range(T)], AUG) for h in range(FOX)] + \
                    [turn(FOX + h, [faug[:, t, 1, h, :] for t in range(T)], AUG) for h in range(FOX)]
        nsa_turns = [turn(8 + j, [nq[:, t, j, :, :].rearrange("p g d -> p (g d)") for t in range(T)], P) for j in range(4)] + \
                    [turn(12, cols_of(proj2, KS, P), P), turn(13, cols_of(proj2, KW, P), P)]
        dil_turns = [turn(14 + j, cols_of(proj2, DQ + j * P, P), P) for j in range(2)]
        dkT = oT[:, 8:10, :]
        dk_turns = [turn(100 + j, cols_of(proj2, DK + j * P, P), P) for j in range(2)]

        def turned(n):
            return dkT[:, n - 100, :] if n >= 100 else featT[:, n, :] if n < 8 else wideT[:, n - 8, :]

        block = ctx.enter_context(nc.Block())

        class Seen:

            def __init__(self, eng):
                self.eng, self.n = eng, {}

            def more(self, s, k=1):
                key = s.name
                self.n[key] = self.n.get(key, 0) + k
                self.eng.wait_ge(s, self.n[key])

        @block.sync
        def _(sp):
            sp.dma_start(cst[:, :], table).then_inc(const_loaded, 16)
            def row_load(tile, r0, vec):
                n = vec.shape[0] // P
                sp.dma_start(prow[r0:r0 + n, tile, :], vec.rearrange("(r p) -> r p", p=P)).then_inc(rows_loaded, 16)
            for l in range(DEPTH):
                row_load(l, 0, norm1_g[l])
                row_load(l, 8, norm2_g[l])
                row_load(l, 16, q_norm_g[l])
                row_load(l, 22, kv_norm_g[l])
                row_load(l, 24, b_ada[l])
            row_load(0, 72, c_in[0])
            for l in range(DEPTH):
                row_load(2 + l, 0, conv_w[l, 0])
                row_load(2 + l, 44, conv_w[l, 1])
                row_load(2 + l, 88, attn_pre[l])
                row_load(2 + l, 96, ffn_pre[l])
                row_load(4 + l, 0, conv_w[l, 2])
                row_load(4 + l, 44, conv_b[l])
                row_load(4 + l, 88, pos_k[l].rearrange("a b -> (a b)"))
                row_load(4 + l, 104, pos_v[l].rearrange("a b -> (a b)"))
            sp.dma_start(posi[0:2, :], positions[0].rearrange("(t p) -> t p", p=P)).then_inc(rows_loaded, 16)
            sp.dma_start(posi[2:4, :], positions_2[0].rearrange("(t p) -> t p", p=P)).then_inc(rows_loaded, 16)
            sp.dma_start(x[:, :, :], x_in[0].rearrange("(t p) n -> p t n", p=P)).then_inc(x_loaded, 16)
            for u, (k, n, parts) in enumerate(units):
                if u >= SLOTS:
                    sp.wait_ge(w_used, u - SLOTS + 1)
                view = slot_view(u, k, n)
                for ps, ks, ns, src in parts:
                    sp.dma_start(view[ps, ks, ns], src).then_inc(w_loaded[u % SLOTS], 16)
            sp.wait_ge(x_ready, LAYERS1 * 2 + (LAYERS1 > 0) + LAYERS2 * 2)
            sp.dma_start(out[0].rearrange("(t p) n -> p t n", p=P), x[:, :, :]).then_inc(out_stored, 16)
            sp.wait_ge(out_stored, 16)

        N_ROWS = 16 * (5 * DEPTH + 1 + 8 * DEPTH + 2)
        N_POOL_ROWS = 16 * 4 * DEPTH

        @block.gpsimd
        def _(pool):
            seen = Seen(pool)
            chain = [0]

            def link(ins):
                chain[0] += 1
                ins.then_inc(pool_chain, 1)
                pool.wait_ge(pool_chain, chain[0])

            for l in range(DEPTH):
                pool.dma_start(small[:, l, 0:FOX], b_forget[l].partition_broadcast(P)).then_inc(small_loaded, 16)
                pool.dma_start(small[:, l, FOX:], b_nsa[l].partition_broadcast(P)).then_inc(small_loaded, 16)
                for a, w in enumerate((cw2_k, cw2_v)):
                    pool.dma_start(cw2[:, l, a, :, :], w[l].rearrange("(k p) n -> p k n", p=P)).then_inc(small_loaded, 16)
            link(pool.memset(half[:, :], -0.5))

            def load_rows(a, b):
                pool.dma_start(rowbc[:, 0, :], a.partition_broadcast(P)).then_inc(bc_loaded, 16)
                pool.dma_start(rowbc[:, 1, :], b.partition_broadcast(P)).then_inc(bc_loaded, 16)

            def rstd(s0, width, n=T):
                seen.more(squares)
                link(pool.tensor_scalar(stat[:, s0:s0 + n], stat[:, s0:s0 + n], 1.0 / width, EPS, ALU.mult, ALU.add))
                pool.tensor_tensor(stat[:, s0 + n:s0 + 2 * n], stat[:, s0:s0 + n], half[:, 0:n], ALU.pow).then_inc(rstd_ready, 1)

            def diagonal(view, told):
                blocks = view.rearrange("p (b q) -> p b q", q=P)[:, 0:3:2, :]
                pool.affine_select(out=blocks, in_=blocks, pattern=[[0, 2], [1, P]], compare_op=ALU.is_gt,
                                   fill=0.0, base=0, channel_multiplier=-1).then_inc(told, 1)

            act_tiles = [0]
            for l in range(LAYERS1):
                if l:
                    seen.more(x_ready, 2)
                load_rows(b_ada[l, 2 * D:3 * D], b_ada[l, 5 * D:6 * D])
                rstd(0, D)
                rstd(4, QR)
                rstd(8, KVR)
                for i in range(NH):
                    seen.more(sb_raw)
                    diagonal(sm[:, i % NB, :], sb_keep)
                rstd(0, D)
            if LAYERS1:
                pool.dma_start(rowbc[:, 0, :], final_norm_g.partition_broadcast(P)).then_inc(bc_loaded, 16)
                rstd(0, D)
            for l in range(LAYERS2):
                if l or LAYERS1:
                    seen.more(x_ready, 2 if l else 3)
                load_rows(attn_post[l], ffn_post[l])
                rstd(0, D)
                rstd(0, D)
                rstd(0, D)
                rstd(0, D)

        @block.tensor
        def _(pe):
            seen = Seen(pe)
            made = {id(for_act): 0, id(for_dve): 0, id(outputs): 0}
            owed = [0]
            used = [0]

            def claim(ring_):
                n = made[id(ring_)]
                made[id(ring_)] = n + 1
                size = len(ring_.banks)
                if n >= size:
                    pe.wait_ge(ring_.read, n - size + 1)
                return ring_.banks[n % size], n + 1

            def mm(o, a, b, start=True, stop=True, full=None):
                ins = pe.matmul(o, a, b, start=start, stop=stop, skip_group_check=True)
                if full is not None:
                    ins.then_inc(full, 1)
                elif owed[0]:
                    ins.then_inc(w_used, owed[0])
                    owed[0] = 0
                return ins

            def flip(o, a, full=None):
                n = a.shape[0]
                ins = pe.transpose(o, a, ident[0:n, 0:n])
                if full is not None:
                    ins.then_inc(full, 1)
                elif owed[0]:
                    ins.then_inc(w_used, owed[0])
                    owed[0] = 0

            def weights():
                u = used[0]
                used[0] += 1
                k, n, _ = units[u]
                pe.wait_ge(w_loaded[u % SLOTS], arrival[u])
                return slot_view(u, k, n), k, n

            def flip_features(src, chunks):
                for j in range(chunks // 2):
                    r = (for_act, for_dve)[j % 2]
                    b, n = claim(r)
                    for c in range(2):
                        for t in range(T):
                            f = 2 * j + c
                            flip(b[:, (2 * c + t) * P:(2 * c + t + 1) * P], src[:, t, f * P:(f + 1) * P],
                                 r.full if c and t else None)
                for r in (for_act, for_dve):
                    pe.wait_ge(r.read, made[id(r)])

            def linear(count, src):
                for _ in range(count):
                    w, k, n = weights()
                    for t, r in enumerate((for_act, for_dve)):
                        b, _n = claim(r)
                        for c in range(k):
                            mm(b[:, 0:n], src[:, c, t * P:(t + 1) * P], w[:, c, :], c == 0, c == k - 1,
                               r.full if c == k - 1 else None)
                    owed[0] += 1

            def linear_dve(count, src, width):
                for _ in range(count):
                    w, k, n = weights()
                    for c0 in range(0, n, width):
                        for t in range(T):
                            b, _n = claim(for_dve)
                            for c in range(k):
                                mm(b[:, 0:width], src[:, c, t * P:(t + 1) * P], w[:, c, c0:c0 + width], c == 0,
                                   c == k - 1, for_dve.full if c == k - 1 else None)
                    owed[0] += 1

            def linear_deep(chunks, src):
                owner = [for_dve, for_dve, outputs, outputs]
                open_ = [claim(r)[0] for r in owner]
                c = 0
                while c < chunks:
                    w, k, _ = weights()
                    for kk in range(k):
                        last = c + kk == chunks - 1
                        for i, b in enumerate(open_):
                            t, hf = i // 2, i % 2
                            mm(b[:, :], src[:, c + kk, t * P:(t + 1) * P], w[:, kk, hf * 512:hf * 512 + 512],
                               c + kk == 0, last, owner[i].full if last else None)
                    c += k
                    owed[0] += 1

            def turns(items):
                for j in range(0, len(items), 2):
                    r = (for_act, for_dve)[j // 2 % 2]
                    b, _n = claim(r)
                    for i, it in enumerate(items[j:j + 2]):
                        for t in range(T):
                            flip(b[0:it["rows"], (2 * i + t) * P:(2 * i + t + 1) * P], it["src"][t],
                                 r.full if t and i == len(items[j:j + 2]) - 1 else None)
                for r in (for_act, for_dve):
                    pe.wait_ge(r.read, made[id(r)])

            def softmax_heads(jobs):
                out_bank = [None]
                pt = {}
                for i in range(len(jobs) + 2):
                    if i < len(jobs):
                        j = jobs[i]
                        b, _n = claim(for_dve)
                        rows = slice(j["base"], j["base"] + j["rows"])
                        q, k = turned(j["q"]), turned(j["k"])
                        mm(b[:, 0:P], q[rows, 0:P], k[rows, 0:P])
                        mm(b[:, P:3 * P], q[rows, P:S], k[rows, 0:S], full=for_dve.full)
                    if 1 <= i < len(jobs) + 1:
                        n = (i - 1) % NB
                        seen.more(p_ready)
                        b, pt[i - 1] = claim(for_act)
                        flip(b[:, 0:P], pr[:, n, 0:P])
                        flip(b[:, P:2 * P], pr[:, n, P:2 * P])
                        flip(b[:, 2 * P:3 * P], pr[:, n, 2 * P:3 * P], for_act.full)
                    if i >= 2:
                        j = jobs[i - 2]
                        n = (i - 2) % NB
                        if out_bank[0] is None:
                            out_bank[0] = claim(outputs)[0]
                        b = out_bank[0][j["obase"]:j["obase"] + HD, :]
                        start = j["first"]
                        if j["cmp"] is not None:
                            h, g = j["cmp"]
                            mm(b[:, 0:S], vcm[:, g, :], pcT[:, h, :], True, False)
                        pe.wait_ge(for_act.read, pt[i - 2])
                        mm(b[:, 0:S], j["v"][:, 0, :], pT[:, n, 0:S], start, False)
                        mm(b[:, P:S], j["v"][:, 1, :], pT[:, n, S:3 * P], False, j["last"],
                           outputs.full if j["done"] else None)
                        if j["done"]:
                            out_bank[0] = None

            def stick_heads():
                zb = {}
                out_bank = None
                stick_tile0.append(made[id(for_dve)])
                for i in range(NH + 2):
                    if i < NH:
                        rows = slice(HD * (i % 2), HD * (i % 2) + HD)
                        q, k = turned(i // 2)[rows, :], turned(4 + i // 2)[rows, :]
                        zb[i], _n = claim(for_dve)
                        mm(zb[i][:, 0:S], k[:, 0:P], q)
                        mm(zb[i][:, S:3 * P], k[:, P:S], q[:, P:S], False, True, for_dve.full)
                    if 1 <= i < NH + 1:
                        b, n = zb[i - 1], (i - 1) % NB
                        seen.more(sb_keep)
                        lk = sm[:, n, :]
                        ntri, nones = cst[:, C_NTRI:C_NTRI + P], cst[:, C_NONE:C_NONE + P]
                        mm(b[:, 0:S], ntri, lk[:, 0:S], False, True)
                        mm(b[:, P:S], nones, lk[:, S:3 * P], False, True)
                        mm(b[:, S:3 * P], ntri, lk[:, S:3 * P], False, True, sb_total)
                    if i >= 2:
                        h, n = i - 2, (i - 2) % NB
                        if h % 2 == 0:
                            out_bank, _n = claim(outputs)
                        b = out_bank[HD * (h % 2):HD * (h % 2) + HD, :]
                        v0 = SB0 + 2 * NH * HD + h * HD
                        seen.more(sb_ready)
                        mm(b[:, 0:S], proj[:, 0, v0:v0 + HD], pr[:, n, 0:S], True, False)
                        mm(b[:, P:S], proj[:, 1, v0:v0 + HD], pr[:, n, S:3 * P], False, True,
                           outputs.full if h % 2 else None)

            pe.wait_ge(const_loaded, 16)
            pe.wait_ge(rows_loaded, N_ROWS)
            pe.wait_ge(small_loaded, N_POOL_ROWS)
            used_rows = [80, 72, 104, 104, 120, 120]
            for part in (range(0, 4), range(4, 6)):
                for m in part:
                    if m % 4 == 0:
                        b, _n = claim(for_act)
                    flip(b[:, (m % 4) * P:(m % 4) * P + used_rows[m]], prow[0:used_rows[m], m, :],
                         for_act.full if m == part[-1] else None)
            b, _n = claim(for_dve)
            seen.more(pos_cast)
            flip(b[:, 0:4], posf[:, :], for_dve.full)

            def modulation(l):
                seen.more(cbc_ready)
                mod_bank, _n = claim(for_act)
                col = 0
                for u in range(12):
                    w, k, n = weights()
                    if u // 2 % 3 == 2:
                        b, _n = claim(for_dve)
                        for c in range(k):
                            mm(b[:, :], cbc[:, c, :], w[:, c, :], c == 0, c == k - 1, for_dve.full if c == k - 1 else None)
                    else:
                        for f in range(4):
                            for c in range(k):
                                mm(mod_bank[:, col:col + 1], w[:, c, f * P:(f + 1) * P], c_act[:, c:c + 1], c == 0,
                                   c == k - 1, for_act.full if col == 31 and c == k - 1 else None)
                            col += 1
                    owed[0] += 1

            for l in range(LAYERS1):
                modulation(l)
                seen.more(scaled)
                flip_features(wide, KD)
                linear(9, featT)
                for _ in range(6):
                    w, k, n = weights()
                    for t in range(T):
                        b, _n = claim(for_act)
                        for c in range(k):
                            mm(b[:, :], featT[:, c, t * P:(t + 1) * P], w[:, c, :], c == 0, c == k - 1,
                               for_act.full if c == k - 1 else None)
                    owed[0] += 1
                seen.more(scaled)
                flip_features(wide, 8)
                linear(2, featT)
                linear_dve(1, featT[:, 6:8, :], 512)
                seen.more(ready_dve)
                turns(mla_turns)
                softmax_heads(mla_jobs)
                turns(sb_turns)
                stick_heads()
                turns(moba_turns)
                softmax_heads(moba_jobs)
                pe.wait_ge(outputs.read, made[id(outputs)])
                for br in range(3):
                    linear_dve(1, oT[:, 4 * br:4 * br + 4, :], 512)
                seen.more(merged)
                flip_features(wide, KD)
                linear_dve(2, featT, 512)
                seen.more(scaled)
                flip_features(wide, KD)
                for _ in range(8):
                    w, k, n = weights()
                    for j in range(2):
                        b, _n = claim(for_act)
                        for f in range(2):
                            for c in range(k):
                                mm(b[:, f * S:(f + 1) * S], w[:, c, (2 * j + f) * P:(2 * j + f + 1) * P], featT[:, c, :],
                                   c == 0, c == k - 1, for_act.full if f and c == k - 1 else None)
                    owed[0] += 1
                pe.wait_ge(for_act.read, made[id(for_act)])
                linear_deep(32, hidT)

            for l in range(LAYERS2):
                seen.more(scaled)
                flip_features(wide, KD)
                linear(6, featT)
                seen.more(fox_lf)
                b, _n = claim(for_dve)
                lf = fox[:, 2, :].rearrange("p (t h) -> p t h", t=T)
                tri, ones = cst[:, C_TRI:C_TRI + P], cst[:, C_ONE:C_ONE + P]
                mm(b[:, 0:FOX], tri, lf[:, 0, :])
                mm(b[:, FOX:2 * FOX], tri, lf[:, 1, :], True, False)
                mm(b[:, FOX:2 * FOX], ones, lf[:, 0, :], False, True, for_dve.full)
                seen.more(ready_dve)
                b, _n = claim(for_dve)
                for a, c0 in enumerate((KC, VC)):
                    for t in range(T):
                        flip(b[:, (2 * a + t) * P:(2 * a + t + 1) * P], proj2[:, t, c0:c0 + P],
                             for_dve.full if a and t else None)
                turns(nsa_turns + dil_turns)
                turns(dk_turns)
                seen.more(win_ready)
                b, _n = claim(for_dve)
                for a in range(2):
                    w, k, n = weights()
                    for c in range(k):
                        mm(b[0:GRP * NCMP, a * CMP_H:(a + 1) * CMP_H], awin[:, a, c, :], w[:, c, :], c == 0, c == k - 1,
                           for_dve.full if a and c == k - 1 else None)
                    owed[0] += 1
                seen.more(ready_dve)
                turns(fox_turns)
                seen.more(gelu_out)
                b, n = claim(for_act)
                for m in range(4):
                    flip(b[:, m * 32:m * 32 + GRP * NCMP], gel[:, 0, m * P:(m + 1) * P], for_act.full if m == 3 else None)
                pe.wait_ge(for_act.read, n)
                b, n = claim(for_act)
                for g in range(GRP):
                    for c in range(2):
                        mm(b[HD * g:HD * g + HD, 0:NCMP], cw2[:, l, 0, c, :], hT[:, c, g * NCMP:(g + 1) * NCMP], c == 0, c == 1)
                for g in range(GRP):
                    for c in range(2):
                        mm(b[0:NCMP, HD * (g + 1):HD * (g + 2)], hT[:, 2 + c, g * NCMP:(g + 1) * NCMP], cw2[:, l, 1, c, :],
                           c == 0, c == 1, for_act.full if g and c else None)
                pe.wait_ge(for_act.read, n)
                for g in range(GRP):
                    b, _n = claim(for_dve)
                    rows = slice(HD * g, HD * g + HD)
                    for h in range(NSA // 2):
                        for t in range(T):
                            at = (t * NSA // 2 + h) * NCMP
                            mm(b[:, at:at + NCMP], turned(8 + h)[rows, t * P:(t + 1) * P], kcT[rows, :],
                               full=for_dve.full if h == NSA // 2 - 1 and t else None)
                seen.more(pc_out)
                for h2 in range(NSA // 2):
                    b, n = claim(for_act)
                    for i in range(2):
                        for t in range(T):
                            flip(b[0:NCMP, (2 * i + t) * P:(2 * i + t + 1) * P], pc[:, t, 2 * h2 + i, :],
                                 for_act.full if i and t else None)
                pe.wait_ge(for_act.read, n)
                softmax_heads(second_jobs)
                pe.wait_ge(outputs.read, made[id(outputs)])
                linear(2, oT)
                seen.more(scaled)
                flip_features(wide, KD)
                conv_tile0.append(made[id(for_dve)])
                for j in range(CH // 2):
                    w, k, n = weights()
                    for hf in range(2):
                        b, _n = claim(for_dve)
                        for f in range(2):
                            for c in range(k):
                                mm(b[:, f * S:(f + 1) * S], w[:, c, (2 * hf + f) * P:(2 * hf + f + 1) * P], featT[:, c, :],
                                   c == 0, c == k - 1, for_dve.full if f and c == k - 1 else None)
                    owed[0] += 1
                seen.more(conv_done, CH // 2)
                linear_deep(CH, hidT)

        @block.scalar
        def _(act):
            seen = Seen(act)
            chain, got, sums_done = [0], [0], [0]

            def link(ins):
                chain[0] += 1
                ins.then_inc(act_chain, 1)
                act.wait_ge(act_chain, chain[0])

            def tile():
                n = got[0]
                got[0] += 1
                act.wait_ge(for_act.full, n + 1)
                return for_act.banks[n % 3]

            def read(ins):
                ins.then_inc(for_act.read, 1)

            def copy_out(dst, src):
                read(act.activation(dst, src, ACT.Copy))

            def sums(src, s0, width):
                for t in range(T):
                    ins = act.activation(sq_scratch(t, width), src[:, t, :], ACT.Square, accum_out=stat[:, s0 + t:s0 + t + 1])
                    if t == T - 1:
                        ins.then_inc(squares, 1)
                sums_done[0] += 1

            def sq_scratch(t, width):
                return (pT, pr)[t][:, :, :].rearrange("p b n -> p (b n)")[:, 0:width]

            def features_out(dst0, chunks, gain=None, shift=None):
                for j in range(0, chunks // 2, 2):
                    b = tile()
                    for c in range(2):
                        f = 2 * j + c
                        kw = dict(scale=gain[:, f:f + 1]) if gain is not None else {}
                        if shift is not None:
                            kw["bias"] = shift[:, f:f + 1]
                        ins = act.activation(featT[:, dst0 + f, :], b[:, c * S:(c + 1) * S],
                                             ACT.Identity if shift is not None else ACT.Copy, **kw)
                        if c:
                            read(ins)

            def turns_out(items):
                for j in range(0, len(items), 4):
                    b = tile()
                    pair = items[j:j + 2]
                    for i, it in enumerate(pair):
                        ins = act.activation(turned(it["dst"])[0:it["rows"], :], b[0:it["rows"], i * S:(i + 1) * S], ACT.Copy,
                                             scale=it["scale"] or 1.0)
                    read(ins)

            def softmax_heads(jobs):
                for i in range(len(jobs) + 1):
                    if i < len(jobs):
                        j, n = jobs[i], i % NB
                        seen.more(s_masked)
                        for t, cols in enumerate((slice(0, P), slice(P, 3 * P))):
                            ins = act.activation(pr[:, n, cols], sm[:, n, cols], ACT.Exp, scale=j["scale"],
                                                 bias=mx[:, n, t:t + 1], accum_out=rs[:, n, t:t + 1])
                        ins.then_inc(s_exp, 1)
                    if i >= 1:
                        n = (i - 1) % NB
                        b = tile()
                        copy_out(pT[:, n, :], b[:, 0:3 * P])

            def stick_heads(l):
                for i in range(NH + 1):
                    if i < NH:
                        n, m = i % NB, stick_tile0[l] + i
                        act.wait_ge(for_dve.full, m + 1)
                        ab = pT[:, n, :]
                        link(act.activation(ab, for_dve.banks[m % 3][:, 0:3 * P], ACT.Abs))
                        link(act.activation(ab, ab, ACT.Exp, scale=-1.0))
                        act.activation(ab, ab, ACT.Ln, bias=1.0).then_inc(sb_log, 1)
                    if i >= 1:
                        n = (i - 1) % NB
                        seen.more(sb_masked)
                        act.activation(pr[:, n, :], pr[:, n, :], ACT.Exp).then_inc(sb_ready, 1)

            b = tile()
            for m, rows in enumerate((80, 72, 104, 104)):
                ins = act.activation(pcol[:, m, 0:rows], b[:, m * P:m * P + rows], ACT.Copy)
            link(ins)
            act.sem_inc(for_act.read, 1)
            act.sem_inc(c_exp, 1)
            b = tile()
            for m in (4, 5):
                ins = act.activation(pcol[:, m, 0:120], b[:, (m - 4) * P:(m - 4) * P + 120], ACT.Copy)
            link(ins)
            act.sem_inc(for_act.read, 1)
            act.sem_inc(c_exp, 1)
            seen.more(angles)
            act.activation(cs[:, :, :, :].rearrange("p a t f -> p (a t f)"), trig[:, 0:2, :].rearrange("p a f -> p (a f)"),
                           ACT.Sin).then_inc(sines, 1)
            act.preload_act_table_set("natural_log_exp_and_others")
            act.activation(c_tmp, pcol[:, 0, 72:80], ACT.Exp, scale=-1.0).then_inc(c_exp, 1)

            act.wait_ge(x_loaded, 16)
            for l in range(LAYERS1):
                b = tile()
                link(act.activation(mod[:, :], b[:, 0:32], ACT.Copy))
                act.sem_inc(for_act.read, 1)
                act.sem_inc(evac_act, 1)
                if l:
                    seen.more(x_ready)
                sums(x, 0, D)
                seen.more(evac_dve)
                features_out(0, KD, mod[:, 8:16], mod[:, 0:8])
                for u in range(9):
                    b = tile()
                    c0 = u * ATT_W
                    n = min(ATT_W, ATT - c0)
                    copy_out(proj[:, 0, c0:c0 + n], b[:, 0:n])
                act.wait_ge(for_act.read, got[0])
                act.sem_inc(evac_act, 1)
                seen.more(evac_dve)
                sums(proj[:, :, 0:QR], 4, QR)
                act.wait_ge(squares, sums_done[0])
                sums(proj[:, :, QR:D], 8, KVR)
                for u in range(6):
                    for t in range(T):
                        b = tile()
                        read(act.activation(gates[:, t, u * 512:u * 512 + 512], b[:, :], ACT.Exp, scale=-1.0))
                act.wait_ge(for_act.read, got[0])
                act.sem_inc(gate_exp, 1)
                gq = pcol[:, l, 16:24]
                features_out(0, 8, gq)
                for u in range(2):
                    b = tile()
                    copy_out(qmla[:, 0, u * UQ_W:(u + 1) * UQ_W], b[:, 0:UQ_W])
                act.wait_ge(for_act.read, got[0])
                act.sem_inc(evac_act, 1)
                turns_out(mla_turns)
                softmax_heads(mla_jobs)
                turns_out(sb_turns)
                stick_heads(l)
                turns_out(moba_turns)
                softmax_heads(moba_jobs)
                features_out(0, KD)
                seen.more(x_ready)
                sums(x, 0, D)
                features_out(0, KD, mod[:, 24:32], mod[:, 16:24])
                for u in range(16):
                    b = tile()
                    dst = hidT[:, 2 * u:2 * u + 2, :].rearrange("p c s -> p (c s)")
                    link(act.activation(dst, b[:, :], ACT.Relu))
                    read(act.activation(dst, dst, ACT.Square))
            if LAYERS1:
                seen.more(x_ready)
                sums(x, 0, D)
            for l in range(LAYERS2):
                if l or LAYERS1:
                    seen.more(x_ready)
                sums(x, 0, D)
                features_out(0, KD, pcol[:, 2 + l, 88:96])
                for u in range(6):
                    b = tile()
                    copy_out(proj2[:, 0, u * IN2_W:(u + 1) * IN2_W], b[:, 0:IN2_W])
                act.wait_ge(for_act.read, got[0])
                act.sem_inc(evac_act, 1)
                seen.more(fox_in)
                link(act.activation(fox[:, 1, :], fox[:, 0, :], ACT.Abs))
                link(act.activation(fox[:, 1, :], fox[:, 1, :], ACT.Exp, scale=-1.0))
                act.activation(fox[:, 1, :], fox[:, 1, :], ACT.Ln, bias=1.0).then_inc(fox_log, 1)
                seen.more(nsa_in)
                act.activation(gn[:, 1, :], gn[:, 0, :], ACT.Exp, scale=-1.0).then_inc(nsa_exp, 1)
                turns_out(nsa_turns + dil_turns)
                turns_out(dk_turns)
                turns_out(fox_turns)
                seen.more(gelu_in)
                act.activation(gel[:, 1, :], gel[:, 1, :], ACT.Exp, scale=-1.0).then_inc(gelu_exp, 1)
                b = tile()
                copy_out(hT[:, :, :], b[:, 0:P].rearrange("p (a n) -> p a n", n=32)[:, :, 0:GRP * NCMP])
                b = tile()
                act.activation(kcT[:, :], b[:, 0:NCMP], ACT.Copy)
                copy_out(vcm[:, :, :], b[0:NCMP, HD:3 * HD].rearrange("p (g d) -> p g d", g=GRP))
                seen.more(pc_in)
                act.activation(pc2[:, :, :, :], pc[:, :, :, :], ACT.Exp).then_inc(pc_exp, 1)
                for h2 in range(NSA // 2):
                    b = tile()
                    copy_out(pcT[:, 2 * h2:2 * h2 + 2, :], b[0:NCMP, :].rearrange("p (h s) -> p h s", s=S))
                softmax_heads(second_jobs)
                for u in range(2):
                    b = tile()
                    copy_out(wide[:, 0, u * 512:u * 512 + 512], b[:, :])
                seen.more(evac_dve)
                act.wait_ge(for_act.read, got[0])
                sums(wide, 0, D)
                seen.more(x_ready)
                sums(x, 0, D)
                features_out(0, KD, pcol[:, 2 + l, 96:104])
                w2c, bc = pcol[:, 4 + l, 0:44], pcol[:, 4 + l, 44:88]
                for j in range(CH // 2 + 1):
                    if j < CH // 2:
                        if j >= 2:
                            seen.more(conv_done)
                        for hf in range(2):
                            m = conv_tile0[l] + 2 * j + hf
                            act.wait_ge(for_dve.full, m + 1)
                            b = for_dve.banks[m % 3]
                            for f in range(2):
                                ch = hf * CH + 2 * j + f
                                ins = act.activation(cv[:, j % 2, hf, f * S:(f + 1) * S], b[:, f * S:(f + 1) * S],
                                                     ACT.Identity, scale=w2c[:, ch:ch + 1], bias=bc[:, ch:ch + 1])
                            ins.then_inc(conv_base, 1)
                    if j >= 1:
                        seen.more(silu_in)
                        m = (j - 1) % 2
                        act.activation(cv[:, m, 2, :], cv[:, m, 0, :], ACT.Exp, scale=-1.0).then_inc(silu_exp, 1)
                seen.more(conv_done, 2)
                seen.more(evac_dve)
                sums(wide, 0, D)

        @block.vector
        def _(dve):
            seen = Seen(dve)
            chain = [0]
            got = {}

            def link(ins):
                chain[0] += 1
                ins.then_inc(dve_chain, 1)
                dve.wait_ge(dve_chain, chain[0])

            def tile(r):
                n = got.get(id(r), 0)
                got[id(r)] = n + 1
                dve.wait_ge(r.full, n + 1)
                return r.banks[n % len(r.banks)]

            def read(r, ins):
                ins.then_inc(r.read, 1)

            def stored(r):
                dve.wait_ge(r.read, got[id(r)])

            def scale_tokens(dst, src, s0, signal=True):
                for t in range(T):
                    ins = dve.tensor_scalar(dst[:, t, :], src[:, t, :], stat[:, s0 + t:s0 + t + 1], None, ALU.mult)
                if signal:
                    ins.then_inc(scaled, 1)
                return ins

            def features_out(chunks, gain=None, shift=None):
                for j in range(1, chunks // 2, 2):
                    b = tile(for_dve)
                    for c in range(2):
                        f = 2 * j + c
                        src, dst = b[:, c * S:(c + 1) * S], featT[:, f, :]
                        if gain is None:
                            ins = dve.tensor_copy(dst, src)
                        elif shift is None:
                            ins = dve.tensor_scalar(dst, src, gain[:, f:f + 1], None, ALU.mult)
                        else:
                            ins = dve.tensor_scalar(dst, src, gain[:, f:f + 1], shift[:, f:f + 1], ALU.mult, ALU.add)
                    read(for_dve, ins)

            def turns_out(items):
                for j in range(2, len(items), 4):
                    b = tile(for_dve)
                    for i, it in enumerate(items[j:j + 2]):
                        ins = dve.tensor_scalar(turned(it["dst"])[0:it["rows"], :], b[0:it["rows"], i * S:(i + 1) * S],
                                                it["scale"] or 1.0, None, ALU.mult)
                    read(for_dve, ins)

            def rope(x1, x2, table0, width, dims):
                t0, t1, heads = dims
                shape = list(x1.shape)

                def trig_of(a):
                    v = cs[:, a, t0:t1, table0:table0 + width]
                    return v.unsqueeze(2).to_broadcast([P, t1 - t0, heads, width]) if len(shape) == 4 else \
                        v.rearrange("p t f -> p (t f)").unsqueeze(1).to_broadcast([P, heads, width])

                cos, sin = trig_of(0), trig_of(1)

                def scratch(a):
                    v = rope_t[:, a, 0:(t1 - t0) * heads * width]
                    return v.rearrange("p (t h f) -> p t h f", t=t1 - t0, h=heads) if len(shape) == 4 else \
                        v.rearrange("p (h f) -> p h f", h=heads)

                dve.tensor_tensor(scratch(0), x1, cos, ALU.mult)
                dve.tensor_tensor(scratch(1), x2, sin, ALU.mult)
                dve.tensor_tensor(scratch(2), x1, sin, ALU.mult)
                link(dve.tensor_tensor(scratch(3), x2, cos, ALU.mult))
                dve.tensor_tensor(x1, scratch(0), scratch(1), ALU.subtract)
                link(dve.tensor_tensor(x2, scratch(2), scratch(3), ALU.add))

            def softmax_heads(jobs):
                for i in range(len(jobs) + 2):
                    if i < len(jobs):
                        j, n = jobs[i], i % NB
                        b = tile(for_dve)
                        for t, (a, z) in enumerate(((0, P), (P, 3 * P))):
                            ins = dve.tensor_tensor_reduce(out=sm[:, n, a:z], in0=b[:, a:z], in1=cst[:, j["mask"] + a:j["mask"] + z],
                                                           scale=1.0, scalar=-3e38, op0=ALU.add, op1=ALU.max,
                                                           accum_out=mx[:, n, t:t + 1])
                        link(ins)
                        dve.sem_inc(for_dve.read, 1)
                        dve.tensor_scalar(mx[:, n, :], mx[:, n, :], -j["scale"], None, ALU.mult).then_inc(s_masked, 1)
                    if 1 <= i < len(jobs) + 1:
                        j, n = jobs[i - 1], (i - 1) % NB
                        seen.more(s_exp)
                        if j["weight"]:
                            for t, (a, z) in enumerate(((0, P), (P, 3 * P))):
                                ins = dve.tensor_tensor_reduce(out=pr[:, n, a:z], in0=pr[:, n, a:z], in1=cst[:, C_DW + a:C_DW + z],
                                                               scale=1.0, scalar=0.0, op0=ALU.mult, op1=ALU.add,
                                                               accum_out=rs[:, n, t:t + 1])
                            link(ins)
                        link(dve.reciprocal(rs[:, n, :], rs[:, n, :]))
                        if j["gate"] is not None:
                            g = gn[:, 1, :].rearrange("p (t n) -> p t n", t=T)[:, :, j["gate"]]
                            link(dve.tensor_tensor(rs[:, n, :], rs[:, n, :], g, ALU.mult))
                        dve.tensor_scalar(pr[:, n, 0:P], pr[:, n, 0:P], rs[:, n, 0:1], None, ALU.mult)
                        dve.tensor_scalar(pr[:, n, P:3 * P], pr[:, n, P:3 * P], rs[:, n, 1:2], None, ALU.mult)\
                           .then_inc(p_ready, 1)
                    if i >= 2 and jobs[i - 2]["done"]:
                        b = tile(outputs)
                        read(outputs, dve.tensor_copy(oT[:, jobs[i - 2]["chunk"], :], b[:, 0:S]))

            def stick_heads(l):
                part, z = T * 3 * D // NH, {}
                for i in range(NH + 2):
                    if i < NH:
                        n = i % NB
                        z[i] = b = tile(for_dve)
                        seen.more(sb_log)
                        dve.scalar_tensor_tensor(out=sm[:, n, :], in0=b[:, 0:3 * P], scalar=0.0, in1=pT[:, n, :],
                                                 op0=ALU.max, op1=ALU.add).then_inc(sb_raw, 1)
                        g = gf[:, part * i:part * (i + 1)]
                        if i == 0:
                            seen.more(gate_exp)
                        link(dve.tensor_scalar(g, g, 1.0, None, ALU.add))
                        dve.reciprocal(g, g)
                    if 1 <= i < NH + 1:
                        seen.more(sb_total)
                        link(dve.tensor_tensor(pr[:, (i - 1) % NB, :], z[i - 1][:, 0:3 * P],
                                               cst[:, C_SMASK:C_SMASK + 3 * P], ALU.add))
                        dve.sem_inc(for_dve.read, 1)
                        dve.sem_inc(sb_masked, 1)
                    if i >= 2 and i % 2:
                        b = tile(outputs)
                        read(outputs, dve.tensor_copy(oT[:, 4 + (i - 2) // 2, :], b[:, 0:S]))

            dve.wait_ge(const_loaded, 16)
            dve.wait_ge(rows_loaded, N_ROWS)
            dve.wait_ge(small_loaded, N_POOL_ROWS)
            dve.tensor_copy(posf[:, :], posi[:, :]).then_inc(pos_cast, 1)
            b = tile(for_dve)
            link(dve.tensor_copy(posc[:, :], b[:, 0:4]))
            dve.sem_inc(for_dve.read, 1)
            for t in range(T):
                dve.tensor_scalar(trig[:, 2, 32 * t:32 * t + 24], cst[:, C_INV:C_INV + 24], posc[:, t:t + 1], None, ALU.mult)
                link(dve.tensor_scalar(trig[:, 2, 32 * t + 24:32 * t + 32], cst[:, C_INV + 24:C_INV + 32],
                                       posc[:, 2 + t:3 + t], None, ALU.mult))
            turnsn = tiny[:, 0:64]
            for a, ahead in ((1, 0.0), (0, 0.25)):
                link(dve.tensor_scalar(turnsn, trig[:, 2, :], 1 / TWO_PI, ahead, ALU.mult, ALU.add))
                link(dve.tensor_scalar(turnsn, turnsn, ROUNDER, None, ALU.add))
                link(dve.tensor_scalar(turnsn, turnsn, -ROUNDER, None, ALU.add))
                link(dve.scalar_tensor_tensor(out=trig[:, a, :], in0=turnsn, scalar=-PI_A, in1=trig[:, 2, :], op0=ALU.mult, op1=ALU.add))
                for part in (PI_B, PI_C):
                    link(dve.scalar_tensor_tensor(out=trig[:, a, :], in0=turnsn, scalar=-part, in1=trig[:, a, :], op0=ALU.mult, op1=ALU.add))
                if ahead:
                    link(dve.tensor_scalar(trig[:, a, :], trig[:, a, :], TWO_PI * ahead, None, ALU.add))
                link(dve.tensor_scalar(trig[:, a, :], trig[:, a, :], PI_SAFE, -PI_SAFE, ALU.min, ALU.max))
            dve.sem_inc(angles, 1)
            seen.more(c_exp, 3)
            link(dve.tensor_scalar(c_tmp, c_tmp, 1.0, None, ALU.add))
            link(dve.reciprocal(c_tmp, c_tmp))
            link(dve.tensor_tensor(c_act, c_tmp, pcol[:, 0, 72:80], ALU.mult))
            seen.more(sines)
            dve.wait_ge(x_loaded, 16)

            for l in range(LAYERS1):
                dve.tensor_copy(cbc, c_act.unsqueeze(2).to_broadcast([P, KD, P])).then_inc(cbc_ready, 1)
                seen.more(bc_loaded, 32)
                for g in range(2):
                    for hf in range(2):
                        b = tile(for_dve)
                        dst = rowbc[:, g, hf * 512:hf * 512 + 512]
                        read(for_dve, dve.tensor_tensor(dst, b[:, :], dst, ALU.add))
                seen.more(evac_act)
                dve.tensor_tensor(mod[:, 0:16], mod[:, 0:16], pcol[:, l, 24:40], ALU.add)
                link(dve.tensor_tensor(mod[:, 16:32], mod[:, 16:32], pcol[:, l, 48:64], ALU.add))
                dve.scalar_tensor_tensor(out=mod[:, 8:16], in0=mod[:, 8:16], scalar=1.0, in1=pcol[:, l, 0:8], op0=ALU.add, op1=ALU.mult)
                link(dve.scalar_tensor_tensor(out=mod[:, 24:32], in0=mod[:, 24:32], scalar=1.0, in1=pcol[:, l, 8:16],
                                              op0=ALU.add, op1=ALU.mult))
                dve.sem_inc(evac_dve, 1)
                seen.more(rstd_ready)
                scale_tokens(wide, x, 2)
                features_out(KD, mod[:, 8:16], mod[:, 0:8])
                for u in range(9):
                    b = tile(for_dve)
                    c0 = u * ATT_W
                    n = min(ATT_W, ATT - c0)
                    read(for_dve, dve.tensor_copy(proj[:, 1, c0:c0 + n], b[:, 0:n]))
                stored(for_dve)
                dve.sem_inc(evac_dve, 1)
                seen.more(evac_act)
                seen.more(rstd_ready, 2)
                scale_tokens(wide[:, :, 0:QR], proj[:, :, 0:QR], 6, False)
                scale_tokens(wide[:, :, QR:D], proj[:, :, QR:D], 10)
                kpe = proj[:, :, QR + KVR:SB0].rearrange("p t (h e) -> p t h e", h=1)
                rope(kpe[:, :, :, 0:16], kpe[:, :, :, 16:32], 0, 16, (0, T, 1))
                qk = proj[:, :, MB0:MB0 + 2 * NH * HD].rearrange("p t (h e) -> p t h e", e=HD)
                rope(qk[:, :, :, 0:8], qk[:, :, :, 8:16], 16, 8, (0, T, 2 * NH))
                for t in range(T):
                    dve.tensor_copy(k_mla[:, t, :, NOPE:QK],
                                    proj[:, t, QR + KVR:SB0].unsqueeze(1).to_broadcast([P, NH, ROPE]))
                features_out(8, pcol[:, l, 16:24])
                for u in range(2):
                    b = tile(for_dve)
                    read(for_dve, dve.tensor_copy(qmla[:, 1, u * UQ_W:(u + 1) * UQ_W], b[:, 0:UQ_W]))
                for hf in range(2):
                    for t in range(T):
                        b = tile(for_dve)
                        kv = b[:, :].rearrange("p (h e) -> p h e", e=NOPE + HD)
                        dve.tensor_copy(k_mla[:, t, 4 * hf:4 * hf + 4, 0:NOPE], kv[:, :, 0:NOPE])
                        read(for_dve, dve.tensor_copy(
                            v_mla[:, t, 4 * hf * HD:4 * (hf + 1) * HD].rearrange("p (h e) -> p h e", e=HD), kv[:, :, NOPE:]))
                stored(for_dve)
                seen.more(evac_act)
                qh = qmla.rearrange("p t (h e) -> p t h e", e=QK)
                rope(qh[:, :, :, NOPE:NOPE + 16], qh[:, :, :, NOPE + 16:QK], 0, 16, (0, T, NH))
                dve.sem_inc(ready_dve, 1)
                turns_out(mla_turns)
                softmax_heads(mla_jobs)
                turns_out(sb_turns)
                stick_heads(l)
                turns_out(moba_turns)
                softmax_heads(moba_jobs)
                dve.wait_ge(outputs.read, got[id(outputs)])
                tmp = pr[:, :, :].rearrange("p b n -> p (b n)")
                k = 0
                for br in range(3):
                    for hf in range(2):
                        for t in range(T):
                            b = tile(for_dve)
                            g = gates[:, t, br * D + hf * 512:br * D + hf * 512 + 512]
                            dst = wide[:, t, hf * 512:hf * 512 + 512]
                            if br == 0:
                                read(for_dve, dve.tensor_tensor(dst, b[:, :], g, ALU.mult))
                                continue
                            tm = tmp[:, 512 * (k % 2):512 * (k % 2) + 512]
                            k += 1
                            read(for_dve, dve.tensor_tensor(tm, b[:, :], g, ALU.mult))
                            stored(for_dve)
                            ins = dve.tensor_tensor(dst, dst, tm, ALU.add)
                link(ins)
                dve.sem_inc(merged, 1)
                features_out(KD)

                def add_gated(g, order):
                    k = 0
                    for r, t, hf in order:
                        b = tile(r)
                        cols = slice(hf * 512, hf * 512 + 512)
                        tm = tmp[:, 512 * (k % 2):512 * (k % 2) + 512]
                        k += 1
                        read(r, dve.tensor_tensor(tm, b[:, :], rowbc[:, g, cols], ALU.mult))
                        stored(r)
                        ins = dve.tensor_tensor(x[:, t, cols], x[:, t, cols], tm, ALU.add)
                    ins.then_inc(x_ready, 1)
                    dve.wait_ge(x_ready, 2 * l + g + 1)

                add_gated(0, [(for_dve, t, hf) for hf in range(2) for t in range(T)])
                seen.more(rstd_ready)
                scale_tokens(wide, x, 2)
                features_out(KD, mod[:, 24:32], mod[:, 16:24])
                add_gated(1, [(for_dve, 0, 0), (for_dve, 0, 1), (outputs, 1, 0), (outputs, 1, 1)])
            if LAYERS1:
                seen.more(rstd_ready)
                seen.more(bc_loaded, 16)
                for t in range(T):
                    ins = dve.scalar_tensor_tensor(out=x[:, t, :], in0=x[:, t, :], scalar=stat[:, 2 + t:3 + t],
                                                   in1=rowbc[:, 0, :], op0=ALU.mult, op1=ALU.mult)
                ins.then_inc(x_ready, 1)
                dve.wait_ge(x_ready, 2 * LAYERS1 + 1)
            x0 = 2 * LAYERS1 + (LAYERS1 > 0)

            for l in range(LAYERS2):
                seen.more(rstd_ready)
                scale_tokens(wide, x, 2)
                features_out(KD, pcol[:, 2 + l, 88:96])
                for u in range(6):
                    b = tile(for_dve)
                    read(for_dve, dve.tensor_copy(proj2[:, 1, u * IN2_W:(u + 1) * IN2_W], b[:, 0:IN2_W]))
                stored(for_dve)
                seen.more(evac_act)
                fv = lambda a: fox[:, a, :].rearrange("p (t h) -> p t h", t=T)
                dve.tensor_tensor(fv(0), proj2[:, :, FG:FG + FOX],
                                  small[:, l, 0:FOX].unsqueeze(1).to_broadcast([P, T, FOX]), ALU.add).then_inc(fox_in, 1)
                dve.tensor_tensor(gn[:, 0, :].rearrange("p (t n) -> p t n", t=T), proj2[:, :, NG:NG + 3 * NSA],
                                  small[:, l, FOX:].unsqueeze(1).to_broadcast([P, T, 3 * NSA]), ALU.add).then_inc(nsa_in, 1)
                for base, heads in ((NQ, NSA), (DQ, 2 * DIL)):
                    v = proj2[:, :, base:base + heads * HD].rearrange("p t (h e) -> p t h e", e=HD)
                    rope(v[:, :, :, 0:8], v[:, :, :, 8:16], 24, 8, (0, T, heads))
                for t in range(T):
                    for base in (KC, KS, KW):
                        v = proj2[:, t, base:base + GRP * HD].rearrange("p (h e) -> p h e", e=HD)
                        rope(v[:, :, 0:8], v[:, :, 8:16], 24, 8, (t, t + 1, GRP))
                for t in range(T):
                    for g in range(GRP):
                        q0 = NQ + 4 * g * HD
                        ins = dve.tensor_copy(nq[:, t, :, g, :], proj2[:, t, q0:q0 + 4 * HD].rearrange("p (j d) -> p j d", d=HD))
                link(ins)
                dve.sem_inc(ready_dve, 1)
                seen.more(fox_log)
                dve.scalar_tensor_tensor(out=fox[:, 2, :], in0=fox[:, 0, :], scalar=0.0, in1=fox[:, 1, :],
                                         op0=ALU.min, op1=ALU.subtract).then_inc(fox_lf, 1)
                for t in range(T):
                    heads = lambda c0: proj2[:, t, c0:c0 + FOX * HD].rearrange("p (h e) -> p h e", e=HD)
                    dve.tensor_scalar(faug[:, t, 0, :, 0:HD], heads(FQ), 1 / math.sqrt(HD), None, ALU.mult)
                    dve.tensor_copy(faug[:, t, 1, :, 0:HD], heads(FK))
                    dve.memset(faug[:, t, 0, :, HD + 1], 1.0)
                    dve.memset(faug[:, t, 1, :, HD], 1.0)
                b = tile(for_dve)
                sums_ = b[:, 0:T * FOX].rearrange("p (t h) -> p t h", t=T)
                dve.tensor_copy(faug[:, :, 0, :, HD], sums_)
                link(dve.tensor_scalar(faug[:, :, 1, :, HD + 1], sums_, -1.0, None, ALU.mult))
                dve.sem_inc(for_dve.read, 1)
                dve.sem_inc(ready_dve, 1)
                b = tile(for_dve)
                src = b[:, :].rearrange("p (a s) -> p a s", a=2)
                for g in range(GRP):
                    rows = slice(HD * g, HD * g + HD)
                    dve.tensor_copy(U[0:HD, :, g, :], src[rows, :, :])
                    ins = dve.tensor_copy(U[HD:P, :, g, 0:S - 1], src[rows, :, 1:S])
                link(ins)
                dve.sem_inc(for_dve.read, 1)
                for a in range(2):
                    for g in range(GRP):
                        for ch in range(2):
                            win = U[:, a, g, :].rearrange("p (n r) -> p r n", r=CMP_ST)[:, 0:CMP_ST:2, ch:ch + NCMP]
                            pos = pcol[:, 4 + l, 88 + 16 * a + 8 * ch:88 + 16 * a + 8 * ch + 8]
                            ins = dve.tensor_tensor(awin[:, a, 8 * ch:8 * ch + 8, g * NCMP:(g + 1) * NCMP], win,
                                                    pos.unsqueeze(2).to_broadcast([P, 8, NCMP]), ALU.add)
                ins.then_inc(win_ready, 1)
                turns_out(nsa_turns + dil_turns)
                seen.more(nsa_exp)
                link(dve.tensor_scalar(gn[:, 1, :], gn[:, 1, :], 1.0, None, ALU.add))
                link(dve.reciprocal(gn[:, 1, :], gn[:, 1, :]))
                b = tile(for_dve)
                link(dve.tensor_copy(gel[:, 0, :], b[0:GRP * NCMP, :]))
                dve.sem_inc(for_dve.read, 1)
                two = 2 * math.sqrt(2 / math.pi)
                link(dve.tensor_tensor(gel[:, 1, :], gel[:, 0, :], gel[:, 0, :], ALU.mult))
                link(dve.tensor_scalar(gel[:, 1, :], gel[:, 1, :], 0.044715 * two, two, ALU.mult, ALU.add))
                dve.tensor_tensor(gel[:, 1, :], gel[:, 1, :], gel[:, 0, :], ALU.mult).then_inc(gelu_in, 1)
                turns_out(fox_turns)
                seen.more(gelu_exp)
                link(dve.tensor_scalar(gel[:, 1, :], gel[:, 1, :], 1.0, None, ALU.add))
                link(dve.reciprocal(gel[:, 1, :], gel[:, 1, :]))
                dve.tensor_tensor(gel[:, 0, :], gel[:, 0, :], gel[:, 1, :], ALU.mult).then_inc(gelu_out, 1)
                for g in range(GRP):
                    b = tile(for_dve)
                    for t in range(T):
                        n = NSA // 2 * NCMP
                        ins = dve.tensor_scalar(pc[:, t, 4 * g:4 * g + 4, :].rearrange("p h n -> p (h n)"),
                                                b[:, t * n:(t + 1) * n], 1 / math.sqrt(HD), None, ALU.mult)
                    read(for_dve, ins)
                stored(for_dve)
                wide_of = lambda v: v.unsqueeze(3).to_broadcast([P, T, NSA, NCMP])
                mask_of = lambda c0: cst[:, c0:c0 + T * NCMP].rearrange("p (t n) -> p t n", t=T).unsqueeze(2)\
                    .to_broadcast([P, T, NSA, NCMP])
                link(dve.tensor_tensor(pc, pc, mask_of(C_CADD), ALU.add))
                link(dve.tensor_reduce(pcs, pc, axis=AX.X, op=ALU.max))
                dve.tensor_tensor(pc, pc, wide_of(pcs), ALU.subtract).then_inc(pc_in, 1)
                seen.more(pc_exp)
                link(dve.tensor_tensor(pc2, pc2, mask_of(C_CMASK), ALU.mult))
                link(dve.tensor_reduce(pcs, pc2, axis=AX.X, op=ALU.add))
                link(dve.tensor_scalar(pcs, pcs, 1e-30, None, ALU.max))
                link(dve.reciprocal(pcs, pcs))
                gc = gn[:, 1, :].rearrange("p (t h b) -> p t h b", t=T, b=3)[:, :, :, 0]
                link(dve.tensor_tensor(pcs, pcs, gc, ALU.mult))
                dve.tensor_tensor(pc, pc2, wide_of(pcs), ALU.mult).then_inc(pc_out, 1)
                softmax_heads(second_jobs)
                for u in range(2):
                    b = tile(for_dve)
                    read(for_dve, dve.tensor_copy(wide[:, 1, u * 512:u * 512 + 512], b[:, :]))
                stored(for_dve)
                dve.sem_inc(evac_dve, 1)

                def add_normed(g):
                    if g == 0:
                        seen.more(bc_loaded, 32)
                    seen.more(rstd_ready)
                    for t in range(T):
                        link(dve.scalar_tensor_tensor(out=wide[:, t, :], in0=wide[:, t, :], scalar=stat[:, 2 + t:3 + t],
                                                      in1=rowbc[:, g, :], op0=ALU.mult, op1=ALU.mult))
                        ins = dve.tensor_tensor(x[:, t, :], x[:, t, :], wide[:, t, :], ALU.add)
                    ins.then_inc(x_ready, 1)
                    dve.wait_ge(x_ready, x0 + 2 * l + g + 1)

                add_normed(0)
                seen.more(rstd_ready)
                scale_tokens(wide, x, 2)
                features_out(KD, pcol[:, 2 + l, 96:104])
                w0c, w1c = pcol[:, 2 + l, 0:44], pcol[:, 2 + l, 44:88]
                for j in range(CH // 2 + 1):
                    if j < CH // 2:
                        for hf in range(2):
                            b = tile(for_dve)
                            seen.more(conv_base)
                            for f in range(2):
                                ch = hf * CH + 2 * j + f
                                dst = cv[:, j % 2, hf, f * S:(f + 1) * S]
                                link(dve.scalar_tensor_tensor(out=dst[:, 1:S], in0=b[:, f * S:(f + 1) * S - 1], scalar=w1c[:, ch:ch + 1],
                                                              in1=dst[:, 1:S], op0=ALU.mult, op1=ALU.add))
                                link(dve.scalar_tensor_tensor(out=dst[:, 2:S], in0=b[:, f * S:(f + 1) * S - 2], scalar=w0c[:, ch:ch + 1],
                                                              in1=dst[:, 2:S], op0=ALU.mult, op1=ALU.add))
                            dve.sem_inc(for_dve.read, 1)
                            if hf == 0:
                                dve.sem_inc(silu_in, 1)
                    if j >= 1:
                        m = (j - 1) % 2
                        seen.more(silu_exp)
                        link(dve.tensor_tensor(cv[:, m, 0, :], cv[:, m, 0, :], cv[:, m, 1, :], ALU.mult))
                        link(dve.tensor_scalar(cv[:, m, 2, :], cv[:, m, 2, :], 1.0, None, ALU.add))
                        link(dve.reciprocal(cv[:, m, 2, :], cv[:, m, 2, :]))
                        dst = hidT[:, 2 * (j - 1):2 * j, :].rearrange("p c s -> p (c s)")
                        dve.tensor_tensor(dst, cv[:, m, 0, :], cv[:, m, 2, :], ALU.mult).then_inc(conv_done, 1)
                for r, t, hf in ((for_dve, 0, 0), (for_dve, 0, 1), (outputs, 1, 0), (outputs, 1, 1)):
                    b = tile(r)
                    read(r, dve.tensor_copy(wide[:, t, hf * 512:hf * 512 + 512], b[:, :]))
                stored(for_dve)
                stored(outputs)
                dve.sem_inc(evac_dve, 1)
                add_normed(1)

    return nc


NAMES = ["x", "c", "positions", "w_ada", "b_ada", "norm1_g", "norm2_g", "w_in", "q_norm_g", "w_uq",
         "kv_norm_g", "w_ukv", "w_o_mla", "w_o_sb", "w_o_moba", "w_out", "w_ff1", "w_ff2", "final_norm_g",
         "positions_2", "attn_pre_norm_2", "attn_post_norm_2", "ffn_pre_norm_2", "ffn_post_norm_2",
         "w_in_2", "b_forget_2", "b_nsa_gate_2", "cmp_pos_k_2", "cmp_w1_k_2", "cmp_w2_k_2", "cmp_pos_v_2",
         "cmp_w1_v_2", "cmp_w2_v_2", "w_out_2", "w_up_2", "conv_w_2", "conv_b_2", "w_down_2"]


def kernel(**inputs):
    import concourse.bacc as bacc
    from concourse.bass_utils import run_bass_kernel_spmd

    nc = bacc.Bacc("TRN2", target_bir_lowering=False, num_devices=1)
    arrays, args = {}, []
    for name in NAMES:
        a = np.ascontiguousarray(inputs[name])
        arrays[f"in_{name}"] = a
        args.append(nc.dram_tensor(f"in_{name}", a.shape, mybir.dt.from_np(a.dtype), kind="ExternalInput").ap())
    table = constants()
    arrays["table"] = table
    args.append(nc.dram_tensor("table", table.shape, F32, kind="ExternalInput").ap())
    args.append(nc.dram_tensor("out_0", (1, S, D), F32, kind="ExternalOutput").ap())
    two_blocks(nc, *args)
    r = run_bass_kernel_spmd(nc, [arrays], core_ids=[0])
    return r.results[0]["out_0"]
```

```python
import contextlib
import math

import numpy as np
import concourse.bass as bass
from concourse import mybir

F32 = mybir.dt.float32
I32 = mybir.dt.int32
ACT = mybir.ActivationFunctionType
ALU = mybir.AluOpType
AX = mybir.AxisListType

P = 128
S, D, DEPTH = 256, 1024, 2
T = S // P
KD = D // P
EPS = 1e-6
NEG = -1e30
THETA = 500000.0
HD = 64

NH = 8
NOPE, ROPE = 64, 32
QK = NOPE + ROPE
QR, KVR = 768, 256
ATT = QR + KVR + ROPE + 6 * NH * HD
SB0 = QR + KVR + ROPE
MB0 = SB0 + 3 * NH * HD
D_IN = ATT + 3 * D
FF1 = 4 * D
ATT_W = 464
UQ_W = NH * QK // 2

FOX, NSA, GRP, DIL = 4, 8, 2, 4
FQ, FK, FV, FG = 0, FOX * HD, 2 * FOX * HD, 3 * FOX * HD
NQ = FG + FOX
KC = NQ + NSA * HD
VC, KS, VS, KW, VW = (KC + n * GRP * HD for n in range(1, 6))
NG = KC + 6 * GRP * HD
DQ = NG + 3 * NSA
DK, DV = DQ + DIL * HD, DQ + 2 * DIL * HD
N_IN = DV + DIL * HD
IN2_W = N_IN // 6
CMP_L, CMP_ST, CMP_H = 32, 16, 256
NCMP = (S - CMP_L) // CMP_ST + 1
FF2 = 2816
CH = FF2 // P
WU = 4096
SLOTS = 3
NSM, NPT = 6, 4
AUG = HD + 2

C_ID, C_ONE, C_TRI, C_NTRI, C_NONE = (n * P for n in range(5))
C_CAUS = 5 * P
C_DMASK = C_CAUS + 3 * P
C_DW = C_DMASK + 3 * P
C_CMASK = C_DW + 3 * P
C_CADD = C_CMASK + T * NCMP
C_SMASK = C_CADD + T * NCMP
C_INV = C_SMASK + 3 * P
C_N = C_INV + 32

TWO_PI = 2 * math.pi
PI_A = 6.28125
PI_B = float(np.float32(np.floor((TWO_PI - PI_A) * 2**20) / 2**20))
PI_C = float(np.float32(TWO_PI - PI_A - PI_B))
ROUNDER = 12582912.0
PI_SAFE = 3.1415925


def constants():
    c = np.zeros((P, C_N), np.float32)
    i = np.arange(P)
    c[:, C_ID:C_ID + P] = np.eye(P)
    c[:, C_ONE:C_ONE + P] = 1.0
    c[:, C_TRI:C_TRI + P] = i[:, None] <= i[None, :]
    c[:, C_NTRI:C_NTRI + P] = -(i[:, None] >= i[None, :]).astype(np.float32)
    c[:, C_NONE:C_NONE + P] = -1.0
    q = np.concatenate([np.broadcast_to(i[:, None], (P, P)), np.broadcast_to(P + i[:, None], (P, S))], 1)
    k = np.concatenate([np.broadcast_to(i[None], (P, P)), np.broadcast_to(np.arange(S)[None], (P, S))], 1)
    back = q - k
    c[:, C_CAUS:C_CAUS + 3 * P] = np.where(back >= 0, 0.0, NEG)
    times = sum(((back >= 0) & (back % d == 0) & (back <= w)).astype(np.float32)
                for w, d in ((128, 1), (512, 4), (2048, 16)))
    c[:, C_DMASK:C_DMASK + 3 * P] = np.where(times > 0, 0.0, NEG)
    c[:, C_DW:C_DW + 3 * P] = times
    after = np.where(i[None, :] > i[:, None], 0.0, NEG)
    c[:, C_SMASK:C_SMASK + P] = after
    c[:, C_SMASK + 2 * P:C_SMASK + 3 * P] = after
    ends = np.arange(NCMP) * CMP_ST + CMP_L - 1
    for t in range(T):
        seen = ends[None, :] <= t * P + i[:, None]
        c[:, C_CMASK + t * NCMP:C_CMASK + (t + 1) * NCMP] = seen
        c[:, C_CADD + t * NCMP:C_CADD + (t + 1) * NCMP] = np.where(seen, 0.0, NEG)
    for at, rot in ((0, ROPE), (16, HD // 4), (24, HD // 4)):
        inv = np.float32(THETA) ** (-np.arange(0, rot, 2, dtype=np.float32) / np.float32(rot))
        c[:, C_INV + at:C_INV + at + rot // 2] = inv
    return c


def two_blocks(nc, x_in, c_in, positions, w_ada, b_ada, norm1_g, norm2_g, w_in, q_norm_g, w_uq,
               kv_norm_g, w_ukv, w_o_mla, w_o_sb, w_o_moba, w_out, w_ff1, w_ff2, final_norm_g,
               positions_2, attn_pre, attn_post, ffn_pre, ffn_post, w_in_2, b_forget, b_nsa,
               pos_k, cw1_k, cw2_k, pos_v, cw1_v, cw2_v, w_out_2, w_up, conv_w, conv_b, w_down,
               table, out, LAYERS1=DEPTH, LAYERS2=DEPTH):
    ctx = contextlib.ExitStack()
    with ctx:
        def sb(name, shape, dt=F32):
            return ctx.enter_context(nc.sbuf_tensor(name, shape, dt))

        def sem(name):
            return ctx.enter_context(nc.semaphore(name))

        cst = sb("cst", [P, C_N])
        x = sb("x", [P, T, D])
        wide = sb("wide", [P, T, D])
        featT = sb("featT", [P, KD, S])
        big = sb("big", [P, 33 * S])
        gates = sb("gates", [P, T, 3 * D])
        kvm = sb("kvm", [P, T, NH * (QK + HD)])
        oT = sb("oT", [P, 12, S])
        sm = sb("sm", [P, NSM, 3 * P])
        pT = sb("pT", [P, NPT, 3 * P])
        qz = sb("qz", [P, 12, S])
        ada = sb("ada", [P, 2, 512])
        rowbc = sb("rowbc", [P, 2, D])
        pcol = sb("pcol", [P, 6, P])
        mod = sb("mod", [P, 32])
        small = sb("small", [P, DEPTH, FOX + 3 * NSA])
        cw2 = sb("cw2", [P, DEPTH, 2, 2, HD])
        posi = sb("posi", [4, P], I32)
        posf = sb("posf", [4, P])
        cs = sb("cs", [P, 2, T, 32])
        trig = sb("trig", [P, 3, T * 32])
        posc = sb("posc", [P, 4])
        tiny = sb("tiny", [P, 64])
        stat = sb("stat", [P, 24])
        mx = sb("mx", [P, NSM, T])
        rs = sb("rs", [P, NSM, T])
        half = sb("half", [P, T])
        fox = sb("fox", [P, 3, T * FOX])
        gn = sb("gn", [P, 2, T * 3 * NSA])
        ring = sb("ring", [P, SLOTS, WU])

        proj = big[:, 0:T * ATT].rearrange("p (t n) -> p t n", t=T)
        proj2 = big[:, 0:T * N_IN].rearrange("p (t n) -> p t n", t=T)
        hidT = big[:, 0:32 * S].rearrange("p (c s) -> p c s", s=S)
        qmla = proj[:, :, 0:QR]
        k_mla = kvm[:, :, 0:NH * QK].rearrange("p t (h e) -> p t h e", e=QK)
        v_mla = kvm[:, :, NH * QK:]
        c_act = tiny[:, 0:8]
        c_tmp = tiny[:, 8:16]
        prow = big[:, 0:6 * P].rearrange("p (m n) -> p m n", m=6)
        rope_t = sm[:, :, :].rearrange("p b n -> p (b n)")[:, 0:4 * 256].rearrange("p (a n) -> p a n", a=4)
        wideT = wide[:, :, :].rearrange("p t n -> p (t n)").rearrange("p (c s) -> p c s", s=S)
        ident = cst[:, C_ID:C_ID + P]
        gf = gates[:, :, :].rearrange("p t n -> p (t n)")
        faug = gf[:, 0:T * 2 * FOX * AUG].rearrange("p (t a h e) -> p t a h e", t=T, a=2, h=FOX)
        UOFF = T * 2 * FOX * AUG
        U = gf[:, UOFF:UOFF + 2 * GRP * S].rearrange("p (a g s) -> p a g s", a=2, g=GRP)
        AOFF = UOFF + 2 * GRP * S
        awin = gf[:, AOFF:AOFF + 2 * 16 * GRP * NCMP].rearrange("p (a c n) -> p a c n", a=2, c=16)
        GOFF = AOFF + 2 * 16 * GRP * NCMP
        gel = gf[0:GRP * NCMP, GOFF:GOFF + 512]
        HOFF = GOFF + 3 * 512
        hT = gf[:, HOFF:HOFF + 4 * GRP * NCMP].rearrange("p (a n) -> p a n", a=4)
        KOFF = HOFF + 4 * GRP * NCMP
        kcT = gf[:, KOFF:KOFF + NCMP]
        vcm = gf[:, KOFF + 16:KOFF + 16 + GRP * HD].rearrange("p (g d) -> p g d", g=GRP)
        nq = gf[:, KOFF + 16 + GRP * HD:KOFF + 16 + GRP * HD + T * NSA * HD].rearrange(
            "p (t j g d) -> p t j g d", t=T, j=4, g=GRP)
        kf = kvm[:, :, :].rearrange("p t n -> p (t n)")
        pc = kf[:, 0:T * NSA * NCMP].rearrange("p (t h n) -> p t h n", t=T, h=NSA)
        pc2 = kf[:, 240:240 + T * NSA * NCMP].rearrange("p (t h n) -> p t h n", t=T, h=NSA)
        pcs = kf[:, 480:480 + T * NSA].rearrange("p (t h) -> p t h", t=T)
        pcT = kf[:, 496:496 + NSA * S].rearrange("p (h s) -> p h s", s=S)
        cv = gf[:, 0:2 * 2 * 512].rearrange("p (b a n) -> p b a n", b=2, a=2)

        banks = [ctx.enter_context(nc.psum_tensor(f"bank{n}", [P, 512], F32)) for n in range(8)]

        class Tiles:

            def __init__(self, name, own):
                self.banks = own
                self.full = sem(f"{name}_full")
                self.read = sem(f"{name}_read")

        for_act = Tiles("for_act", banks[0:2])
        for_dve = Tiles("for_dve", banks[2:6])
        outputs = Tiles("outputs", banks[6:8])

        w_used = sem("w_used")
        w_loaded = [sem(f"w_loaded{n}") for n in range(SLOTS)]
        const_loaded = sem("const_loaded")
        rows_loaded = sem("rows_loaded")
        small_loaded = sem("small_loaded")
        x_loaded = sem("x_loaded")
        bc_loaded = sem("bc_loaded")
        out_stored = sem("out_stored")
        act_chain, dve_chain, pool_chain = sem("act_chain"), sem("dve_chain"), sem("pool_chain")
        pos_cast = sem("pos_cast")
        angles = sem("angles")
        sines = sem("sines")
        c_exp = sem("c_exp")
        ada_used = sem("ada_used")
        ada_ready = sem("ada_ready")
        zeroed = sem("zeroed")
        squares = sem("squares")
        rstd_ready = sem("rstd_ready")
        scaled = sem("scaled")
        part_ready = sem("part_ready")
        evac_act = sem("evac_act")
        ready_dve = sem("ready_dve")
        merged = sem("merged")
        s_masked = sem("s_masked")
        s_exp = sem("s_exp")
        p_ready = sem("p_ready")
        sb_log, sb_raw, sb_keep = sem("sb_log"), sem("sb_raw"), sem("sb_keep")
        sb_total, sb_masked, sb_ready = sem("sb_total"), sem("sb_masked"), sem("sb_ready")
        evac_dve = sem("evac_dve")
        conv_done = sem("conv_done")
        stick_tile0, conv_tile0 = [], []
        fox_in, fox_log, fox_lf = sem("fox_in"), sem("fox_log"), sem("fox_lf")
        nsa_in, nsa_exp = sem("nsa_in"), sem("nsa_exp")
        win_ready = sem("win_ready")
        pc_in, pc_exp, pc_out = sem("pc_in"), sem("pc_exp"), sem("pc_out")
        conv_base, silu_in, silu_out = sem("conv_base"), sem("silu_in"), sem("silu_out")
        PARTS1, PARTS2 = 8, 16

        def rows_of(w, n0, n1, c0, c1):
            return w[n0 * P:n1 * P, c0:c1].rearrange("(k p) n -> p k n", p=P)

        def slot_view(u, k, n):
            return ring[:, u % SLOTS, 0:k * n].rearrange("p (k n) -> p k n", k=k)

        units = []

        def plain(w, k0, k1, c0, c1, reader="pe"):
            k, n = k1 - k0, c1 - c0
            units.append(dict(k=k, n=n, reader=reader,
                              parts=[(slice(0, P), slice(0, k), slice(0, n), rows_of(w, k0, k1, c0, c1))]))

        def ada_unit(l, u):
            plain(w_ada[l], 0, KD, 512 * u, 512 * u + 512, "dve")

        ADA_LATE = [4, 5, 6, 7, 8, 9, 10, 11]
        for l in range(LAYERS1):
            if l == 0:
                for u in range(4):
                    ada_unit(l, u)
            for u in range(15):
                c0 = u * ATT_W if u < 9 else ATT + 512 * (u - 9)
                plain(w_in[l], 0, KD, c0, min(c0 + ATT_W, ATT) if u < 9 else c0 + 512)
                if u < 8:
                    ada_unit(l, ADA_LATE[u])
            for u in range(2):
                plain(w_uq[l], 0, QR // P, UQ_W * u, UQ_W * u + UQ_W)
            plain(w_ukv[l], 0, KVR // P, 0, 2 * NH * HD)
            for w in (w_o_mla, w_o_sb, w_o_moba):
                plain(w[l], 0, 4, 0, D)
            for u in range(2):
                plain(w_out[l], 0, KD, 512 * u, 512 * u + 512)
            for u in range(8):
                plain(w_ff1[l], 0, KD, 512 * u, 512 * u + 512)
                if l + 1 < LAYERS1 and u < 4:
                    ada_unit(l + 1, u)
            for u in range(8):
                plain(w_ff2[l], 4 * u, 4 * u + 4, 0, D)
        for l in range(LAYERS2):
            for u in range(6):
                plain(w_in_2[l], 0, KD, IN2_W * u, IN2_W * u + IN2_W)
            for w in (cw1_k, cw1_v):
                plain(w[l], 0, 16, 0, CMP_H)
            for u in range(2):
                cols = slice(512 * u, 512 * u + 512)
                w = w_out_2[l]
                lo = FOX * HD
                lower = w[lo:lo + 4 * HD, cols].rearrange("(j p) n -> p j n", p=HD)
                upper = w[lo + 4 * HD:lo + 8 * HD, cols].rearrange("(j p) n -> p j n", p=HD)
                units.append(dict(k=KD, n=512, reader="pe", parts=[
                    (slice(0, P), slice(0, 2), slice(0, 512), rows_of(w, 0, 2, cols.start, cols.stop)),
                    (slice(0, HD), slice(2, 6), slice(0, 512), lower),
                    (slice(HD, P), slice(2, 6), slice(0, 512), upper),
                    (slice(0, P), slice(6, 8), slice(0, 512), rows_of(w, 6, 8, cols.start, cols.stop))]))
            for j in range(CH // 2):
                a0, b0 = 256 * j, FF2 + 256 * j
                units.append(dict(k=KD, n=512, reader="pe", parts=[
                    (slice(0, P), slice(0, KD), slice(0, 256), rows_of(w_up[l], 0, KD, a0, a0 + 256)),
                    (slice(0, P), slice(0, KD), slice(256, 512), rows_of(w_up[l], 0, KD, b0, b0 + 256))]))
            for k0 in range(0, CH, 4):
                plain(w_down[l], k0, min(k0 + 4, CH), 0, D)
        loads, read_by = [0] * SLOTS, {"pe": 0, "dve": 0}
        for u, it in enumerate(units):
            loads[u % SLOTS] += 16 * len(it["parts"])
            read_by[it["reader"]] += 1
            it.update(slot=u % SLOTS, loaded=loads[u % SLOTS], turn=read_by[it["reader"]],
                      view=slot_view(u, it["k"], it["n"]))
        used_by = {"pe": w_used, "dve": ada_used}

        def units_for(reader):
            return iter([it for it in units if it["reader"] == reader])

        def turn(src, rows, *dst, scale=1.0):
            return dict(src=src, rows=rows, dst=dst, scale=scale)

        def cols_of(src, c0, n):
            return [src[:, t, c0:c0 + n] for t in range(T)]

        def flat(n):
            return featT[:, n, :] if n < 8 else wideT[:, n - 8, :]

        def padded(n):
            return [(0, HD, qz[:, n, :]), (HD, P, qz[:, n + 1, :])]

        def whole(n, rows=P):
            return (0, rows, flat(n))

        def job(heads, scale, chunk, mask=C_CAUS, weight=False, first=True, last=True, cmp=None):
            return dict(heads=heads, scale=scale, chunk=chunk, mask=mask, weight=weight, first=first, last=last, cmp=cmp)

        def head(q, k, v, gate=None):
            return dict(q=q, k=k, v=v, gate=gate)

        SC = 1 / math.sqrt(HD)
        mla_turns = [turn(cols_of(qmla, h * QK, QK), QK, whole(h, QK)) for h in range(NH)] + \
                    [turn([k_mla[:, t, h, :] for t in range(T)], QK, whole(NH + h, QK)) for h in range(NH)]
        mla_jobs = [job([head(flat(h)[0:QK, :], flat(NH + h)[0:QK, :], v_mla[:, :, h * HD:(h + 1) * HD])
                         for h in (2 * j, 2 * j + 1)], 1 / math.sqrt(QK), j) for j in range(NH // 2)]
        sb_turns = [turn(cols_of(proj, SB0 + j * P, P), P, *padded(2 * j), scale=SC) for j in range(4)] + \
                   [turn(cols_of(proj, SB0 + NH * HD + j * P, P), P, whole(j)) for j in range(4)]
        moba_turns = [turn(cols_of(proj, MB0 + j * P, P), P, *padded(2 * j)) for j in range(4)] + \
                     [turn(cols_of(proj, MB0 + NH * HD + j * P, P), P, whole(4 + j)) for j in range(4)]
        v0 = MB0 + 2 * NH * HD
        moba_jobs = [job([head(qz[:, h, :], flat(4 + j), proj[:, :, v0 + h * HD:v0 + (h + 1) * HD])
                          for h in (2 * j, 2 * j + 1)], SC, 8 + j) for j in range(NH // 2)]
        fox_turns = [turn([faug[:, t, a, h, :] for t in range(T)], AUG, whole(FOX * a + h, AUG))
                     for a in range(2) for h in range(FOX)]
        nsa_turns = [turn([nq[:, t, j, :, :].rearrange("p g d -> p (g d)") for t in range(T)], P, *padded(2 * j))
                     for j in range(4)] + \
                    [turn(cols_of(proj2, KS, P), P, whole(8)), turn(cols_of(proj2, KW, P), P, whole(9))]
        dil_turns = [turn(cols_of(proj2, DQ + j * P, P), P, *padded(8 + 2 * j)) for j in range(2)] + \
                    [turn(cols_of(proj2, DK + j * P, P), P, whole(10 + j)) for j in range(2)]
        second_jobs = [job([head(flat(h)[0:AUG, :], flat(FOX + h)[0:AUG, :], proj2[:, :, FV + h * HD:FV + (h + 1) * HD])
                            for h in (2 * j, 2 * j + 1)], 1.0, j) for j in range(FOX // 2)]
        for j in range(NSA // 2):
            for br, (vb, kt) in enumerate(((VS, 8), (VW, 9))):
                second_jobs.append(job([head(qz[:, 2 * j + g, :], flat(kt), proj2[:, :, vb + g * HD:vb + (g + 1) * HD],
                                             gate=3 * (j + g * NSA // 2) + 1 + br) for g in range(GRP)],
                                       SC, 2 + j, first=False, last=br == 1,
                                       cmp=[j, j + NSA // 2] if br == 0 else None))
        for j in range(DIL // 2):
            second_jobs.append(job([head(qz[:, 8 + h, :], flat(10 + j), proj2[:, :, DV + h * HD:DV + (h + 1) * HD])
                                    for h in (2 * j, 2 * j + 1)], SC, 6 + j, mask=C_DMASK, weight=True))

        LAST_PART = PARTS1 * LAYERS1 + (4 if LAYERS1 else 0) + PARTS2 * LAYERS2
        block = ctx.enter_context(nc.Block())

        class Seen:

            def __init__(self, eng):
                self.eng, self.n = eng, {}

            def more(self, s, k=1):
                key = s.name
                self.n[key] = self.n.get(key, 0) + k
                self.eng.wait_ge(s, self.n[key])

        @block.sync
        def _(sp):
            sp.dma_start(cst[:, :], table).then_inc(const_loaded, 16)
            def row_load(tile, r0, vec):
                n = vec.shape[0] // P
                sp.dma_start(prow[r0:r0 + n, tile, :], vec.rearrange("(r p) -> r p", p=P)).then_inc(rows_loaded, 16)
            for l in range(DEPTH):
                row_load(l, 0, norm1_g[l])
                row_load(l, 8, norm2_g[l])
                row_load(l, 16, q_norm_g[l])
                row_load(l, 22, kv_norm_g[l])
                row_load(l, 24, b_ada[l])
            row_load(0, 72, c_in[0])
            for l in range(DEPTH):
                row_load(2 + l, 0, conv_w[l, 0])
                row_load(2 + l, 44, conv_w[l, 1])
                row_load(2 + l, 88, attn_pre[l])
                row_load(2 + l, 96, ffn_pre[l])
                row_load(4 + l, 0, conv_w[l, 2])
                row_load(4 + l, 44, conv_b[l])
                row_load(4 + l, 88, pos_k[l].rearrange("a b -> (a b)"))
                row_load(4 + l, 104, pos_v[l].rearrange("a b -> (a b)"))
            sp.dma_start(posi[0:2, :], positions[0].rearrange("(t p) -> t p", p=P)).then_inc(rows_loaded, 16)
            sp.dma_start(posi[2:4, :], positions_2[0].rearrange("(t p) -> t p", p=P)).then_inc(rows_loaded, 16)
            sp.dma_start(x[:, :, :], x_in[0].rearrange("(t p) n -> p t n", p=P)).then_inc(x_loaded, 16)
            for u, it in enumerate(units):
                if u >= SLOTS:
                    last = units[u - SLOTS]
                    sp.wait_ge(used_by[last["reader"]], last["turn"])
                for ps, ks, ns, src in it["parts"]:
                    sp.dma_start(it["view"][ps, ks, ns], src).then_inc(w_loaded[it["slot"]], 16)
            sp.wait_ge(part_ready, LAST_PART)
            sp.dma_start(out[0].rearrange("(t p) n -> p t n", p=P), x[:, :, :]).then_inc(out_stored, 16)
            sp.wait_ge(out_stored, 16)

        x1 = PARTS1 * LAYERS1 + (4 if LAYERS1 else 0)
        N_ROWS = 16 * (5 * DEPTH + 1 + 8 * DEPTH + 2)
        N_POOL_ROWS = 16 * 4 * DEPTH

        @block.gpsimd
        def _(pool):
            seen = Seen(pool)
            chain = [0]

            def link(ins):
                chain[0] += 1
                ins.then_inc(pool_chain, 1)
                pool.wait_ge(pool_chain, chain[0])

            for l in range(DEPTH):
                pool.dma_start(small[:, l, 0:FOX], b_forget[l].partition_broadcast(P)).then_inc(small_loaded, 16)
                pool.dma_start(small[:, l, FOX:], b_nsa[l].partition_broadcast(P)).then_inc(small_loaded, 16)
                for a, w in enumerate((cw2_k, cw2_v)):
                    pool.dma_start(cw2[:, l, a, :, :], w[l].rearrange("(k p) n -> p k n", p=P)).then_inc(small_loaded, 16)
            link(pool.memset(half[:, :], -0.5))

            def load_rows(a, b):
                pool.dma_start(rowbc[:, 0, :], a.partition_broadcast(P)).then_inc(bc_loaded, 16)
                pool.dma_start(rowbc[:, 1, :], b.partition_broadcast(P)).then_inc(bc_loaded, 16)

            def rstd(s0, width):
                seen.more(squares)
                link(pool.tensor_scalar(stat[:, s0:s0 + T], stat[:, s0:s0 + T], 1.0 / width, EPS, ALU.mult, ALU.add))
                pool.tensor_tensor(stat[:, s0 + T:s0 + 2 * T], stat[:, s0:s0 + T], half[:, 0:T], ALU.pow).then_inc(rstd_ready, 1)

            def rstd_parts(need):
                for t in range(T):
                    seen.more(squares, need[t])
                    link(pool.tensor_scalar(stat[:, 4 + t:5 + t], stat[:, 2 * t:2 * t + 1], 1.0 / D, EPS, ALU.mult, ALU.add))
                    link(pool.tensor_scalar(stat[:, 6 + t:7 + t], stat[:, 2 * t + 1:2 * t + 2], 1.0 / D, stat[:, 4 + t:5 + t],
                                            ALU.mult, ALU.add))
                    pool.tensor_tensor(stat[:, 8 + t:9 + t], stat[:, 6 + t:7 + t], half[:, 0:1], ALU.pow).then_inc(rstd_ready, 1)

            def diagonal(view, told):
                blocks = view.rearrange("p (b q) -> p b q", q=P)[:, 0:3:2, :]
                pool.affine_select(out=blocks, in_=blocks, pattern=[[0, 2], [1, P]], compare_op=ALU.is_gt,
                                   fill=0.0, base=0, channel_multiplier=-1).then_inc(told, 1)

            pool.memset(qz[:, :, :], 0.0).then_inc(zeroed, 1)
            IN_TURN, BY_HALVES = (2, 2), (3, 1)
            for l in range(LAYERS1):
                if l:
                    pool.wait_ge(part_ready, PARTS1 * l)
                load_rows(b_ada[l, 2 * D:3 * D], b_ada[l, 5 * D:6 * D])
                rstd_parts(IN_TURN)
                rstd(12, QR)
                rstd(16, KVR)
                for h in range(NH):
                    seen.more(sb_raw)
                    diagonal(sm[:, h % NSM, :], sb_keep)
                rstd_parts(BY_HALVES)
            if LAYERS1:
                pool.dma_start(rowbc[:, 0, :], final_norm_g.partition_broadcast(P)).then_inc(bc_loaded, 16)
                rstd_parts(IN_TURN)
            for l in range(LAYERS2):
                if x1 + l:
                    pool.wait_ge(part_ready, x1 + PARTS2 * l)
                if l == 0:
                    pool.memset(pcT, 0.0).then_inc(zeroed, 1)
                    pool.memset(vcm, 0.0).then_inc(zeroed, 1)
                load_rows(attn_post[l], ffn_post[l])
                rstd_parts(IN_TURN)
                rstd_parts(BY_HALVES)
                rstd_parts(IN_TURN)
                rstd_parts(IN_TURN)

        @block.tensor
        def _(pe):
            seen = Seen(pe)
            made = {id(for_act): 0, id(for_dve): 0, id(outputs): 0}
            owed = [0]
            mine = units_for("pe")

            def claim(ring_):
                n = made[id(ring_)]
                made[id(ring_)] = n + 1
                size = len(ring_.banks)
                if n >= size:
                    pe.wait_ge(ring_.read, n - size + 1)
                return ring_.banks[n % size], n + 1

            def mm(o, a, b, start=True, stop=True, full=None):
                ins = pe.matmul(o, a, b, start=start, stop=stop, skip_group_check=True)
                if full is not None:
                    ins.then_inc(full, 1)
                elif owed[0]:
                    ins.then_inc(w_used, owed[0])
                    owed[0] = 0
                return ins

            def flip(o, a, full=None):
                n = a.shape[0]
                ins = pe.transpose(o, a, ident[0:n, 0:n])
                if full is not None:
                    ins.then_inc(full, 1)
                elif owed[0]:
                    ins.then_inc(w_used, owed[0])
                    owed[0] = 0

            def weights():
                it = next(mine)
                pe.wait_ge(w_loaded[it["slot"]], it["loaded"])
                return it["view"], it["k"], it["n"]

            def flip_features(ready):
                for t in range(T):
                    seen.more(ready)
                    for j, r in enumerate((for_act, for_dve)):
                        b, _n = claim(r)
                        for c in range(4):
                            f = 4 * j + c
                            flip(b[:, c * P:(c + 1) * P], wide[:, t, f * P:(f + 1) * P], r.full if c == 3 else None)
                for r in (for_act, for_dve):
                    pe.wait_ge(r.read, made[id(r)])

            def linear(count, src):
                for _ in range(count):
                    w, k, n = weights()
                    for t, r in enumerate((for_act, for_dve)):
                        b, _n = claim(r)
                        for c in range(k):
                            mm(b[:, 0:n], src[:, c, t * P:(t + 1) * P], w[:, c, :], c == 0, c == k - 1,
                               r.full if c == k - 1 else None)
                    owed[0] += 1

            def linear_dve(count, src, width):
                for _ in range(count):
                    w, k, n = weights()
                    for c0 in range(0, n, width):
                        for t in range(T):
                            b, _n = claim(for_dve)
                            for c in range(k):
                                mm(b[:, 0:width], src[:, c, t * P:(t + 1) * P], w[:, c, c0:c0 + width], c == 0,
                                   c == k - 1, for_dve.full if c == k - 1 else None)
                    owed[0] += 1

            def linear_deep(chunks, src):
                owner = [for_dve, for_dve, outputs, outputs]
                open_ = [claim(r)[0] for r in owner]
                c = 0
                while c < chunks:
                    w, k, _ = weights()
                    for i, b in enumerate(open_):
                        t, hf = i // 2, i % 2
                        for kk in range(k):
                            last = c + kk == chunks - 1
                            mm(b[:, :], src[:, c + kk, t * P:(t + 1) * P], w[:, kk, hf * 512:hf * 512 + 512],
                               c + kk == 0, last, owner[i].full if last else None)
                    c += k
                    owed[0] += 1

            def turns(items):
                for j in range(0, len(items), 2):
                    r = (for_act, for_dve)[j // 2 % 2]
                    b, _n = claim(r)
                    for i, it in enumerate(items[j:j + 2]):
                        for t in range(T):
                            flip(b[0:it["rows"], (2 * i + t) * P:(2 * i + t + 1) * P], it["src"][t],
                                 r.full if t and i == len(items[j:j + 2]) - 1 else None)
                for r in (for_act, for_dve):
                    pe.wait_ge(r.read, made[id(r)])

            def softmax_heads(jobs):
                pt, out_bank = {}, None
                for i in range(len(jobs) + 3):
                    if i < len(jobs):
                        for hd in jobs[i]["heads"]:
                            b, _n = claim(for_dve)
                            mm(b[:, 0:P], hd["q"][:, 0:P], hd["k"][:, 0:P])
                            mm(b[:, P:3 * P], hd["q"][:, P:S], hd["k"], full=for_dve.full)
                    if 2 <= i < len(jobs) + 2:
                        for e in range(2):
                            n = (2 * (i - 2) + e) % NSM
                            seen.more(p_ready)
                            b, pt[i - 2, e] = claim(for_act)
                            for c in range(3):
                                flip(b[:, c * P:(c + 1) * P], sm[:, n, c * P:(c + 1) * P], for_act.full if c == 2 else None)
                    if i >= 3:
                        j = jobs[i - 3]
                        if out_bank is None:
                            out_bank = claim(outputs)[0]
                        start = j["first"]
                        if j["cmp"] is not None:
                            for e, h in enumerate(j["cmp"]):
                                mm(out_bank[HD * e:HD * e + HD, 0:S], vcm[:, e, :], pcT[:, h, :], True, False)
                        pe.wait_ge(for_act.read, pt[i - 3, 1])
                        for c in range(2):
                            for e, hd in enumerate(j["heads"]):
                                n = (2 * (i - 3) + e) % NPT
                                o = out_bank[HD * e:HD * e + HD, c * P:S]
                                mm(o, hd["v"][:, c, :], pT[:, n, S * c:S + P * c], start and c == 0, j["last"] and c == 1,
                                   outputs.full if j["last"] and c and e else None)
                        if j["last"]:
                            out_bank = None

            def stick_heads():
                zb = {}
                stick_tile0.append(made[id(for_dve)])
                ntri, nones = cst[:, C_NTRI:C_NTRI + P], cst[:, C_NONE:C_NONE + P]
                for i in range(NH // 2 + 2):
                    if i < NH // 2:
                        for h in (2 * i, 2 * i + 1):
                            q, k = qz[:, h, :], flat(i)
                            zb[h], _n = claim(for_dve)
                            mm(zb[h][:, 0:S], k[:, 0:P], q)
                            mm(zb[h][:, S:3 * P], k[:, P:S], q[:, P:S], False, True, for_dve.full)
                    if 1 <= i < NH // 2 + 1:
                        for h in (2 * i - 2, 2 * i - 1):
                            b, lk = zb[h], sm[:, h % NSM, :]
                            seen.more(sb_keep)
                            mm(b[:, 0:S], ntri, lk[:, 0:S], False, True)
                            mm(b[:, P:S], nones, lk[:, S:3 * P], False, True)
                            mm(b[:, S:3 * P], ntri, lk[:, S:3 * P], False, True, sb_total)
                    if i >= 2:
                        out_bank, _n = claim(outputs)
                        seen.more(sb_ready, 2)
                        for c in range(2):
                            for e in range(2):
                                h = 2 * (i - 2) + e
                                v0 = SB0 + 2 * NH * HD + h * HD
                                mm(out_bank[HD * e:HD * e + HD, c * P:S], proj[:, c, v0:v0 + HD],
                                   sm[:, h % NSM, S * c:S + P * c], c == 0, c == 1, outputs.full if c and e else None)

            pe.wait_ge(const_loaded, 16)
            pe.wait_ge(rows_loaded, N_ROWS)
            pe.wait_ge(small_loaded, N_POOL_ROWS)
            used_rows = [80, 72, 104, 104, 120, 120]
            for part in (range(0, 4), range(4, 6)):
                for m in part:
                    if m % 4 == 0:
                        b, _n = claim(for_act)
                    flip(b[:, (m % 4) * P:(m % 4) * P + used_rows[m]], prow[0:used_rows[m], m, :],
                         for_act.full if m == part[-1] else None)
            b, _n = claim(for_dve)
            seen.more(pos_cast)
            flip(b[:, 0:4], posf[:, :], for_dve.full)

            def modulation(u):
                b, _n = claim(for_dve)
                seen.more(ada_ready)
                acc = ada[:, u % 2, :]
                if u // 2 % 3 == 2:
                    mm(b[:, :], cst[:, C_ONE:C_ONE + P], acc, full=for_dve.full)
                    return
                for f in range(4):
                    mm(b[:, f:f + 1], acc[:, f * P:(f + 1) * P], cst[:, C_ONE:C_ONE + 1], full=for_dve.full if f == 3 else None)

            seen.more(zeroed)
            for l in range(LAYERS1):
                if l == 0:
                    for u in range(4):
                        modulation(u)
                flip_features(scaled)
                for u in range(9):
                    linear(1, featT)
                    if u >= 1:
                        modulation(ADA_LATE[u - 1])
                for _ in range(6):
                    w, k, n = weights()
                    for t in range(T):
                        b, _n = claim(for_act)
                        for c in range(k):
                            mm(b[:, :], featT[:, c, t * P:(t + 1) * P], w[:, c, :], c == 0, c == k - 1,
                               for_act.full if c == k - 1 else None)
                    owed[0] += 1
                flip_features(scaled)
                linear(2, featT)
                linear_dve(1, featT[:, 6:8, :], 512)
                seen.more(ready_dve)
                turns(mla_turns)
                softmax_heads(mla_jobs)
                turns(sb_turns)
                stick_heads()
                turns(moba_turns)
                softmax_heads(moba_jobs)
                pe.wait_ge(outputs.read, made[id(outputs)])
                w_o = [weights()[0] for _ in range(3)]
                for t in range(T):
                    for hf in range(2):
                        for br in range(3):
                            b, _n = claim(for_dve)
                            for c in range(4):
                                mm(b[:, :], oT[:, 4 * br + c, t * P:(t + 1) * P], w_o[br][:, c, hf * 512:hf * 512 + 512],
                                   c == 0, c == 3, for_dve.full if c == 3 else None)
                owed[0] += 3
                flip_features(merged)
                linear_dve(2, featT, 512)
                flip_features(scaled)
                for u in range(8):
                    w, k, n = weights()
                    for j in range(2):
                        b, _n = claim(for_act)
                        for f in range(2):
                            for c in range(k):
                                mm(b[:, f * S:(f + 1) * S], w[:, c, (2 * j + f) * P:(2 * j + f + 1) * P], featT[:, c, :],
                                   c == 0, c == k - 1, for_act.full if f and c == k - 1 else None)
                    owed[0] += 1
                    if l + 1 < LAYERS1 and 1 <= u < 5:
                        modulation(u - 1)
                pe.wait_ge(for_act.read, made[id(for_act)])
                linear_deep(32, hidT)

            for l in range(LAYERS2):
                flip_features(scaled)
                linear(6, featT)
                seen.more(fox_lf)
                b, _n = claim(for_dve)
                lf = fox[:, 2, :].rearrange("p (t h) -> p t h", t=T)
                tri, ones = cst[:, C_TRI:C_TRI + P], cst[:, C_ONE:C_ONE + P]
                mm(b[:, 0:FOX], tri, lf[:, 0, :])
                mm(b[:, FOX:2 * FOX], tri, lf[:, 1, :], True, False)
                mm(b[:, FOX:2 * FOX], ones, lf[:, 0, :], False, True, for_dve.full)
                seen.more(ready_dve)
                b, _n = claim(for_dve)
                for a, c0 in enumerate((KC, VC)):
                    for t in range(T):
                        flip(b[:, (2 * a + t) * P:(2 * a + t + 1) * P], proj2[:, t, c0:c0 + P],
                             for_dve.full if a and t else None)
                turns(nsa_turns + dil_turns)
                seen.more(win_ready)
                b, n = claim(for_act)
                ws = [weights()[0] for _ in range(2)]
                for c in range(16):
                    for a in range(2):
                        mm(b[HD * a:HD * a + GRP * NCMP, 0:CMP_H], awin[:, a, c, :], ws[a][:, c, :], c == 0, c == 15,
                           for_act.full if a and c == 15 else None)
                owed[0] += 2
                seen.more(ready_dve)
                turns(fox_turns)
                pe.wait_ge(for_act.read, n)
                b, n = claim(for_act)
                for m in range(4):
                    flip(b[:, m * 32:m * 32 + GRP * NCMP], gel[:, m * P:(m + 1) * P], for_act.full if m == 3 else None)
                pe.wait_ge(for_act.read, n)
                b, n = claim(for_act)
                for g in range(GRP):
                    for c in range(2):
                        mm(b[HD * g:HD * g + HD, 0:NCMP], cw2[:, l, 0, c, :], hT[:, c, g * NCMP:(g + 1) * NCMP], c == 0, c == 1)
                for g in range(GRP):
                    for c in range(2):
                        mm(b[0:NCMP, HD * (g + 1):HD * (g + 2)], hT[:, 2 + c, g * NCMP:(g + 1) * NCMP], cw2[:, l, 1, c, :],
                           c == 0, c == 1, for_act.full if g and c else None)
                pe.wait_ge(for_act.read, n)
                for g in range(GRP):
                    b, _n = claim(for_dve)
                    for h in range(NSA // 2):
                        for t in range(T):
                            at = (t * NSA // 2 + h) * NCMP
                            mm(b[:, at:at + NCMP], qz[:, 2 * h + g, t * P:(t + 1) * P], kcT,
                               full=for_dve.full if h == NSA // 2 - 1 and t else None)
                seen.more(pc_out)
                for h2 in range(NSA // 2):
                    b, n = claim(for_act)
                    for i in range(2):
                        for t in range(T):
                            flip(b[0:NCMP, (2 * i + t) * P:(2 * i + t + 1) * P], pc[:, t, 2 * h2 + i, :],
                                 for_act.full if i and t else None)
                pe.wait_ge(for_act.read, n)
                if l == 0:
                    seen.more(zeroed, 2)
                softmax_heads(second_jobs)
                pe.wait_ge(outputs.read, made[id(outputs)])
                linear_dve(2, oT, 512)
                flip_features(scaled)
                conv_tile0.append(made[id(for_dve)])
                for j in range(CH // 2):
                    w, k, n = weights()
                    for hf in range(2):
                        b, _n = claim(for_dve)
                        for f in range(2):
                            for c in range(k):
                                mm(b[:, f * S:(f + 1) * S], w[:, c, (2 * hf + f) * P:(2 * hf + f + 1) * P], featT[:, c, :],
                                   c == 0, c == k - 1, for_dve.full if f and c == k - 1 else None)
                    owed[0] += 1
                seen.more(conv_done, CH // 2)
                linear_deep(CH, hidT)

        @block.scalar
        def _(act):
            seen = Seen(act)
            chain, got, sums_done = [0], [0], [0]

            def link(ins):
                chain[0] += 1
                ins.then_inc(act_chain, 1)
                act.wait_ge(act_chain, chain[0])

            def tile():
                n = got[0]
                got[0] += 1
                act.wait_ge(for_act.full, n + 1)
                return for_act.banks[n % 2]

            def read(ins):
                ins.then_inc(for_act.read, 1)

            def copy_out(dst, src):
                read(act.activation(dst, src, ACT.Copy))

            scratch = [v[:, :, :].rearrange("p b n -> p (b n)") for v in (pT, sm)]

            def sums(src, s0, width):
                for t in range(T):
                    ins = act.activation(scratch[t][:, 0:width], src[:, t, :], ACT.Square, accum_out=stat[:, s0 + t:s0 + t + 1])
                    if t == T - 1:
                        ins.then_inc(squares, 1)
                sums_done[0] += 1

            IN_TURN = [(0, 0), (0, 1), (1, 0), (1, 1)]
            BY_HALVES = [(0, 0), (1, 0), (0, 1), (1, 1)]

            def sums_of_parts(src, order, wait=True):
                for t, hf in order:
                    if wait:
                        seen.more(part_ready)
                    act.activation(scratch[t][:, hf * 512:hf * 512 + 512], src[:, t, hf * 512:hf * 512 + 512], ACT.Square,
                                   accum_out=stat[:, 2 * t + hf:2 * t + hf + 1]).then_inc(squares, 1)
                    sums_done[0] += 1

            def features_out(gain=None, shift=None):
                for t in range(T):
                    b = tile()
                    if gain is None:
                        copy_out(featT[:, 0:4, t * P:(t + 1) * P], b[:, :].rearrange("p (c s) -> p c s", c=4))
                        continue
                    for f in range(4):
                        kw = dict(scale=gain[:, f:f + 1])
                        if shift is not None:
                            kw["bias"] = shift[:, f:f + 1]
                        ins = act.activation(featT[:, f, t * P:(t + 1) * P], b[:, f * P:(f + 1) * P],
                                             ACT.Identity if shift is not None else ACT.Copy, **kw)
                    read(ins)

            def turns_out(items):
                for j in range(0, len(items), 4):
                    b = tile()
                    for i, it in enumerate(items[j:j + 2]):
                        for r0, r1, dst in it["dst"]:
                            ins = act.activation(dst[r0:r1, :], b[r0:r1, i * S:(i + 1) * S], ACT.Copy, scale=it["scale"])
                    read(ins)

            def softmax_heads(jobs):
                for i in range(len(jobs) + 2):
                    if i < len(jobs):
                        for e in range(2):
                            n = (2 * i + e) % NSM
                            seen.more(s_masked)
                            for t, cols in enumerate((slice(0, P), slice(P, 3 * P))):
                                ins = act.activation(sm[:, n, cols], sm[:, n, cols], ACT.Exp, scale=jobs[i]["scale"],
                                                     bias=mx[:, n, t:t + 1], accum_out=rs[:, n, t:t + 1])
                            ins.then_inc(s_exp, 1)
                    if i >= 2:
                        for e in range(2):
                            b = tile()
                            copy_out(pT[:, (2 * (i - 2) + e) % NPT, :], b[:, 0:3 * P])

            def stick_heads(l):
                for i in range(NH // 2 + 1):
                    if i < NH // 2:
                        for h in (2 * i, 2 * i + 1):
                            m = stick_tile0[l] + h
                            act.wait_ge(for_dve.full, m + 1)
                            ab = pT[:, h % NPT, :]
                            link(act.activation(ab, for_dve.banks[m % 4][:, 0:3 * P], ACT.Abs))
                            link(act.activation(ab, ab, ACT.Exp, scale=-1.0))
                            act.activation(ab, ab, ACT.Ln, bias=1.0).then_inc(sb_log, 1)
                    if i >= 1:
                        for h in (2 * i - 2, 2 * i - 1):
                            a = sm[:, h % NSM, :]
                            seen.more(sb_masked)
                            act.activation(a, a, ACT.Exp).then_inc(sb_ready, 1)

            b = tile()
            for m, rows in enumerate((80, 72, 104, 104)):
                ins = act.activation(pcol[:, m, 0:rows], b[:, m * P:m * P + rows], ACT.Copy)
            link(ins)
            act.sem_inc(for_act.read, 1)
            act.sem_inc(c_exp, 1)
            b = tile()
            for m in (4, 5):
                ins = act.activation(pcol[:, m, 0:120], b[:, (m - 4) * P:(m - 4) * P + 120], ACT.Copy)
            link(ins)
            act.sem_inc(for_act.read, 1)
            act.sem_inc(c_exp, 1)
            seen.more(angles)
            act.activation(cs[:, :, :, :].rearrange("p a t f -> p (a t f)"), trig[:, 0:2, :].rearrange("p a f -> p (a f)"),
                           ACT.Sin).then_inc(sines, 1)
            act.preload_act_table_set("natural_log_exp_and_others")
            act.activation(c_tmp, pcol[:, 0, 72:80], ACT.Exp, scale=-1.0).then_inc(c_exp, 1)

            act.wait_ge(x_loaded, 16)
            if LAYERS1:
                sums_of_parts(x, IN_TURN, False)
            for l in range(LAYERS1):
                if l:
                    sums_of_parts(x, IN_TURN)
                seen.more(evac_dve)
                features_out(mod[:, 8:16], mod[:, 0:8])
                for u in range(9):
                    b = tile()
                    c0 = u * ATT_W
                    n = min(ATT_W, ATT - c0)
                    copy_out(proj[:, 0, c0:c0 + n], b[:, 0:n])
                act.wait_ge(for_act.read, got[0])
                act.sem_inc(evac_act, 1)
                seen.more(evac_dve)
                sums(proj[:, :, 0:QR], 12, QR)
                act.wait_ge(squares, sums_done[0])
                sums(proj[:, :, QR:QR + KVR], 16, KVR)
                for u in range(6):
                    for t in range(T):
                        b = tile()
                        read(act.activation(gates[:, t, u * 512:u * 512 + 512], b[:, :], ACT.Sigmoid))
                act.preload_act_table_set("natural_log_exp_and_others")
                features_out(pcol[:, l, 16:24])
                for u in range(2):
                    b = tile()
                    copy_out(qmla[:, 0, u * UQ_W:(u + 1) * UQ_W], b[:, 0:UQ_W])
                act.wait_ge(for_act.read, got[0])
                act.sem_inc(evac_act, 1)
                turns_out(mla_turns)
                softmax_heads(mla_jobs)
                turns_out(sb_turns)
                stick_heads(l)
                turns_out(moba_turns)
                softmax_heads(moba_jobs)
                features_out()
                sums_of_parts(x, BY_HALVES)
                seen.more(evac_dve)
                features_out(mod[:, 24:32], mod[:, 16:24])
                for u in range(16):
                    b = tile()
                    dst = hidT[:, 2 * u:2 * u + 2, :].rearrange("p c s -> p (c s)")
                    link(act.activation(dst, b[:, :], ACT.Relu))
                    read(act.activation(dst, dst, ACT.Square))
            if LAYERS1:
                sums_of_parts(x, IN_TURN)
            for l in range(LAYERS2):
                sums_of_parts(x, IN_TURN, bool(l or LAYERS1))
                features_out(pcol[:, 2 + l, 88:96])
                for u in range(6):
                    b = tile()
                    copy_out(proj2[:, 0, u * IN2_W:(u + 1) * IN2_W], b[:, 0:IN2_W])
                act.wait_ge(for_act.read, got[0])
                act.sem_inc(evac_act, 1)
                seen.more(fox_in)
                link(act.activation(fox[:, 1, :], fox[:, 0, :], ACT.Abs))
                link(act.activation(fox[:, 1, :], fox[:, 1, :], ACT.Exp, scale=-1.0))
                act.activation(fox[:, 1, :], fox[:, 1, :], ACT.Ln, bias=1.0).then_inc(fox_log, 1)
                seen.more(nsa_in)
                act.activation(gn[:, 1, :], gn[:, 0, :], ACT.Exp, scale=-1.0).then_inc(nsa_exp, 1)
                turns_out(nsa_turns + dil_turns)
                b = tile()
                for a in range(2):
                    ins = act.activation(gel[:, a * CMP_H:(a + 1) * CMP_H], b[HD * a:HD * a + GRP * NCMP, 0:CMP_H],
                                         ACT.Gelu_apprx_tanh)
                read(ins)
                act.preload_act_table_set("natural_log_exp_and_others")
                turns_out(fox_turns)
                b = tile()
                copy_out(hT[:, :, :], b[:, 0:P].rearrange("p (a n) -> p a n", n=32)[:, :, 0:GRP * NCMP])
                b = tile()
                act.activation(kcT[:, :], b[:, 0:NCMP], ACT.Copy)
                copy_out(vcm[0:NCMP, :, :], b[0:NCMP, HD:3 * HD].rearrange("p (g d) -> p g d", g=GRP))
                seen.more(pc_in)
                act.activation(pc2[:, :, :, :], pc[:, :, :, :], ACT.Exp).then_inc(pc_exp, 1)
                for h2 in range(NSA // 2):
                    b = tile()
                    copy_out(pcT[0:NCMP, 2 * h2:2 * h2 + 2, :], b[0:NCMP, :].rearrange("p (h s) -> p h s", s=S))
                softmax_heads(second_jobs)
                sums_of_parts(wide, BY_HALVES)
                sums_of_parts(x, IN_TURN)
                features_out(pcol[:, 2 + l, 96:104])
                w2c, bc = pcol[:, 4 + l, 0:44], pcol[:, 4 + l, 44:88]
                for j in range(CH // 2 + 1):
                    if j < CH // 2:
                        if j >= 2:
                            seen.more(conv_done)
                        for hf in range(2):
                            m = conv_tile0[l] + 2 * j + hf
                            act.wait_ge(for_dve.full, m + 1)
                            b = for_dve.banks[m % 4]
                            for f in range(2):
                                ch = hf * CH + 2 * j + f
                                ins = act.activation(cv[:, j % 2, hf, f * S:(f + 1) * S], b[:, f * S:(f + 1) * S],
                                                     ACT.Identity, scale=w2c[:, ch:ch + 1], bias=bc[:, ch:ch + 1])
                            ins.then_inc(conv_base, 1)
                    if j >= 1:
                        seen.more(silu_in)
                        a = cv[:, (j - 1) % 2, 0, :]
                        act.activation(a, a, ACT.Silu).then_inc(silu_out, 1)
                seen.more(conv_done, 2)
                sums_of_parts(wide, IN_TURN)

        @block.vector
        def _(dve):
            seen = Seen(dve)
            chain = [0]
            got = {}

            def link(ins):
                chain[0] += 1
                ins.then_inc(dve_chain, 1)
                dve.wait_ge(dve_chain, chain[0])

            def tile(r):
                n = got.get(id(r), 0)
                got[id(r)] = n + 1
                dve.wait_ge(r.full, n + 1)
                return r.banks[n % len(r.banks)]

            def read(r, ins):
                ins.then_inc(r.read, 1)

            def stored(r):
                dve.wait_ge(r.read, got[id(r)])

            def scale_tokens(src=x):
                for t in range(T):
                    seen.more(rstd_ready)
                    dve.tensor_scalar(wide[:, t, :], src[:, t, :], stat[:, 8 + t:9 + t], None, ALU.mult).then_inc(scaled, 1)

            def features_out(gain=None, shift=None):
                for t in range(T):
                    b = tile(for_dve)
                    if gain is None:
                        read(for_dve, dve.tensor_copy(featT[:, 4:8, t * P:(t + 1) * P], b[:, :].rearrange("p (c s) -> p c s", c=4)))
                        continue
                    for f in range(4, 8):
                        src, dst = b[:, (f - 4) * P:(f - 3) * P], featT[:, f, t * P:(t + 1) * P]
                        if shift is None:
                            ins = dve.tensor_scalar(dst, src, gain[:, f:f + 1], None, ALU.mult)
                        else:
                            ins = dve.tensor_scalar(dst, src, gain[:, f:f + 1], shift[:, f:f + 1], ALU.mult, ALU.add)
                    read(for_dve, ins)

            def turns_out(items):
                for j in range(2, len(items), 4):
                    b = tile(for_dve)
                    for i, it in enumerate(items[j:j + 2]):
                        for r0, r1, dst in it["dst"]:
                            ins = dve.tensor_scalar(dst[r0:r1, :], b[r0:r1, i * S:(i + 1) * S], it["scale"], None, ALU.mult)
                    read(for_dve, ins)

            ada_units = units_for("dve")

            def ada_rows(u):
                it, acc = next(ada_units), ada[:, u % 2, :]
                dve.wait_ge(w_loaded[it["slot"]], it["loaded"])
                link(dve.tensor_scalar(acc, it["view"][:, 0, :], c_act[:, 0:1], None, ALU.mult))
                for c in range(1, KD):
                    link(dve.scalar_tensor_tensor(out=acc, in0=it["view"][:, c, :], scalar=c_act[:, c:c + 1], in1=acc,
                                                  op0=ALU.mult, op1=ALU.add))
                dve.sem_inc(ada_used, 1)
                dve.sem_inc(ada_ready, 1)

            def modulation_out(l, u):
                b = tile(for_dve)
                v, hf = u // 2, u % 2
                if v % 3 == 2:
                    dst = rowbc[:, v // 3, hf * 512:hf * 512 + 512]
                    read(for_dve, dve.tensor_tensor(dst, b[:, :], dst, ALU.add))
                    return
                at = 16 * (v // 3) + 8 * (v % 3) + 4 * hf
                link(dve.tensor_tensor(mod[:, at:at + 4], b[:, 0:4], pcol[:, l, 24 + 4 * u:28 + 4 * u], ALU.add))
                dve.sem_inc(for_dve.read, 1)
                if v % 3 == 1:
                    g = pcol[:, l, 8 * (v // 3) + 4 * hf:8 * (v // 3) + 4 * hf + 4]
                    link(dve.scalar_tensor_tensor(out=mod[:, at:at + 4], in0=mod[:, at:at + 4], scalar=1.0, in1=g,
                                                  op0=ALU.add, op1=ALU.mult))
                    if hf:
                        dve.sem_inc(evac_dve, 1)

            def rope(x1, x2, table0, width, dims):
                t0, t1, heads = dims
                shape = list(x1.shape)

                def trig_of(a):
                    v = cs[:, a, t0:t1, table0:table0 + width]
                    return v.unsqueeze(2).to_broadcast([P, t1 - t0, heads, width]) if len(shape) == 4 else \
                        v.rearrange("p t f -> p (t f)").unsqueeze(1).to_broadcast([P, heads, width])

                cos, sin = trig_of(0), trig_of(1)

                def scratch(a):
                    v = rope_t[:, a, 0:(t1 - t0) * heads * width]
                    return v.rearrange("p (t h f) -> p t h f", t=t1 - t0, h=heads) if len(shape) == 4 else \
                        v.rearrange("p (h f) -> p h f", h=heads)

                dve.tensor_tensor(scratch(0), x1, cos, ALU.mult)
                dve.tensor_tensor(scratch(1), x2, sin, ALU.mult)
                dve.tensor_tensor(scratch(2), x1, sin, ALU.mult)
                link(dve.tensor_tensor(scratch(3), x2, cos, ALU.mult))
                dve.tensor_tensor(x1, scratch(0), scratch(1), ALU.subtract)
                link(dve.tensor_tensor(x2, scratch(2), scratch(3), ALU.add))

            def softmax_heads(jobs):
                both = ((0, 0, P), (1, P, 3 * P))
                for i in range(len(jobs) + 4):
                    if i < len(jobs):
                        j = jobs[i]
                        for e in range(2):
                            n = (2 * i + e) % NSM
                            b = tile(for_dve)
                            for t, a, z in both:
                                ins = dve.tensor_tensor_reduce(out=sm[:, n, a:z], in0=b[:, a:z],
                                                               in1=cst[:, j["mask"] + a:j["mask"] + z],
                                                               scale=1.0, scalar=-3e38, op0=ALU.add, op1=ALU.max,
                                                               accum_out=mx[:, n, t:t + 1])
                            link(ins)
                            dve.sem_inc(for_dve.read, 1)
                            dve.tensor_scalar(mx[:, n, :], mx[:, n, :], -j["scale"], None, ALU.mult).then_inc(s_masked, 1)
                    if 1 <= i < len(jobs) + 1:
                        j = jobs[i - 1]
                        for e in range(2):
                            n = (2 * (i - 1) + e) % NSM
                            seen.more(s_exp)
                            if j["weight"]:
                                for t, a, z in both:
                                    ins = dve.tensor_tensor_reduce(out=sm[:, n, a:z], in0=sm[:, n, a:z],
                                                                   in1=cst[:, C_DW + a:C_DW + z],
                                                                   scale=1.0, scalar=0.0, op0=ALU.mult, op1=ALU.add,
                                                                   accum_out=rs[:, n, t:t + 1])
                                link(ins)
                            link(dve.reciprocal(rs[:, n, :], rs[:, n, :]))
                            gate = j["heads"][e]["gate"]
                            if gate is not None:
                                g = gn[:, 1, :].rearrange("p (t n) -> p t n", t=T)[:, :, gate]
                                link(dve.tensor_tensor(rs[:, n, :], rs[:, n, :], g, ALU.mult))
                            for t, a, z in both:
                                ins = dve.tensor_scalar(sm[:, n, a:z], sm[:, n, a:z], rs[:, n, t:t + 1], None, ALU.mult)
                            ins.then_inc(p_ready, 1)
                    if i >= 4 and jobs[i - 4]["last"]:
                        b = tile(outputs)
                        read(outputs, dve.tensor_copy(oT[:, jobs[i - 4]["chunk"], :], b[:, 0:S]))

            def stick_heads():
                z = {}
                for i in range(NH // 2 + 3):
                    if i < NH // 2:
                        for h in (2 * i, 2 * i + 1):
                            z[h] = tile(for_dve)
                            seen.more(sb_log)
                            dve.scalar_tensor_tensor(out=sm[:, h % NSM, :], in0=z[h][:, 0:3 * P], scalar=0.0,
                                                     in1=pT[:, h % NPT, :], op0=ALU.max, op1=ALU.add).then_inc(sb_raw, 1)
                    if 1 <= i < NH // 2 + 1:
                        for h in (2 * i - 2, 2 * i - 1):
                            seen.more(sb_total)
                            link(dve.tensor_tensor(sm[:, h % NSM, :], z[h][:, 0:3 * P], cst[:, C_SMASK:C_SMASK + 3 * P], ALU.add))
                            dve.sem_inc(for_dve.read, 1)
                            dve.sem_inc(sb_masked, 1)
                    if i >= 3:
                        b = tile(outputs)
                        read(outputs, dve.tensor_copy(oT[:, 4 + i - 3, :], b[:, 0:S]))

            dve.wait_ge(const_loaded, 16)
            dve.wait_ge(rows_loaded, N_ROWS)
            dve.wait_ge(small_loaded, N_POOL_ROWS)
            dve.tensor_copy(posf[:, :], posi[:, :]).then_inc(pos_cast, 1)
            b = tile(for_dve)
            link(dve.tensor_copy(posc[:, :], b[:, 0:4]))
            dve.sem_inc(for_dve.read, 1)
            for t in range(T):
                dve.tensor_scalar(trig[:, 2, 32 * t:32 * t + 24], cst[:, C_INV:C_INV + 24], posc[:, t:t + 1], None, ALU.mult)
                link(dve.tensor_scalar(trig[:, 2, 32 * t + 24:32 * t + 32], cst[:, C_INV + 24:C_INV + 32],
                                       posc[:, 2 + t:3 + t], None, ALU.mult))
            turnsn = tiny[:, 0:64]
            for a, ahead in ((1, 0.0), (0, 0.25)):
                link(dve.tensor_scalar(turnsn, trig[:, 2, :], 1 / TWO_PI, ahead, ALU.mult, ALU.add))
                link(dve.tensor_scalar(turnsn, turnsn, ROUNDER, None, ALU.add))
                link(dve.tensor_scalar(turnsn, turnsn, -ROUNDER, None, ALU.add))
                link(dve.scalar_tensor_tensor(out=trig[:, a, :], in0=turnsn, scalar=-PI_A, in1=trig[:, 2, :], op0=ALU.mult, op1=ALU.add))
                for part in (PI_B, PI_C):
                    link(dve.scalar_tensor_tensor(out=trig[:, a, :], in0=turnsn, scalar=-part, in1=trig[:, a, :], op0=ALU.mult, op1=ALU.add))
                if ahead:
                    link(dve.tensor_scalar(trig[:, a, :], trig[:, a, :], TWO_PI * ahead, None, ALU.add))
                link(dve.tensor_scalar(trig[:, a, :], trig[:, a, :], PI_SAFE, -PI_SAFE, ALU.min, ALU.max))
            dve.sem_inc(angles, 1)
            seen.more(c_exp, 3)
            link(dve.tensor_scalar(c_tmp, c_tmp, 1.0, None, ALU.add))
            link(dve.reciprocal(c_tmp, c_tmp))
            link(dve.tensor_tensor(c_act, c_tmp, pcol[:, 0, 72:80], ALU.mult))
            seen.more(sines)
            dve.wait_ge(x_loaded, 16)

            for l in range(LAYERS1):
                if l == 0:
                    for u in range(4):
                        ada_rows(u)
                        if u:
                            modulation_out(l, u - 1)
                    modulation_out(l, 3)
                scale_tokens()
                features_out(mod[:, 8:16], mod[:, 0:8])
                seen.more(bc_loaded, 32)
                for u in range(9):
                    b = tile(for_dve)
                    c0 = u * ATT_W
                    n = min(ATT_W, ATT - c0)
                    read(for_dve, dve.tensor_copy(proj[:, 1, c0:c0 + n], b[:, 0:n]))
                    if u == 8:
                        stored(for_dve)
                        dve.sem_inc(evac_dve, 1)
                    if u >= 1:
                        modulation_out(l, ADA_LATE[u - 1])
                    if u < 8:
                        ada_rows(ADA_LATE[u])
                seen.more(evac_act)
                seen.more(rstd_ready, 2)
                for t in range(T):
                    dve.tensor_scalar(wide[:, t, 0:QR], proj[:, t, 0:QR], stat[:, 14 + t:15 + t], None, ALU.mult)
                    dve.tensor_scalar(wide[:, t, QR:D], proj[:, t, QR:QR + KVR], stat[:, 18 + t:19 + t], None, ALU.mult)\
                       .then_inc(scaled, 1)
                kpe = proj[:, :, QR + KVR:SB0].rearrange("p t (h e) -> p t h e", h=1)
                rope(kpe[:, :, :, 0:16], kpe[:, :, :, 16:32], 0, 16, (0, T, 1))
                qk = proj[:, :, MB0:MB0 + 2 * NH * HD].rearrange("p t (h e) -> p t h e", e=HD)
                rope(qk[:, :, :, 0:8], qk[:, :, :, 8:16], 16, 8, (0, T, 2 * NH))
                for t in range(T):
                    dve.tensor_copy(k_mla[:, t, :, NOPE:QK],
                                    proj[:, t, QR + KVR:SB0].unsqueeze(1).to_broadcast([P, NH, ROPE]))
                features_out(pcol[:, l, 16:24])
                for u in range(2):
                    b = tile(for_dve)
                    read(for_dve, dve.tensor_copy(qmla[:, 1, u * UQ_W:(u + 1) * UQ_W], b[:, 0:UQ_W]))
                for hf in range(2):
                    for t in range(T):
                        b = tile(for_dve)
                        kv = b[:, :].rearrange("p (h e) -> p h e", e=NOPE + HD)
                        dve.tensor_copy(k_mla[:, t, 4 * hf:4 * hf + 4, 0:NOPE], kv[:, :, 0:NOPE])
                        read(for_dve, dve.tensor_copy(
                            v_mla[:, t, 4 * hf * HD:4 * (hf + 1) * HD].rearrange("p (h e) -> p h e", e=HD), kv[:, :, NOPE:]))
                stored(for_dve)
                seen.more(evac_act)
                qh = qmla.rearrange("p t (h e) -> p t h e", e=QK)
                rope(qh[:, :, :, NOPE:NOPE + 16], qh[:, :, :, NOPE + 16:QK], 0, 16, (0, T, NH))
                dve.sem_inc(ready_dve, 1)
                turns_out(mla_turns)
                softmax_heads(mla_jobs)
                turns_out(sb_turns)
                stick_heads()
                turns_out(moba_turns)
                softmax_heads(moba_jobs)
                dve.wait_ge(outputs.read, got[id(outputs)])
                tmp = sm[:, :, :].rearrange("p b n -> p (b n)")[:, D:2 * D]
                k = 0
                for t in range(T):
                    for hf in range(2):
                        for br in range(3):
                            b = tile(for_dve)
                            g = gates[:, t, br * D + hf * 512:br * D + hf * 512 + 512]
                            dst = wide[:, t, hf * 512:hf * 512 + 512]
                            if br == 0:
                                read(for_dve, dve.tensor_tensor(dst, b[:, :], g, ALU.mult))
                                continue
                            tm = tmp[:, 512 * (k % 2):512 * (k % 2) + 512]
                            k += 1
                            read(for_dve, dve.tensor_tensor(tm, b[:, :], g, ALU.mult))
                            stored(for_dve)
                            link(dve.tensor_tensor(dst, dst, tm, ALU.add))
                    dve.sem_inc(merged, 1)
                features_out()

                def add_gated(g, order):
                    for k, (r, t, hf) in enumerate(order):
                        b = tile(r)
                        cols = slice(hf * 512, hf * 512 + 512)
                        tm = tmp[:, 512 * (k % 2):512 * (k % 2) + 512]
                        read(r, dve.tensor_tensor(tm, b[:, :], rowbc[:, g, cols], ALU.mult))
                        stored(r)
                        dve.tensor_tensor(x[:, t, cols], x[:, t, cols], tm, ALU.add).then_inc(part_ready, 1)
                    dve.wait_ge(part_ready, PARTS1 * l + 4 * g + 4)

                add_gated(0, [(for_dve, t, hf) for hf in range(2) for t in range(T)])
                scale_tokens()
                features_out(mod[:, 24:32], mod[:, 16:24])
                if l + 1 < LAYERS1:
                    for u in range(4):
                        ada_rows(u)
                        if u:
                            modulation_out(l + 1, u - 1)
                    modulation_out(l + 1, 3)
                add_gated(1, [(for_dve, 0, 0), (for_dve, 0, 1), (outputs, 1, 0), (outputs, 1, 1)])
            if LAYERS1:
                seen.more(bc_loaded, 16)
                for t in range(T):
                    seen.more(rstd_ready)
                    for hf in range(2):
                        cols = slice(hf * 512, hf * 512 + 512)
                        dve.scalar_tensor_tensor(out=x[:, t, cols], in0=x[:, t, cols], scalar=stat[:, 8 + t:9 + t],
                                                 in1=rowbc[:, 0, cols], op0=ALU.mult, op1=ALU.mult).then_inc(part_ready, 1)
                dve.wait_ge(part_ready, x1)

            parts = [x1]
            for l in range(LAYERS2):
                scale_tokens()
                features_out(pcol[:, 2 + l, 88:96])
                for u in range(6):
                    b = tile(for_dve)
                    read(for_dve, dve.tensor_copy(proj2[:, 1, u * IN2_W:(u + 1) * IN2_W], b[:, 0:IN2_W]))
                stored(for_dve)
                seen.more(evac_act)
                fv = lambda a: fox[:, a, :].rearrange("p (t h) -> p t h", t=T)
                dve.tensor_tensor(fv(0), proj2[:, :, FG:FG + FOX],
                                  small[:, l, 0:FOX].unsqueeze(1).to_broadcast([P, T, FOX]), ALU.add).then_inc(fox_in, 1)
                dve.tensor_tensor(gn[:, 0, :].rearrange("p (t n) -> p t n", t=T), proj2[:, :, NG:NG + 3 * NSA],
                                  small[:, l, FOX:].unsqueeze(1).to_broadcast([P, T, 3 * NSA]), ALU.add).then_inc(nsa_in, 1)
                for base, heads in ((NQ, NSA), (DQ, 2 * DIL)):
                    v = proj2[:, :, base:base + heads * HD].rearrange("p t (h e) -> p t h e", e=HD)
                    rope(v[:, :, :, 0:8], v[:, :, :, 8:16], 24, 8, (0, T, heads))
                for t in range(T):
                    for base in (KC, KS, KW):
                        v = proj2[:, t, base:base + GRP * HD].rearrange("p (h e) -> p h e", e=HD)
                        rope(v[:, :, 0:8], v[:, :, 8:16], 24, 8, (t, t + 1, GRP))
                for t in range(T):
                    for g in range(GRP):
                        q0 = NQ + 4 * g * HD
                        ins = dve.tensor_copy(nq[:, t, :, g, :], proj2[:, t, q0:q0 + 4 * HD].rearrange("p (j d) -> p j d", d=HD))
                link(ins)
                dve.sem_inc(ready_dve, 1)
                seen.more(fox_log)
                dve.scalar_tensor_tensor(out=fox[:, 2, :], in0=fox[:, 0, :], scalar=0.0, in1=fox[:, 1, :],
                                         op0=ALU.min, op1=ALU.subtract).then_inc(fox_lf, 1)
                for t in range(T):
                    heads = lambda c0: proj2[:, t, c0:c0 + FOX * HD].rearrange("p (h e) -> p h e", e=HD)
                    dve.tensor_scalar(faug[:, t, 0, :, 0:HD], heads(FQ), 1 / math.sqrt(HD), None, ALU.mult)
                    dve.tensor_copy(faug[:, t, 1, :, 0:HD], heads(FK))
                    dve.memset(faug[:, t, 0, :, HD + 1], 1.0)
                    dve.memset(faug[:, t, 1, :, HD], 1.0)
                b = tile(for_dve)
                sums_ = b[:, 0:T * FOX].rearrange("p (t h) -> p t h", t=T)
                dve.tensor_copy(faug[:, :, 0, :, HD], sums_)
                link(dve.tensor_scalar(faug[:, :, 1, :, HD + 1], sums_, -1.0, None, ALU.mult))
                dve.sem_inc(for_dve.read, 1)
                dve.sem_inc(ready_dve, 1)
                b = tile(for_dve)
                src = b[:, :].rearrange("p (a s) -> p a s", a=2)
                for g in range(GRP):
                    rows = slice(HD * g, HD * g + HD)
                    dve.tensor_copy(U[0:HD, :, g, :], src[rows, :, :])
                    ins = dve.tensor_copy(U[HD:P, :, g, 0:S - 1], src[rows, :, 1:S])
                link(ins)
                dve.sem_inc(for_dve.read, 1)
                for a in range(2):
                    for g in range(GRP):
                        for ch in range(2):
                            win = U[:, a, g, :].rearrange("p (n r) -> p r n", r=CMP_ST)[:, 0:CMP_ST:2, ch:ch + NCMP]
                            pos = pcol[:, 4 + l, 88 + 16 * a + 8 * ch:88 + 16 * a + 8 * ch + 8]
                            ins = dve.tensor_tensor(awin[:, a, 8 * ch:8 * ch + 8, g * NCMP:(g + 1) * NCMP], win,
                                                    pos.unsqueeze(2).to_broadcast([P, 8, NCMP]), ALU.add)
                ins.then_inc(win_ready, 1)
                turns_out(nsa_turns + dil_turns)
                seen.more(nsa_exp)
                link(dve.tensor_scalar(gn[:, 1, :], gn[:, 1, :], 1.0, None, ALU.add))
                link(dve.reciprocal(gn[:, 1, :], gn[:, 1, :]))
                turns_out(fox_turns)
                for g in range(GRP):
                    b = tile(for_dve)
                    for t in range(T):
                        n = NSA // 2 * NCMP
                        ins = dve.tensor_scalar(pc[:, t, 4 * g:4 * g + 4, :].rearrange("p h n -> p (h n)"),
                                                b[:, t * n:(t + 1) * n], 1 / math.sqrt(HD), None, ALU.mult)
                    read(for_dve, ins)
                stored(for_dve)
                wide_of = lambda v: v.unsqueeze(3).to_broadcast([P, T, NSA, NCMP])
                mask_of = lambda c0: cst[:, c0:c0 + T * NCMP].rearrange("p (t n) -> p t n", t=T).unsqueeze(2)\
                    .to_broadcast([P, T, NSA, NCMP])
                link(dve.tensor_tensor(pc, pc, mask_of(C_CADD), ALU.add))
                link(dve.tensor_reduce(pcs, pc, axis=AX.X, op=ALU.max))
                dve.tensor_tensor(pc, pc, wide_of(pcs), ALU.subtract).then_inc(pc_in, 1)
                seen.more(pc_exp)
                link(dve.tensor_tensor(pc2, pc2, mask_of(C_CMASK), ALU.mult))
                link(dve.tensor_reduce(pcs, pc2, axis=AX.X, op=ALU.add))
                link(dve.tensor_scalar(pcs, pcs, 1e-30, None, ALU.max))
                link(dve.reciprocal(pcs, pcs))
                gc = gn[:, 1, :].rearrange("p (t h b) -> p t h b", t=T, b=3)[:, :, :, 0]
                link(dve.tensor_tensor(pcs, pcs, gc, ALU.mult))
                dve.tensor_tensor(pc, pc2, wide_of(pcs), ALU.mult).then_inc(pc_out, 1)
                softmax_heads(second_jobs)

                def norm_parts(order):
                    for r, t, hf in order:
                        b = tile(r)
                        dve.tensor_copy(wide[:, t, hf * 512:hf * 512 + 512], b[:, :]).then_inc(part_ready, 1)
                        parts[0] += 1
                        dve.wait_ge(part_ready, parts[0])
                        dve.sem_inc(r.read, 1)

                def add_normed(g):
                    if g == 0:
                        seen.more(bc_loaded, 32)
                    for t in range(T):
                        seen.more(rstd_ready)
                        for hf in range(2):
                            cols = slice(hf * 512, hf * 512 + 512)
                            link(dve.scalar_tensor_tensor(out=wide[:, t, cols], in0=wide[:, t, cols],
                                                          scalar=stat[:, 8 + t:9 + t],
                                                          in1=rowbc[:, g, cols], op0=ALU.mult, op1=ALU.mult))
                            dve.tensor_tensor(x[:, t, cols], x[:, t, cols], wide[:, t, cols], ALU.add).then_inc(part_ready, 1)
                            parts[0] += 1
                    dve.wait_ge(part_ready, parts[0])

                norm_parts([(for_dve, t, hf) for hf in range(2) for t in range(T)])
                add_normed(0)
                scale_tokens()
                features_out(pcol[:, 2 + l, 96:104])
                w0c, w1c = pcol[:, 2 + l, 0:44], pcol[:, 2 + l, 44:88]
                for j in range(CH // 2 + 1):
                    if j < CH // 2:
                        for hf in range(2):
                            b = tile(for_dve)
                            seen.more(conv_base)
                            for f in range(2):
                                ch = hf * CH + 2 * j + f
                                dst = cv[:, j % 2, hf, f * S:(f + 1) * S]
                                link(dve.scalar_tensor_tensor(out=dst[:, 1:S], in0=b[:, f * S:(f + 1) * S - 1], scalar=w1c[:, ch:ch + 1],
                                                              in1=dst[:, 1:S], op0=ALU.mult, op1=ALU.add))
                                link(dve.scalar_tensor_tensor(out=dst[:, 2:S], in0=b[:, f * S:(f + 1) * S - 2], scalar=w0c[:, ch:ch + 1],
                                                              in1=dst[:, 2:S], op0=ALU.mult, op1=ALU.add))
                            dve.sem_inc(for_dve.read, 1)
                            if hf == 0:
                                dve.sem_inc(silu_in, 1)
                    if j >= 1:
                        m = (j - 1) % 2
                        seen.more(silu_out)
                        dst = hidT[:, 2 * (j - 1):2 * j, :].rearrange("p c s -> p (c s)")
                        dve.tensor_tensor(dst, cv[:, m, 0, :], cv[:, m, 1, :], ALU.mult).then_inc(conv_done, 1)
                norm_parts([(for_dve, 0, 0), (for_dve, 0, 1), (outputs, 1, 0), (outputs, 1, 1)])
                add_normed(1)

    return nc


NAMES = ["x", "c", "positions", "w_ada", "b_ada", "norm1_g", "norm2_g", "w_in", "q_norm_g", "w_uq",
         "kv_norm_g", "w_ukv", "w_o_mla", "w_o_sb", "w_o_moba", "w_out", "w_ff1", "w_ff2", "final_norm_g",
         "positions_2", "attn_pre_norm_2", "attn_post_norm_2", "ffn_pre_norm_2", "ffn_post_norm_2",
         "w_in_2", "b_forget_2", "b_nsa_gate_2", "cmp_pos_k_2", "cmp_w1_k_2", "cmp_w2_k_2", "cmp_pos_v_2",
         "cmp_w1_v_2", "cmp_w2_v_2", "w_out_2", "w_up_2", "conv_w_2", "conv_b_2", "w_down_2"]


def kernel(**inputs):
    import concourse.bacc as bacc
    from concourse.bass_utils import run_bass_kernel_spmd

    nc = bacc.Bacc("TRN2", target_bir_lowering=False, num_devices=1)
    arrays, args = {}, []
    for name in NAMES:
        a = np.ascontiguousarray(inputs[name])
        arrays[f"in_{name}"] = a
        args.append(nc.dram_tensor(f"in_{name}", a.shape, mybir.dt.from_np(a.dtype), kind="ExternalInput").ap())
    table = constants()
    arrays["table"] = table
    args.append(nc.dram_tensor("table", table.shape, F32, kind="ExternalInput").ap())
    args.append(nc.dram_tensor("out_0", (1, S, D), F32, kind="ExternalOutput").ap())
    two_blocks(nc, *args)
    r = run_bass_kernel_spmd(nc, [arrays], core_ids=[0])
    return r.results[0]["out_0"]
```

```python
import contextlib
import math

import numpy as np
import concourse.bass as bass
from concourse import mybir

F32 = mybir.dt.float32
F32R = mybir.dt.float32r
I32 = mybir.dt.int32
ACT = mybir.ActivationFunctionType
ALU = mybir.AluOpType
AX = mybir.AxisListType

P = 128
S, D, DEPTH = 256, 1024, 2
T = S // P
KD = D // P
EPS = 1e-6
NEG = -1e30
THETA = 500000.0
HD = 64

NH = 8
NOPE, ROPE = 64, 32
QK = NOPE + ROPE
QR, KVR = 768, 256
ATT = QR + KVR + ROPE + 6 * NH * HD
SB0 = QR + KVR + ROPE
MB0 = SB0 + 3 * NH * HD
D_IN = ATT + 3 * D
FF1 = 4 * D
ATT_W = 464
UQ_W = NH * QK // 2

FOX, NSA, GRP, DIL = 4, 8, 2, 4
FQ, FK, FV, FG = 0, FOX * HD, 2 * FOX * HD, 3 * FOX * HD
NQ = FG + FOX
KC = NQ + NSA * HD
VC, KS, VS, KW, VW = (KC + n * GRP * HD for n in range(1, 6))
NG = KC + 6 * GRP * HD
DQ = NG + 3 * NSA
DK, DV = DQ + DIL * HD, DQ + 2 * DIL * HD
N_IN = DV + DIL * HD
IN2_W = N_IN // 6
CMP_L, CMP_ST, CMP_H = 32, 16, 256
NCMP = (S - CMP_L) // CMP_ST + 1
FF2 = 2816
CH = FF2 // P
WU = 4096
SLOTS = 3
QUARTERS = 4
NSM, NPT = 6, 4
AUG = HD + 2

C_ID, C_ONE, C_TRI, C_NTRI, C_NONE = (n * P for n in range(5))
C_CAUS = 5 * P
C_DMASK = C_CAUS + 3 * P
C_DW = C_DMASK + 3 * P
C_CMASK = C_DW + 3 * P
C_CADD = C_CMASK + T * NCMP
C_SMASK = C_CADD + T * NCMP
C_INV = C_SMASK + 3 * P
C_N = C_INV + 32

TWO_PI = 2 * math.pi
PI_A = 6.28125
PI_B = float(np.float32(np.floor((TWO_PI - PI_A) * 2**20) / 2**20))
PI_C = float(np.float32(TWO_PI - PI_A - PI_B))
ROUNDER = 12582912.0
PI_SAFE = 3.1415925


def constants():
    c = np.zeros((P, C_N), np.float32)
    i = np.arange(P)
    c[:, C_ID:C_ID + P] = np.eye(P)
    c[:, C_ONE:C_ONE + P] = 1.0
    c[:, C_TRI:C_TRI + P] = i[:, None] <= i[None, :]
    c[:, C_NTRI:C_NTRI + P] = -(i[:, None] >= i[None, :]).astype(np.float32)
    c[:, C_NONE:C_NONE + P] = -1.0
    q = np.concatenate([np.broadcast_to(i[:, None], (P, P)), np.broadcast_to(P + i[:, None], (P, S))], 1)
    k = np.concatenate([np.broadcast_to(i[None], (P, P)), np.broadcast_to(np.arange(S)[None], (P, S))], 1)
    back = q - k
    c[:, C_CAUS:C_CAUS + 3 * P] = np.where(back >= 0, 0.0, NEG)
    times = sum(((back >= 0) & (back % d == 0) & (back <= w)).astype(np.float32)
                for w, d in ((128, 1), (512, 4), (2048, 16)))
    c[:, C_DMASK:C_DMASK + 3 * P] = np.where(times > 0, 0.0, NEG)
    c[:, C_DW:C_DW + 3 * P] = times
    after = np.where(i[None, :] > i[:, None], 0.0, NEG)
    c[:, C_SMASK:C_SMASK + P] = after
    c[:, C_SMASK + 2 * P:C_SMASK + 3 * P] = after
    ends = np.arange(NCMP) * CMP_ST + CMP_L - 1
    for t in range(T):
        seen = ends[None, :] <= t * P + i[:, None]
        c[:, C_CMASK + t * NCMP:C_CMASK + (t + 1) * NCMP] = seen
        c[:, C_CADD + t * NCMP:C_CADD + (t + 1) * NCMP] = np.where(seen, 0.0, NEG)
    for at, rot in ((0, ROPE), (16, HD // 4), (24, HD // 4)):
        inv = np.float32(THETA) ** (-np.arange(0, rot, 2, dtype=np.float32) / np.float32(rot))
        c[:, C_INV + at:C_INV + at + rot // 2] = inv
    return c


def two_blocks(nc, x_in, c_in, positions, w_ada, b_ada, norm1_g, norm2_g, w_in, q_norm_g, w_uq,
               kv_norm_g, w_ukv, w_o_mla, w_o_sb, w_o_moba, w_out, w_ff1, w_ff2, final_norm_g,
               positions_2, attn_pre, attn_post, ffn_pre, ffn_post, w_in_2, b_forget, b_nsa,
               pos_k, cw1_k, cw2_k, pos_v, cw1_v, cw2_v, w_out_2, w_up, conv_w, conv_b, w_down,
               table, out, LAYERS1=DEPTH, LAYERS2=DEPTH):
    ctx = contextlib.ExitStack()
    with ctx:
        def sb(name, shape, dt=F32):
            return ctx.enter_context(nc.sbuf_tensor(name, shape, dt))

        def sem(name):
            return ctx.enter_context(nc.semaphore(name))

        shared = (
            ("featT", [P, KD, S]),
            ("oT", [P, 12, S]),
            ("kvm", [P, T, NH * (QK + HD)]),
            ("pT", [P, NPT, 3 * P]),
            ("gates", [P, T, 3 * D]),
            ("ring", [P, SLOTS, WU]))
        with contextlib.ExitStack() as first:
            featT, oT, kvm, pT, gates, ring = [first.enter_context(nc.sbuf_tensor(n, shape, F32)) for n, shape in shared]
        featT_r, oT_r, kvm_r, pT_r, gates_r, ring_r = [sb(n + "_r", shape, F32R) for n, shape in shared]
        cst = sb("cst", [P, C_N])
        x = sb("x", [P, T, D])
        wide = sb("wide", [P, T, D])
        big = sb("big", [P, 33 * S])
        sm = sb("sm", [P, NSM, 3 * P])
        qz = sb("qz", [P, 12, S])
        ada = sb("ada", [P, 2, 512])
        rowbc = sb("rowbc", [P, 2, D])
        pcol = sb("pcol", [P, 6, P])
        mod = sb("mod", [P, 32])
        small = sb("small", [P, DEPTH, FOX + 3 * NSA])
        cw2 = sb("cw2", [P, DEPTH, 2, 2, HD])
        posi = sb("posi", [4, P], I32)
        posf = sb("posf", [4, P])
        cs = sb("cs", [P, 2, T, 32])
        trig = sb("trig", [P, 3, T * 32])
        posc = sb("posc", [P, 4])
        tiny = sb("tiny", [P, 80])
        stat = sb("stat", [P, 24])
        mx = sb("mx", [P, NSM, T])
        rs = sb("rs", [P, NSM, T])
        half = sb("half", [P, T])
        fox = sb("fox", [P, 3, T * FOX])
        gn = sb("gn", [P, 2, T * 3 * NSA])

        proj = big[:, 0:T * ATT].rearrange("p (t n) -> p t n", t=T)
        proj2 = big[:, 0:T * N_IN].rearrange("p (t n) -> p t n", t=T)
        hidT = big[:, 0:32 * S].rearrange("p (c s) -> p c s", s=S)
        qmla = proj[:, :, 0:QR]
        k_mla = kvm[:, :, 0:NH * QK].rearrange("p t (h e) -> p t h e", e=QK)
        v_mla = kvm[:, :, NH * QK:]
        featF = oT[:, 0:8, :]
        featL = oT_r[:, 0:8, :]
        kvm_flat = kvm_r[:, :, :].rearrange("p t n -> p (t n)")
        high = [kvm_flat[:, 0:1024], kvm_flat[:, 1024:2048],
                oT_r[:, 8:12, :].rearrange("p c s -> p (c s)"), pT_r[:, :, :].rearrange("p b n -> p (b n)")[:, 0:1024]]
        hid_parts = gates_r[:, :, :].rearrange("p t n -> p (t n)")[:, 2048:6144].rearrange("p (a b c s) -> p a b c s", a=2, b=2, c=4)
        c_act = tiny[:, 0:8]
        c_tmp = tiny[:, 8:16]
        rope_t = sm[:, :, :].rearrange("p b n -> p (b n)")[:, 0:4 * 256].rearrange("p (a n) -> p a n", a=4)
        wideT = wide[:, :, :].rearrange("p t n -> p (t n)").rearrange("p (c s) -> p c s", s=S)
        ident = cst[:, C_ID:C_ID + P]
        gf = gates[:, :, :].rearrange("p t n -> p (t n)")
        prow = gf[:, 0:6 * P].rearrange("p (m n) -> p m n", m=6)
        faug = gf[:, 0:T * 2 * FOX * AUG].rearrange("p (t a h e) -> p t a h e", t=T, a=2, h=FOX)
        UOFF = T * 2 * FOX * AUG
        U = gf[:, UOFF:UOFF + 2 * GRP * S].rearrange("p (a g s) -> p a g s", a=2, g=GRP)
        AOFF = UOFF + 2 * GRP * S
        awin = gf[:, AOFF:AOFF + 2 * 16 * GRP * NCMP].rearrange("p (a c n) -> p a c n", a=2, c=16)
        GOFF = AOFF + 2 * 16 * GRP * NCMP
        gel = gf[0:GRP * NCMP, GOFF:GOFF + 512]
        HOFF = GOFF + 3 * 512
        hT = gf[:, HOFF:HOFF + 4 * GRP * NCMP].rearrange("p (a n) -> p a n", a=4)
        KOFF = HOFF + 4 * GRP * NCMP
        kcT = gf[:, KOFF:KOFF + NCMP]
        vcm = gf[:, KOFF + 16:KOFF + 16 + GRP * HD].rearrange("p (g d) -> p g d", g=GRP)
        nq = gf[:, KOFF + 16 + GRP * HD:KOFF + 16 + GRP * HD + T * NSA * HD].rearrange(
            "p (t j g d) -> p t j g d", t=T, j=4, g=GRP)
        kf = kvm[:, :, :].rearrange("p t n -> p (t n)")
        pc = kf[:, 0:T * NSA * NCMP].rearrange("p (t h n) -> p t h n", t=T, h=NSA)
        pc2 = kf[:, 240:240 + T * NSA * NCMP].rearrange("p (t h n) -> p t h n", t=T, h=NSA)
        pcs = kf[:, 480:480 + T * NSA].rearrange("p (t h) -> p t h", t=T)
        pcT = kf[:, 496:496 + NSA * S].rearrange("p (h s) -> p h s", s=S)
        cv = gf[:, 0:2 * 2 * 512].rearrange("p (b a n) -> p b a n", b=2, a=2)

        banks = [ctx.enter_context(nc.psum_tensor(f"bank{n}", [P, 512], F32)) for n in range(8)]

        class Tiles:

            def __init__(self, name, own):
                self.banks = own
                self.full = sem(f"{name}_full")
                self.read = sem(f"{name}_read")

        for_act = Tiles("for_act", banks[0:2])
        for_dve = Tiles("for_dve", banks[2:6])
        outputs = Tiles("outputs", banks[6:8])

        w_used = sem("w_used")
        w_loaded = [sem(f"w_loaded{n}") for n in range(SLOTS)]
        w_rest = [sem(f"w_rest{n}") for n in range(SLOTS)]
        const_loaded = sem("const_loaded")
        masks_loaded = sem("masks_loaded")
        c_loaded = sem("c_loaded")
        rows_loaded = sem("rows_loaded")
        late_loaded = sem("late_loaded")
        small_loaded = sem("small_loaded")
        x_loaded = sem("x_loaded")
        bc_loaded = sem("bc_loaded")
        out_stored = sem("out_stored")
        act_chain, dve_chain, pool_chain = sem("act_chain"), sem("dve_chain"), sem("pool_chain")
        pos_cast = sem("pos_cast")
        angles = sem("angles")
        sines = sem("sines")
        c_exp = sem("c_exp")
        ada_used = sem("ada_used")
        ada_ready = sem("ada_ready")
        zeroed = sem("zeroed")
        squares = sem("squares")
        rstd_ready = sem("rstd_ready")
        scaled = sem("scaled")
        part_ready = sem("part_ready")
        evac_act = sem("evac_act")
        ready_dve = sem("ready_dve")
        merged = sem("merged")
        s_masked = sem("s_masked")
        s_exp = sem("s_exp")
        p_ready = sem("p_ready")
        sb_log, sb_raw, sb_keep = sem("sb_log"), sem("sb_raw"), sem("sb_keep")
        sb_total, sb_masked, sb_ready = sem("sb_total"), sem("sb_masked"), sem("sb_ready")
        evac_dve = sem("evac_dve")
        conv_done = sem("conv_done")
        feature_tiles = []
        hid_split = sem("hid_split")
        hid_tile0 = []
        stick_tile0, conv_tile0 = [], []
        fox_in, fox_log, fox_lf = sem("fox_in"), sem("fox_log"), sem("fox_lf")
        nsa_in, nsa_exp = sem("nsa_in"), sem("nsa_exp")
        win_ready = sem("win_ready")
        pc_in, pc_exp, pc_out = sem("pc_in"), sem("pc_exp"), sem("pc_out")
        quarter_used = sem("quarter_used")
        high_ready = sem("high_ready")
        low_dve, low_pool = sem("low_dve"), sem("low_pool")
        feat_high = sem("feat_high")
        feat_dve, feat_pool = sem("feat_dve"), sem("feat_pool")
        conv_base, silu_in, silu_out = sem("conv_base"), sem("silu_in"), sem("silu_out")
        PARTS1, PARTS2 = 8, 16

        def rows_of(w, n0, n1, c0, c1):
            return w[n0 * P:n1 * P, c0:c1].rearrange("(k p) n -> p k n", p=P)

        def slot_view(u, k, n, of=ring):
            return of[:, u % SLOTS, 0:k * n].rearrange("p (k n) -> p k n", k=k)

        units = []
        in_2_done = []

        def plain(w, k0, k1, c0, c1, reader="pe"):
            k, n = k1 - k0, c1 - c0
            units.append(dict(k=k, n=n, reader=reader, split=0,
                              parts=[(slice(0, P), slice(0, k), slice(0, n), rows_of(w, k0, k1, c0, c1))]))

        def split(w, *cols, rows=(0, KD), per=2):
            parts, k = [], rows[1] - rows[0]
            for k0 in (0, k // 2):
                at = 0
                for c0, c1 in cols:
                    parts.append((slice(0, P), slice(k0, k0 + k // 2), slice(at, at + c1 - c0),
                                  rows_of(w, rows[0] + k0, rows[0] + k0 + k // 2, c0, c1)))
                    at += c1 - c0
            units.append(dict(k=k, n=at, reader="pe", split=k // per, per=per, parts=parts))

        def ada_unit(l, u):
            plain(w_ada[l], 0, KD, 512 * u, 512 * u + 512, "dve")

        ADA_LATE = {0: 4, 2: 5, 4: 6, 6: 7, 8: 8, 10: 9, 12: 10, 13: 11}
        for l in range(LAYERS1):
            if l == 0:
                for u in range(4):
                    ada_unit(l, u)
            for u in range(15):
                c0 = u * ATT_W if u < 9 else ATT + 512 * (u - 9)
                split(w_in[l], (c0, min(c0 + ATT_W, ATT) if u < 9 else c0 + 512))
                if u in ADA_LATE:
                    ada_unit(l, ADA_LATE[u])
            for u in range(2):
                plain(w_uq[l], 0, QR // P, UQ_W * u, UQ_W * u + UQ_W)
            plain(w_ukv[l], 0, KVR // P, 0, 2 * NH * HD)
            for w in (w_o_mla, w_o_sb, w_o_moba):
                plain(w[l], 0, 4, 0, D)
            for u in range(2):
                split(w_out[l], (512 * u, 512 * u + 512))
            for u in range(8):
                split(w_ff1[l], (512 * u, 512 * u + 512))
                if l + 1 < LAYERS1 and u < 4:
                    ada_unit(l + 1, u)
            for u in range(8):
                split(w_ff2[l], (0, D), rows=(4 * u, 4 * u + 4), per=1)
        for l in range(LAYERS2):
            for u in range(6):
                split(w_in_2[l], (IN2_W * u, IN2_W * u + IN2_W))
            in_2_done.append(sum(it["split"] for it in units))
            for w in (cw1_k, cw1_v):
                plain(w[l], 0, 16, 0, CMP_H)
            for u in range(2):
                cols = slice(512 * u, 512 * u + 512)
                w = w_out_2[l]
                lo = FOX * HD
                lower = w[lo:lo + 4 * HD, cols].rearrange("(j p) n -> p j n", p=HD)
                upper = w[lo + 4 * HD:lo + 8 * HD, cols].rearrange("(j p) n -> p j n", p=HD)
                units.append(dict(k=KD, n=512, reader="pe", split=0, parts=[
                    (slice(0, P), slice(0, 2), slice(0, 512), rows_of(w, 0, 2, cols.start, cols.stop)),
                    (slice(0, HD), slice(2, 6), slice(0, 512), lower),
                    (slice(HD, P), slice(2, 6), slice(0, 512), upper),
                    (slice(0, P), slice(6, 8), slice(0, 512), rows_of(w, 6, 8, cols.start, cols.stop))]))
            for j in range(CH // 2):
                a0, b0 = 256 * j, FF2 + 256 * j
                split(w_up[l], (a0, a0 + 256), (b0, b0 + 256))
            for k0 in range(0, CH, 4):
                split(w_down[l], (0, D), rows=(k0, min(k0 + 4, CH)), per=1)
        loads, rests, read_by = [0] * SLOTS, [0] * SLOTS, {"pe": 0, "dve": 0}
        for u, it in enumerate(units):
            n = len(it["parts"])
            it["first"] = n // 2 if it["split"] else n
            loads[u % SLOTS] += 16 * it["first"]
            rests[u % SLOTS] += 16 * (n - it["first"])
            read_by[it["reader"]] += 1
            it.update(slot=u % SLOTS, loaded=loads[u % SLOTS], rest=rests[u % SLOTS], turn=read_by[it["reader"]],
                      view=slot_view(u, it["k"], it["n"]), view_r=slot_view(u, it["k"], it["n"], ring_r))
        used_by = {"pe": w_used, "dve": ada_used}
        split_units, lows, q = [], {"dve": 0, "pool": 0}, 0
        for it in units:
            if it["split"]:
                quarters = []
                split_units.append(quarters)
                for j in range(it["split"]):
                    owner = "pool" if j % 2 else "dve"
                    lows[owner] += 1
                    n, per = it["n"], it["per"]
                    quarters.append(dict(
                        q=q, owner=owner, turn=lows[owner],
                        loaded=(w_loaded[it["slot"]], it["loaded"]) if j < it["split"] // 2 else (w_rest[it["slot"]], it["rest"]),
                        raw=it["view"][:, per * j:per * j + per, :], low=it["view_r"][:, per * j:per * j + per, :],
                        high=high[q % QUARTERS][:, 0:per * n].rearrange("p (k n) -> p k n", k=per)))
                    q += 1

        def units_for(reader):
            return iter([it for it in units if it["reader"] == reader])

        def turn(src, rows, *dst, scale=1.0):
            return dict(src=src, rows=rows, dst=dst, scale=scale)

        def cols_of(src, c0, n):
            return [src[:, t, c0:c0 + n] for t in range(T)]

        def flat(n):
            return featT[:, n, :] if n < 8 else wideT[:, n - 8, :]

        def padded(n):
            return [(0, HD, qz[:, n, :]), (HD, P, qz[:, n + 1, :])]

        def whole(n, rows=P):
            return (0, rows, flat(n))

        def job(heads, scale, chunk, mask=C_CAUS, weight=False, first=True, last=True, cmp=None):
            return dict(heads=heads, scale=scale, chunk=chunk, mask=mask, weight=weight, first=first, last=last, cmp=cmp)

        def head(q, k, v, gate=None):
            return dict(q=q, k=k, v=v, gate=gate)

        SC = 1 / math.sqrt(HD)
        mla_turns = [turn(cols_of(qmla, h * QK, QK), QK, whole(h, QK)) for h in range(NH)] + \
                    [turn([k_mla[:, t, h, :] for t in range(T)], QK, whole(NH + h, QK)) for h in range(NH)]
        mla_jobs = [job([head(flat(h)[0:QK, :], flat(NH + h)[0:QK, :], v_mla[:, :, h * HD:(h + 1) * HD])
                         for h in (2 * j, 2 * j + 1)], 1 / math.sqrt(QK), j) for j in range(NH // 2)]
        sb_turns = [turn(cols_of(proj, SB0 + j * P, P), P, *padded(2 * j), scale=SC) for j in range(4)] + \
                   [turn(cols_of(proj, SB0 + NH * HD + j * P, P), P, whole(j)) for j in range(4)]
        moba_turns = [turn(cols_of(proj, MB0 + j * P, P), P, *padded(2 * j)) for j in range(4)] + \
                     [turn(cols_of(proj, MB0 + NH * HD + j * P, P), P, whole(4 + j)) for j in range(4)]
        v0 = MB0 + 2 * NH * HD
        moba_jobs = [job([head(qz[:, h, :], flat(4 + j), proj[:, :, v0 + h * HD:v0 + (h + 1) * HD])
                          for h in (2 * j, 2 * j + 1)], SC, 8 + j) for j in range(NH // 2)]
        fox_turns = [turn([faug[:, t, a, h, :] for t in range(T)], AUG, whole(FOX * a + h, AUG))
                     for a in range(2) for h in range(FOX)]
        nsa_turns = [turn([nq[:, t, j, :, :].rearrange("p g d -> p (g d)") for t in range(T)], P, *padded(2 * j))
                     for j in range(4)] + \
                    [turn(cols_of(proj2, KS, P), P, whole(8)), turn(cols_of(proj2, KW, P), P, whole(9))]
        dil_turns = [turn(cols_of(proj2, DQ + j * P, P), P, *padded(8 + 2 * j)) for j in range(2)] + \
                    [turn(cols_of(proj2, DK + j * P, P), P, whole(10 + j)) for j in range(2)]
        second_jobs = [job([head(flat(h)[0:AUG, :], flat(FOX + h)[0:AUG, :], proj2[:, :, FV + h * HD:FV + (h + 1) * HD])
                            for h in (2 * j, 2 * j + 1)], 1.0, j) for j in range(FOX // 2)]
        for j in range(NSA // 2):
            for br, (vb, kt) in enumerate(((VS, 8), (VW, 9))):
                second_jobs.append(job([head(qz[:, 2 * j + g, :], flat(kt), proj2[:, :, vb + g * HD:vb + (g + 1) * HD],
                                             gate=3 * (j + g * NSA // 2) + 1 + br) for g in range(GRP)],
                                       SC, 2 + j, first=False, last=br == 1,
                                       cmp=[j, j + NSA // 2] if br == 0 else None))
        for j in range(DIL // 2):
            second_jobs.append(job([head(qz[:, 8 + h, :], flat(10 + j), proj2[:, :, DV + h * HD:DV + (h + 1) * HD])
                                    for h in (2 * j, 2 * j + 1)], SC, 6 + j, mask=C_DMASK, weight=True))

        LAST_PART = PARTS1 * LAYERS1 + (4 if LAYERS1 else 0) + PARTS2 * LAYERS2
        block = ctx.enter_context(nc.Block())

        class Seen:

            def __init__(self, eng):
                self.eng, self.n = eng, {}

            def more(self, s, k=1):
                key = s.name
                self.n[key] = self.n.get(key, 0) + k
                self.eng.wait_ge(s, self.n[key])

        @block.sync
        def _(sp):
            def row_load(tile, r0, vec, told):
                n = vec.shape[0] // P
                sp.dma_start(prow[r0:r0 + n, tile, :], vec.rearrange("(r p) -> r p", p=P)).then_inc(told, 16)

            def norm_rows(l, told):
                row_load(l, 0, norm1_g[l], told)
                row_load(l, 8, norm2_g[l], told)
                row_load(l, 16, q_norm_g[l], told)
                row_load(l, 22, kv_norm_g[l], told)
                row_load(l, 24, b_ada[l], told)

            def load_unit(it):
                for n, (ps, ks, ns, src) in enumerate(it["parts"]):
                    told = w_loaded if n < it["first"] else w_rest
                    sp.dma_start(it["view"][ps, ks, ns], src).then_inc(told[it["slot"]], 16)

            row_load(0, 72, c_in[0], c_loaded)
            norm_rows(0, c_loaded)
            sp.dma_start(cst[:, 0:C_CAUS], table[:, 0:C_CAUS]).then_inc(const_loaded, 16)
            for it in units[0:2]:
                load_unit(it)
            sp.dma_start(x[:, :, :], x_in[0].rearrange("(t p) n -> p t n", p=P)).then_inc(x_loaded, 16)
            norm_rows(1, rows_loaded)
            load_unit(units[2])
            for u in range(SLOTS, len(units)):
                last = units[u - SLOTS]
                sp.wait_ge(used_by[last["reader"]], last["turn"])
                load_unit(units[u])
                if u == SLOTS + 1:
                    sp.dma_start(cst[:, C_CAUS:], table[:, C_CAUS:]).then_inc(masks_loaded, 16)
                    for l in range(DEPTH):
                        row_load(2 + l, 0, conv_w[l, 0], late_loaded)
                        row_load(2 + l, 44, conv_w[l, 1], late_loaded)
                        row_load(2 + l, 88, attn_pre[l], late_loaded)
                        row_load(2 + l, 96, ffn_pre[l], late_loaded)
                        row_load(4 + l, 0, conv_w[l, 2], late_loaded)
                        row_load(4 + l, 44, conv_b[l], late_loaded)
                        row_load(4 + l, 88, pos_k[l].rearrange("a b -> (a b)"), late_loaded)
                        row_load(4 + l, 104, pos_v[l].rearrange("a b -> (a b)"), late_loaded)
                    sp.dma_start(posi[0:2, :], positions[0].rearrange("(t p) -> t p", p=P)).then_inc(late_loaded, 16)
                    sp.dma_start(posi[2:4, :], positions_2[0].rearrange("(t p) -> t p", p=P)).then_inc(late_loaded, 16)
            sp.wait_ge(part_ready, LAST_PART)
            sp.dma_start(out[0].rearrange("(t p) n -> p t n", p=P), x[:, :, :]).then_inc(out_stored, 16)
            sp.wait_ge(out_stored, 16)

        x1 = PARTS1 * LAYERS1 + (4 if LAYERS1 else 0)
        N_LATE = 16 * (8 * DEPTH + 2)
        LATE_AT = 2
        N_POOL_ROWS = 16 * 4 * DEPTH

        @block.gpsimd
        def _(pool):
            seen = Seen(pool)
            chain = [0]

            def link(ins):
                chain[0] += 1
                ins.then_inc(pool_chain, 1)
                pool.wait_ge(pool_chain, chain[0])

            for l in range(DEPTH):
                pool.dma_start(small[:, l, 0:FOX], b_forget[l].partition_broadcast(P)).then_inc(small_loaded, 16)
                pool.dma_start(small[:, l, FOX:], b_nsa[l].partition_broadcast(P)).then_inc(small_loaded, 16)
                for a, w in enumerate((cw2_k, cw2_v)):
                    pool.dma_start(cw2[:, l, a, :, :], w[l].rearrange("(k p) n -> p k n", p=P)).then_inc(small_loaded, 16)
            link(pool.memset(half[:, :], -0.5))

            def load_rows(a, b):
                pool.dma_start(rowbc[:, 0, :], a.partition_broadcast(P)).then_inc(bc_loaded, 16)
                pool.dma_start(rowbc[:, 1, :], b.partition_broadcast(P)).then_inc(bc_loaded, 16)

            def rstd(s0, width):
                seen.more(squares)
                link(pool.tensor_scalar(stat[:, s0:s0 + T], stat[:, s0:s0 + T], 1.0 / width, EPS, ALU.mult, ALU.add))
                pool.tensor_tensor(stat[:, s0 + T:s0 + 2 * T], stat[:, s0:s0 + T], half[:, 0:T], ALU.pow).then_inc(rstd_ready, 1)

            def rstd_parts(need):
                for t in range(T):
                    seen.more(squares, need[t])
                    link(pool.tensor_scalar(stat[:, 4 + t:5 + t], stat[:, 2 * t:2 * t + 1], 1.0 / D, EPS, ALU.mult, ALU.add))
                    link(pool.tensor_scalar(stat[:, 6 + t:7 + t], stat[:, 2 * t + 1:2 * t + 2], 1.0 / D, stat[:, 4 + t:5 + t],
                                            ALU.mult, ALU.add))
                    pool.tensor_tensor(stat[:, 8 + t:9 + t], stat[:, 6 + t:7 + t], half[:, 0:1], ALU.pow).then_inc(rstd_ready, 1)

            cut = iter(split_units)

            def low_part(it):
                seen.more(high_ready)
                pool.tensor_tensor(it["low"], it["raw"], it["high"].bitcast(F32), ALU.subtract).then_inc(low_pool, 1)

            def begin():
                unit = next(cut)
                low_part(unit[1])
                low_features()
                low_part(unit[3])

            def low_parts(units_):
                for _ in range(units_):
                    for it in next(cut):
                        if it["owner"] == "pool":
                            low_part(it)

            def low_features():
                for t in range(T):
                    cols = slice(t * P, (t + 1) * P)
                    seen.more(feat_high)
                    pool.tensor_tensor(featL[:, 0:4, cols], featF[:, 0:4, cols], featT_r[:, 0:4, cols].bitcast(F32),
                                       ALU.subtract).then_inc(feat_pool, 1)

            def diagonal(view, told):
                blocks = view.rearrange("p (b q) -> p b q", q=P)[:, 0:3:2, :]
                pool.affine_select(out=blocks, in_=blocks, pattern=[[0, 2], [1, P]], compare_op=ALU.is_gt,
                                   fill=0.0, base=0, channel_multiplier=-1).then_inc(told, 1)

            pool.memset(qz[:, :, :], 0.0).then_inc(zeroed, 1)
            IN_TURN, BY_HALVES = (2, 2), (3, 1)
            for l in range(LAYERS1):
                if l:
                    pool.wait_ge(part_ready, PARTS1 * l)
                load_rows(b_ada[l, 2 * D:3 * D], b_ada[l, 5 * D:6 * D])
                rstd_parts(IN_TURN)
                begin()
                low_parts(9)
                rstd(12, QR)
                rstd(16, KVR)
                low_parts(5)
                for h in range(NH):
                    seen.more(sb_raw)
                    diagonal(sm[:, h % NSM, :], sb_keep)
                begin()
                low_parts(1)
                rstd_parts(BY_HALVES)
                begin()
                low_parts(7 + 8)
            if LAYERS1:
                pool.dma_start(rowbc[:, 0, :], final_norm_g.partition_broadcast(P)).then_inc(bc_loaded, 16)
                rstd_parts(IN_TURN)
            for l in range(LAYERS2):
                if x1 + l:
                    pool.wait_ge(part_ready, x1 + PARTS2 * l)
                pool.memset(vcm, 0.0).then_inc(zeroed, 1)
                load_rows(attn_post[l], ffn_post[l])
                rstd_parts(IN_TURN)
                begin()
                low_parts(5)
                pool.wait_ge(quarter_used, in_2_done[l])
                pool.memset(pcT, 0.0).then_inc(zeroed, 1)
                low_parts(1)
                rstd_parts(BY_HALVES)
                rstd_parts(IN_TURN)
                low_features()
                low_parts(CH // 2 - 1 + (CH + 3) // 4)
                rstd_parts(IN_TURN)

        @block.tensor
        def _(pe):
            seen = Seen(pe)
            made = {id(for_act): 0, id(for_dve): 0, id(outputs): 0}
            owed = []
            cut = iter(split_units)
            mine = units_for("pe")

            def claim(ring_):
                n = made[id(ring_)]
                made[id(ring_)] = n + 1
                size = len(ring_.banks)
                if n >= size:
                    pe.wait_ge(ring_.read, n - size + 1)
                return ring_.banks[n % size], n + 1

            def mm(o, a, b, start=True, stop=True, full=None):
                ins = pe.matmul(o, a, b, start=start, stop=stop, skip_group_check=True)
                if full is not None:
                    ins.then_inc(full, 1)
                elif owed:
                    ins.then_inc(*owed.pop(0))
                return ins

            def flip(o, a, full=None):
                n = a.shape[0]
                ins = pe.transpose(o, a, ident[0:n, 0:n])
                if full is not None:
                    ins.then_inc(full, 1)
                elif owed:
                    ins.then_inc(*owed.pop(0))

            def weights():
                it = next(mine)
                pe.wait_ge(w_loaded[it["slot"]], it["loaded"])
                return it["view"], it["k"], it["n"]

            def flip_features(ready, parts=False):
                for t in range(T):
                    seen.more(ready)
                    for j, r in enumerate((for_act, for_dve)):
                        b, _n = claim(r)
                        for c in range(4):
                            f = 4 * j + c
                            flip(b[:, c * P:(c + 1) * P], wide[:, t, f * P:(f + 1) * P], r.full if c == 3 else None)
                    if parts:
                        feature_tiles.append(made[id(for_act)])
                if parts:
                    fresh.update(all_parts)
                    return
                for r in (for_act, for_dve):
                    pe.wait_ge(r.read, made[id(r)])

            all_parts = [(t, c) for t in range(T) for c in range(0, KD, 4)]
            fresh = set()

            def features(c, tiles):
                for t in tiles:
                    if (t, c - c % 4) in fresh:
                        fresh.discard((t, c - c % 4))
                        seen.more(feat_dve if c >= 4 else feat_pool)

            def next_quarters():
                unit = next(cut)
                waited = set()

                def get(j):
                    if j not in waited:
                        waited.add(j)
                        pe.wait_ge(low_dve if unit[j]["owner"] == "dve" else low_pool, unit[j]["turn"])
                    return unit[j]["high"], unit[j]["low"]

                return get, next(mine)["n"]

            def three(o, a, b, start, stop, full=None):
                mm(o, a[0], b[0], start, False)
                mm(o, a[0], b[1], False, False)
                mm(o, a[1], b[0], False, stop, full)

            def feature_parts(c, cols):
                return featT_r[:, c, cols], featL[:, c, cols]

            def tokens_by_quarters(rings):
                get, n = next_quarters()
                open_ = [claim(r)[0] for r in rings]
                for j in range(QUARTERS):
                    w = get(j)
                    for t in range(T):
                        for kk in range(2):
                            c = 2 * j + kk
                            features(c, [t])
                            three(open_[t][:, 0:n], feature_parts(c, slice(t * P, t * P + P)), (w[0][:, kk, :], w[1][:, kk, :]),
                                  c == 0, c == KD - 1, rings[t].full if c == KD - 1 else None)
                    owed.append((quarter_used, 1))
                owed.append((w_used, 1))

            def tokens_by_tiles(r):
                get, n = next_quarters()
                for t in range(T):
                    b, _n = claim(r)
                    for j in range(QUARTERS):
                        w = get(j)
                        for kk in range(2):
                            c = 2 * j + kk
                            features(c, [t])
                            three(b[:, 0:n], feature_parts(c, slice(t * P, t * P + P)), (w[0][:, kk, :], w[1][:, kk, :]),
                                  c == 0, c == KD - 1, r.full if c == KD - 1 else None)
                        if t:
                            owed.append((quarter_used, 1))
                owed.append((w_used, 1))

            def channels(r, by_quarters):
                get, n = next_quarters()
                both = slice(0, S)
                if by_quarters:
                    open_ = [claim(r)[0] for _ in range(2)]
                    steps = [(j, (0, 1)) for j in range(QUARTERS)]
                else:
                    open_ = [None, None]
                    steps = [(j, (i,)) for i in range(2) for j in range(QUARTERS)]
                for j, tiles in steps:
                    w = get(j)
                    for i in tiles:
                        if open_[i] is None:
                            open_[i] = claim(r)[0]
                        for f in range(2):
                            cols = slice((2 * i + f) * P, (2 * i + f + 1) * P)
                            for kk in range(2):
                                c = 2 * j + kk
                                features(c, range(T))
                                a, b = (w[0][:, kk, cols], w[1][:, kk, cols]), feature_parts(c, both)
                                three(open_[i][:, f * S:(f + 1) * S], a, b, c == 0 and f == 0, c == KD - 1,
                                      r.full if f and c == KD - 1 else None)
                    if 1 in tiles:
                        owed.append((quarter_used, 1))
                owed.append((w_used, 1))

            def linear(count, src):
                for _ in range(count):
                    w, k, n = weights()
                    for t, r in enumerate((for_act, for_dve)):
                        b, _n = claim(r)
                        for c in range(k):
                            mm(b[:, 0:n], src[:, c, t * P:(t + 1) * P], w[:, c, :], c == 0, c == k - 1,
                               r.full if c == k - 1 else None)
                    owed.append((w_used, 1))

            def linear_dve(count, src, width):
                for _ in range(count):
                    w, k, n = weights()
                    for c0 in range(0, n, width):
                        for t in range(T):
                            b, _n = claim(for_dve)
                            for c in range(k):
                                mm(b[:, 0:width], src[:, c, t * P:(t + 1) * P], w[:, c, c0:c0 + width], c == 0,
                                   c == k - 1, for_dve.full if c == k - 1 else None)
                    owed.append((w_used, 1))

            def linear_deep(chunks):
                owner = [for_dve, for_dve, outputs, outputs]
                open_ = [claim(r)[0] for r in owner]
                for c0 in range(0, chunks, 4):
                    get, _n = next_quarters()
                    seen.more(hid_split)
                    k = min(4, chunks - c0)
                    last_unit = c0 + k == chunks
                    steps = [(i, kk) for i in range(4) for kk in range(k)] if last_unit else \
                        [(i, kk) for kk in range(k) for i in range(4)]
                    for i, kk in steps:
                        t, cols = i // 2, slice(i % 2 * 512, i % 2 * 512 + 512)
                        w = get(kk)
                        h = [hid_parts[:, c0 // 4 % 2, part, kk, t * P:(t + 1) * P] for part in range(2)]
                        last = c0 + kk == chunks - 1
                        three(open_[i][:, :], h, (w[0][:, 0, cols], w[1][:, 0, cols]), c0 + kk == 0, last,
                              owner[i].full if last else None)
                        if i == 3:
                            owed.append((quarter_used, 1))
                    owed.append((w_used, 1))

            def turns(items):
                for j in range(0, len(items), 2):
                    r = (for_act, for_dve)[j // 2 % 2]
                    b, _n = claim(r)
                    for i, it in enumerate(items[j:j + 2]):
                        for t in range(T):
                            flip(b[0:it["rows"], (2 * i + t) * P:(2 * i + t + 1) * P], it["src"][t],
                                 r.full if t and i == len(items[j:j + 2]) - 1 else None)
                for r in (for_act, for_dve):
                    pe.wait_ge(r.read, made[id(r)])

            def softmax_heads(jobs):
                pt, out_bank = {}, None
                for i in range(len(jobs) + 3):
                    if i < len(jobs):
                        for hd in jobs[i]["heads"]:
                            b, _n = claim(for_dve)
                            mm(b[:, 0:P], hd["q"][:, 0:P], hd["k"][:, 0:P])
                            mm(b[:, P:3 * P], hd["q"][:, P:S], hd["k"], full=for_dve.full)
                    if 2 <= i < len(jobs) + 2:
                        for e in range(2):
                            n = (2 * (i - 2) + e) % NSM
                            seen.more(p_ready)
                            b, pt[i - 2, e] = claim(for_act)
                            for c in range(3):
                                flip(b[:, c * P:(c + 1) * P], sm[:, n, c * P:(c + 1) * P], for_act.full if c == 2 else None)
                    if i >= 3:
                        j = jobs[i - 3]
                        if out_bank is None:
                            out_bank = claim(outputs)[0]
                        start = j["first"]
                        if j["cmp"] is not None:
                            for e, h in enumerate(j["cmp"]):
                                mm(out_bank[HD * e:HD * e + HD, 0:S], vcm[:, e, :], pcT[:, h, :], True, False)
                        pe.wait_ge(for_act.read, pt[i - 3, 1])
                        for c in range(2):
                            for e, hd in enumerate(j["heads"]):
                                n = (2 * (i - 3) + e) % NPT
                                o = out_bank[HD * e:HD * e + HD, c * P:S]
                                mm(o, hd["v"][:, c, :], pT[:, n, S * c:S + P * c], start and c == 0, j["last"] and c == 1,
                                   outputs.full if j["last"] and c and e else None)
                        if j["last"]:
                            out_bank = None

            def stick_heads():
                zb = {}
                stick_tile0.append(made[id(for_dve)])
                ntri, nones = cst[:, C_NTRI:C_NTRI + P], cst[:, C_NONE:C_NONE + P]
                for i in range(NH // 2 + 2):
                    if i < NH // 2:
                        for h in (2 * i, 2 * i + 1):
                            q, k = qz[:, h, :], flat(i)
                            zb[h], _n = claim(for_dve)
                            mm(zb[h][:, 0:S], k[:, 0:P], q)
                            mm(zb[h][:, S:3 * P], k[:, P:S], q[:, P:S], False, True, for_dve.full)
                    if 1 <= i < NH // 2 + 1:
                        for h in (2 * i - 2, 2 * i - 1):
                            b, lk = zb[h], sm[:, h % NSM, :]
                            seen.more(sb_keep)
                            mm(b[:, 0:S], ntri, lk[:, 0:S], False, True)
                            mm(b[:, P:S], nones, lk[:, S:3 * P], False, True)
                            mm(b[:, S:3 * P], ntri, lk[:, S:3 * P], False, True, sb_total)
                    if i >= 2:
                        out_bank, _n = claim(outputs)
                        seen.more(sb_ready, 2)
                        for c in range(2):
                            for e in range(2):
                                h = 2 * (i - 2) + e
                                v0 = SB0 + 2 * NH * HD + h * HD
                                mm(out_bank[HD * e:HD * e + HD, c * P:S], proj[:, c, v0:v0 + HD],
                                   sm[:, h % NSM, S * c:S + P * c], c == 0, c == 1, outputs.full if c and e else None)

            def rows_to_columns(tiles, rows):
                b, _n = claim(for_act)
                for i, m in enumerate(tiles):
                    flip(b[:, i * P:i * P + rows[i]], prow[0:rows[i], m, :], for_act.full if m == tiles[-1] else None)

            def late_parameters():
                pe.wait_ge(late_loaded, N_LATE)
                pe.wait_ge(small_loaded, N_POOL_ROWS)
                rows_to_columns((2, 3, 4, 5), (104, 104, 120, 120))
                b, _n = claim(for_dve)
                seen.more(pos_cast)
                flip(b[:, 0:4], posf[:, :], for_dve.full)

            pe.wait_ge(const_loaded, 16)
            pe.wait_ge(c_loaded, 16 * 6)
            rows_to_columns((0,), (80,))
            pe.wait_ge(rows_loaded, 16 * 5)
            rows_to_columns((1,), (72,))

            def modulation(u):
                b, _n = claim(for_dve)
                seen.more(ada_ready)
                acc = ada[:, u % 2, :]
                if u // 2 % 3 == 2:
                    mm(b[:, :], cst[:, C_ONE:C_ONE + P], acc, full=for_dve.full)
                    return
                for f in range(4):
                    mm(b[:, f:f + 1], acc[:, f * P:(f + 1) * P], cst[:, C_ONE:C_ONE + 1], full=for_dve.full if f == 3 else None)

            seen.more(zeroed)
            for l in range(LAYERS1):
                if l == 0:
                    for u in range(4):
                        modulation(u)
                flip_features(scaled, True)
                for u in range(15):
                    if u < 9:
                        tokens_by_quarters((for_act, for_dve))
                    else:
                        tokens_by_tiles(for_act)
                    if u - 1 in ADA_LATE:
                        modulation(ADA_LATE[u - 1])
                    if l == 0 and u == LATE_AT:
                        late_parameters()
                flip_features(scaled)
                linear(2, featT)
                linear_dve(1, featT[:, 6:8, :], 512)
                seen.more(ready_dve)
                turns(mla_turns)
                softmax_heads(mla_jobs)
                turns(sb_turns)
                stick_heads()
                turns(moba_turns)
                softmax_heads(moba_jobs)
                pe.wait_ge(outputs.read, made[id(outputs)])
                for br in range(3):
                    w, k, n = weights()
                    for t in range(T):
                        for hf in range(2):
                            b, _n = claim(for_dve)
                            for c in range(4):
                                mm(b[:, :], oT[:, 4 * br + c, t * P:(t + 1) * P], w[:, c, hf * 512:hf * 512 + 512],
                                   c == 0, c == 3, for_dve.full if c == 3 else None)
                    owed.append((w_used, 1))
                flip_features(merged, True)
                for _ in range(2):
                    tokens_by_tiles(for_dve)
                flip_features(scaled, True)
                hid_tile0.append(made[id(for_act)])
                for u in range(8):
                    channels(for_act, False)
                    if l + 1 < LAYERS1 and 1 <= u < 5:
                        modulation(u - 1)
                linear_deep(FF1 // P)

            if not LAYERS1:
                late_parameters()
            for l in range(LAYERS2):
                flip_features(scaled, True)
                for _ in range(6):
                    tokens_by_quarters((for_act, for_dve))
                seen.more(fox_lf)
                b, _n = claim(for_dve)
                lf = fox[:, 2, :].rearrange("p (t h) -> p t h", t=T)
                tri, ones = cst[:, C_TRI:C_TRI + P], cst[:, C_ONE:C_ONE + P]
                mm(b[:, 0:FOX], tri, lf[:, 0, :])
                mm(b[:, FOX:2 * FOX], tri, lf[:, 1, :], True, False)
                mm(b[:, FOX:2 * FOX], ones, lf[:, 0, :], False, True, for_dve.full)
                seen.more(ready_dve)
                b, _n = claim(for_dve)
                for a, c0 in enumerate((KC, VC)):
                    for t in range(T):
                        flip(b[:, (2 * a + t) * P:(2 * a + t + 1) * P], proj2[:, t, c0:c0 + P],
                             for_dve.full if a and t else None)
                turns(nsa_turns + dil_turns)
                seen.more(win_ready)
                b, n = claim(for_act)
                ws = [weights()[0] for _ in range(2)]
                for c in range(16):
                    for a in range(2):
                        mm(b[HD * a:HD * a + GRP * NCMP, 0:CMP_H], awin[:, a, c, :], ws[a][:, c, :], c == 0, c == 15,
                           for_act.full if a and c == 15 else None)
                owed.append((w_used, 2))
                seen.more(ready_dve)
                turns(fox_turns)
                pe.wait_ge(for_act.read, n)
                b, n = claim(for_act)
                for m in range(4):
                    flip(b[:, m * 32:m * 32 + GRP * NCMP], gel[:, m * P:(m + 1) * P], for_act.full if m == 3 else None)
                pe.wait_ge(for_act.read, n)
                b, n = claim(for_act)
                for g in range(GRP):
                    for c in range(2):
                        mm(b[HD * g:HD * g + HD, 0:NCMP], cw2[:, l, 0, c, :], hT[:, c, g * NCMP:(g + 1) * NCMP], c == 0, c == 1)
                for g in range(GRP):
                    for c in range(2):
                        mm(b[0:NCMP, HD * (g + 1):HD * (g + 2)], hT[:, 2 + c, g * NCMP:(g + 1) * NCMP], cw2[:, l, 1, c, :],
                           c == 0, c == 1, for_act.full if g and c else None)
                pe.wait_ge(for_act.read, n)
                for g in range(GRP):
                    b, _n = claim(for_dve)
                    for h in range(NSA // 2):
                        for t in range(T):
                            at = (t * NSA // 2 + h) * NCMP
                            mm(b[:, at:at + NCMP], qz[:, 2 * h + g, t * P:(t + 1) * P], kcT,
                               full=for_dve.full if h == NSA // 2 - 1 and t else None)
                seen.more(pc_out)
                for h2 in range(NSA // 2):
                    b, n = claim(for_act)
                    for i in range(2):
                        for t in range(T):
                            flip(b[0:NCMP, (2 * i + t) * P:(2 * i + t + 1) * P], pc[:, t, 2 * h2 + i, :],
                                 for_act.full if i and t else None)
                pe.wait_ge(for_act.read, n)
                softmax_heads(second_jobs)
                pe.wait_ge(outputs.read, made[id(outputs)])
                linear_dve(2, oT, 512)
                flip_features(scaled, True)
                conv_tile0.append(made[id(for_dve)])
                for j in range(CH // 2):
                    channels(for_dve, True)
                linear_deep(CH)

        @block.scalar
        def _(act):
            seen = Seen(act)
            chain, got, sums_done = [0], [0], [0]

            def link(ins):
                chain[0] += 1
                ins.then_inc(act_chain, 1)
                act.wait_ge(act_chain, chain[0])

            def tile():
                n = got[0]
                got[0] += 1
                act.wait_ge(for_act.full, n + 1)
                return for_act.banks[n % 2]

            def read(ins):
                ins.then_inc(for_act.read, 1)

            def copy_out(dst, src):
                read(act.activation(dst, src, ACT.Copy))

            scratch = [sm[:, :, :].rearrange("p b n -> p (b n)")[:, t * D:(t + 1) * D] for t in range(T)]

            def sums(src, s0, width):
                for t in range(T):
                    ins = act.activation(scratch[t][:, 0:width], src[:, t, :], ACT.Square, accum_out=stat[:, s0 + t:s0 + t + 1])
                    if t == T - 1:
                        ins.then_inc(squares, 1)
                sums_done[0] += 1

            IN_TURN = [(0, 0), (0, 1), (1, 0), (1, 1)]
            BY_HALVES = [(0, 0), (1, 0), (0, 1), (1, 1)]

            def sums_of_parts(src, order, wait=True):
                for t, hf in order:
                    if wait:
                        seen.more(part_ready)
                    act.activation(scratch[t][:, hf * 512:hf * 512 + 512], src[:, t, hf * 512:hf * 512 + 512], ACT.Square,
                                   accum_out=stat[:, 2 * t + hf:2 * t + hf + 1]).then_inc(squares, 1)
                    sums_done[0] += 1

            def features_out(gain=None, shift=None, parts=False):
                dst = featF if parts else featT
                for t in range(T):
                    b = tile()
                    if gain is None:
                        copy_out(dst[:, 0:4, t * P:(t + 1) * P], b[:, :].rearrange("p (c s) -> p c s", c=4))
                        continue
                    for f in range(4):
                        kw = dict(scale=gain[:, f:f + 1])
                        if shift is not None:
                            kw["bias"] = shift[:, f:f + 1]
                        ins = act.activation(dst[:, f, t * P:(t + 1) * P], b[:, f * P:(f + 1) * P],
                                             ACT.Identity if shift is not None else ACT.Copy, **kw)
                    read(ins)

            def turns_out(items):
                for j in range(0, len(items), 4):
                    b = tile()
                    for i, it in enumerate(items[j:j + 2]):
                        for r0, r1, dst in it["dst"]:
                            ins = act.activation(dst[r0:r1, :], b[r0:r1, i * S:(i + 1) * S], ACT.Copy, scale=it["scale"])
                    read(ins)

            def softmax_heads(jobs):
                for i in range(len(jobs) + 2):
                    if i < len(jobs):
                        for e in range(2):
                            n = (2 * i + e) % NSM
                            seen.more(s_masked)
                            for t, cols in enumerate((slice(0, P), slice(P, 3 * P))):
                                ins = act.activation(sm[:, n, cols], sm[:, n, cols], ACT.Exp, scale=jobs[i]["scale"],
                                                     bias=mx[:, n, t:t + 1], accum_out=rs[:, n, t:t + 1])
                            ins.then_inc(s_exp, 1)
                    if i >= 2:
                        for e in range(2):
                            b = tile()
                            copy_out(pT[:, (2 * (i - 2) + e) % NPT, :], b[:, 0:3 * P])

            def stick_heads(l):
                for i in range(NH // 2 + 1):
                    if i < NH // 2:
                        for h in (2 * i, 2 * i + 1):
                            m = stick_tile0[l] + h
                            act.wait_ge(for_dve.full, m + 1)
                            ab = pT[:, h % NPT, :]
                            link(act.activation(ab, for_dve.banks[m % 4][:, 0:3 * P], ACT.Abs))
                            link(act.activation(ab, ab, ACT.Exp, scale=-1.0))
                            act.activation(ab, ab, ACT.Ln, bias=1.0).then_inc(sb_log, 1)
                    if i >= 1:
                        for h in (2 * i - 2, 2 * i - 1):
                            a = sm[:, h % NSM, :]
                            seen.more(sb_masked)
                            act.activation(a, a, ACT.Exp).then_inc(sb_ready, 1)

            def columns_out(tiles, rows):
                b = tile()
                for i, m in enumerate(tiles):
                    ins = act.activation(pcol[:, m, 0:rows[i]], b[:, i * P:i * P + rows[i]], ACT.Copy)
                link(ins)
                act.sem_inc(for_act.read, 1)
                act.sem_inc(c_exp, 1)

            def late_parameters():
                columns_out((2, 3, 4, 5), (104, 104, 120, 120))
                seen.more(angles)
                act.activation(cs[:, :, :, :].rearrange("p a t f -> p (a t f)"), trig[:, 0:2, :].rearrange("p a f -> p (a f)"),
                               ACT.Sin).then_inc(sines, 1)

            act.preload_act_table_set("natural_log_exp_and_others")
            columns_out((0,), (80,))
            act.activation(c_tmp, pcol[:, 0, 72:80], ACT.Exp, scale=-1.0).then_inc(c_exp, 1)
            columns_out((1,), (72,))

            act.wait_ge(x_loaded, 16)
            if LAYERS1:
                sums_of_parts(x, IN_TURN, False)
            for l in range(LAYERS1):
                if l:
                    sums_of_parts(x, IN_TURN)
                seen.more(evac_dve)
                features_out(mod[:, 8:16], mod[:, 0:8], True)
                for u in range(9):
                    b = tile()
                    c0 = u * ATT_W
                    n = min(ATT_W, ATT - c0)
                    copy_out(proj[:, 0, c0:c0 + n], b[:, 0:n])
                    if l == 0 and u == LATE_AT:
                        late_parameters()
                act.wait_ge(for_act.read, got[0])
                act.sem_inc(evac_act, 1)
                seen.more(evac_dve)
                sums(proj[:, :, 0:QR], 12, QR)
                act.wait_ge(squares, sums_done[0])
                sums(proj[:, :, QR:QR + KVR], 16, KVR)
                for u in range(6):
                    for t in range(T):
                        b = tile()
                        read(act.activation(gates[:, t, u * 512:u * 512 + 512], b[:, :], ACT.Sigmoid))
                act.preload_act_table_set("natural_log_exp_and_others")
                features_out(pcol[:, l, 16:24])
                for u in range(2):
                    b = tile()
                    copy_out(qmla[:, 0, u * UQ_W:(u + 1) * UQ_W], b[:, 0:UQ_W])
                act.wait_ge(for_act.read, got[0])
                act.sem_inc(evac_act, 1)
                turns_out(mla_turns)
                softmax_heads(mla_jobs)
                turns_out(sb_turns)
                stick_heads(l)
                turns_out(moba_turns)
                softmax_heads(moba_jobs)
                features_out(parts=True)
                sums_of_parts(x, BY_HALVES)
                seen.more(evac_dve)
                features_out(mod[:, 24:32], mod[:, 16:24], True)
                for u in range(16):
                    b = tile()
                    dst = hidT[:, 2 * u:2 * u + 2, :].rearrange("p c s -> p (c s)")
                    link(act.activation(dst, b[:, :], ACT.Relu))
                    read(act.activation(dst, dst, ACT.Square))
            if LAYERS1:
                sums_of_parts(x, IN_TURN)
            else:
                late_parameters()
                act.preload_act_table_set("natural_log_exp_and_others")
            for l in range(LAYERS2):
                sums_of_parts(x, IN_TURN, bool(l or LAYERS1))
                features_out(pcol[:, 2 + l, 88:96], parts=True)
                for u in range(6):
                    b = tile()
                    copy_out(proj2[:, 0, u * IN2_W:(u + 1) * IN2_W], b[:, 0:IN2_W])
                act.wait_ge(for_act.read, got[0])
                act.sem_inc(evac_act, 1)
                seen.more(fox_in)
                link(act.activation(fox[:, 1, :], fox[:, 0, :], ACT.Abs))
                link(act.activation(fox[:, 1, :], fox[:, 1, :], ACT.Exp, scale=-1.0))
                act.activation(fox[:, 1, :], fox[:, 1, :], ACT.Ln, bias=1.0).then_inc(fox_log, 1)
                seen.more(nsa_in)
                act.activation(gn[:, 1, :], gn[:, 0, :], ACT.Exp, scale=-1.0).then_inc(nsa_exp, 1)
                turns_out(nsa_turns + dil_turns)
                b = tile()
                for a in range(2):
                    ins = act.activation(gel[:, a * CMP_H:(a + 1) * CMP_H], b[HD * a:HD * a + GRP * NCMP, 0:CMP_H],
                                         ACT.Gelu_apprx_tanh)
                read(ins)
                act.preload_act_table_set("natural_log_exp_and_others")
                turns_out(fox_turns)
                b = tile()
                copy_out(hT[:, :, :], b[:, 0:P].rearrange("p (a n) -> p a n", n=32)[:, :, 0:GRP * NCMP])
                b = tile()
                act.wait_ge(zeroed, 1 + 2 * (l + 1))
                act.activation(kcT[:, :], b[:, 0:NCMP], ACT.Copy)
                copy_out(vcm[0:NCMP, :, :], b[0:NCMP, HD:3 * HD].rearrange("p (g d) -> p g d", g=GRP))
                seen.more(pc_in)
                act.activation(pc2[:, :, :, :], pc[:, :, :, :], ACT.Exp).then_inc(pc_exp, 1)
                for h2 in range(NSA // 2):
                    b = tile()
                    copy_out(pcT[0:NCMP, 2 * h2:2 * h2 + 2, :], b[0:NCMP, :].rearrange("p (h s) -> p h s", s=S))
                softmax_heads(second_jobs)
                sums_of_parts(wide, BY_HALVES)
                sums_of_parts(x, IN_TURN)
                features_out(pcol[:, 2 + l, 96:104], parts=True)
                w2c, bc = pcol[:, 4 + l, 0:44], pcol[:, 4 + l, 44:88]
                for j in range(CH // 2 + 1):
                    if j < CH // 2:
                        if j >= 2:
                            seen.more(conv_done)
                        for hf in range(2):
                            m = conv_tile0[l] + 2 * j + hf
                            act.wait_ge(for_dve.full, m + 1)
                            b = for_dve.banks[m % 4]
                            for f in range(2):
                                ch = hf * CH + 2 * j + f
                                ins = act.activation(cv[:, j % 2, hf, f * S:(f + 1) * S], b[:, f * S:(f + 1) * S],
                                                     ACT.Identity, scale=w2c[:, ch:ch + 1], bias=bc[:, ch:ch + 1])
                            ins.then_inc(conv_base, 1)
                    if j >= 1:
                        seen.more(silu_in)
                        a = cv[:, (j - 1) % 2, 0, :]
                        act.activation(a, a, ACT.Silu).then_inc(silu_out, 1)
                seen.more(conv_done, 2)
                sums_of_parts(wide, IN_TURN)

        @block.vector
        def _(dve):
            seen = Seen(dve)
            chain = [0]
            got = {}

            def link(ins):
                chain[0] += 1
                ins.then_inc(dve_chain, 1)
                dve.wait_ge(dve_chain, chain[0])

            def tile(r):
                n = got.get(id(r), 0)
                got[id(r)] = n + 1
                dve.wait_ge(r.full, n + 1)
                return r.banks[n % len(r.banks)]

            def read(r, ins):
                ins.then_inc(r.read, 1)

            def stored(r):
                dve.wait_ge(r.read, got[id(r)])

            def scale_tokens(src=x):
                for t in range(T):
                    seen.more(rstd_ready)
                    dve.tensor_scalar(wide[:, t, :], src[:, t, :], stat[:, 8 + t:9 + t], None, ALU.mult).then_inc(scaled, 1)

            cut = iter(split_units)
            split_features = iter(feature_tiles)

            def split_quarter(it):
                if it["q"] >= QUARTERS:
                    dve.wait_ge(quarter_used, it["q"] - QUARTERS + 1)
                dve.wait_ge(*it["loaded"])
                ins = dve.tensor_copy(it["high"], it["raw"])
                if it["owner"] == "pool":
                    ins.then_inc(high_ready, 1)
                    return
                link(ins)
                dve.tensor_tensor(it["low"], it["raw"], it["high"].bitcast(F32), ALU.subtract).then_inc(low_dve, 1)

            def split_unit(between=None):
                for j, it in enumerate(next(cut)):
                    split_quarter(it)
                    if between is not None:
                        between(j)

            begun = []

            def first_quarters(n):
                if not begun:
                    begun.extend(next(cut))
                for _ in range(n):
                    split_quarter(begun.pop(0))

            def split_hidden(c0, chunks, made_by, count):
                dve.wait_ge(made_by, count)
                n = min(4, chunks - c0)
                high_, low_ = [hid_parts[:, c0 // 4 % 2, part, 0:n, :] for part in range(2)]
                src = hidT[:, c0:c0 + n, :]
                link(dve.tensor_copy(high_, src))
                dve.tensor_tensor(low_, src, high_.bitcast(F32), ALU.subtract).then_inc(hid_split, 1)

            def split_tokens(t):
                cols = slice(t * P, (t + 1) * P)
                dve.tensor_copy(featT_r[:, 0:4, cols], featF[:, 0:4, cols]).then_inc(feat_high, 1)
                link(dve.tensor_copy(featT_r[:, 4:8, cols], featF[:, 4:8, cols]))
                dve.tensor_tensor(featL[:, 4:8, cols], featF[:, 4:8, cols], featT_r[:, 4:8, cols].bitcast(F32),
                                  ALU.subtract).then_inc(feat_dve, 1)

            def features_out(gain=None, shift=None, parts=False):
                out_ = featF if parts else featT
                for t in range(T):
                    cols = slice(t * P, (t + 1) * P)
                    b = tile(for_dve)
                    for f in range(4, 8):
                        src, dst = b[:, (f - 4) * P:(f - 3) * P], out_[:, f, cols]
                        if gain is None:
                            src, dst = b[:, :].rearrange("p (c s) -> p c s", c=4), out_[:, 4:8, cols]
                            ins = dve.tensor_copy(dst, src)
                            break
                        if shift is None:
                            ins = dve.tensor_scalar(dst, src, gain[:, f:f + 1], None, ALU.mult)
                        else:
                            ins = dve.tensor_scalar(dst, src, gain[:, f:f + 1], shift[:, f:f + 1], ALU.mult, ALU.add)
                    read(for_dve, ins)
                    if parts:
                        stored(for_dve)
                        dve.wait_ge(for_act.read, next(split_features))
                        split_tokens(t)

            def turns_out(items):
                for j in range(2, len(items), 4):
                    b = tile(for_dve)
                    for i, it in enumerate(items[j:j + 2]):
                        for r0, r1, dst in it["dst"]:
                            ins = dve.tensor_scalar(dst[r0:r1, :], b[r0:r1, i * S:(i + 1) * S], it["scale"], None, ALU.mult)
                    read(for_dve, ins)

            ada_units = units_for("dve")

            def ada_rows(u):
                it, acc = next(ada_units), ada[:, u % 2, :]

                def step(j):
                    if j == 0:
                        dve.wait_ge(w_loaded[it["slot"]], it["loaded"])
                    for c in (2 * j, 2 * j + 1):
                        row, by = it["view"][:, c, :], c_act[:, c:c + 1]
                        if c == 0:
                            link(dve.tensor_scalar(acc, row, by, None, ALU.mult))
                        else:
                            link(dve.scalar_tensor_tensor(out=acc, in0=row, scalar=by, in1=acc, op0=ALU.mult, op1=ALU.add))
                    if j == 3:
                        dve.sem_inc(ada_used, 1)
                        dve.sem_inc(ada_ready, 1)
                return step

            def modulation_out(l, u):
                b = tile(for_dve)
                v, hf = u // 2, u % 2
                if v % 3 == 2:
                    dst = rowbc[:, v // 3, hf * 512:hf * 512 + 512]
                    read(for_dve, dve.tensor_tensor(dst, b[:, :], dst, ALU.add))
                    return
                at = 16 * (v // 3) + 8 * (v % 3) + 4 * hf
                link(dve.tensor_tensor(mod[:, at:at + 4], b[:, 0:4], pcol[:, l, 24 + 4 * u:28 + 4 * u], ALU.add))
                dve.sem_inc(for_dve.read, 1)
                if v % 3 == 1:
                    g = pcol[:, l, 8 * (v // 3) + 4 * hf:8 * (v // 3) + 4 * hf + 4]
                    link(dve.scalar_tensor_tensor(out=mod[:, at:at + 4], in0=mod[:, at:at + 4], scalar=1.0, in1=g,
                                                  op0=ALU.add, op1=ALU.mult))
                    if hf:
                        dve.sem_inc(evac_dve, 1)

            def rope(x1, x2, table0, width, dims):
                t0, t1, heads = dims
                shape = list(x1.shape)

                def trig_of(a):
                    v = cs[:, a, t0:t1, table0:table0 + width]
                    return v.unsqueeze(2).to_broadcast([P, t1 - t0, heads, width]) if len(shape) == 4 else \
                        v.rearrange("p t f -> p (t f)").unsqueeze(1).to_broadcast([P, heads, width])

                cos, sin = trig_of(0), trig_of(1)

                def scratch(a):
                    v = rope_t[:, a, 0:(t1 - t0) * heads * width]
                    return v.rearrange("p (t h f) -> p t h f", t=t1 - t0, h=heads) if len(shape) == 4 else \
                        v.rearrange("p (h f) -> p h f", h=heads)

                dve.tensor_tensor(scratch(0), x1, cos, ALU.mult)
                dve.tensor_tensor(scratch(1), x2, sin, ALU.mult)
                dve.tensor_tensor(scratch(2), x1, sin, ALU.mult)
                link(dve.tensor_tensor(scratch(3), x2, cos, ALU.mult))
                dve.tensor_tensor(x1, scratch(0), scratch(1), ALU.subtract)
                link(dve.tensor_tensor(x2, scratch(2), scratch(3), ALU.add))

            def softmax_heads(jobs):
                both = ((0, 0, P), (1, P, 3 * P))
                for i in range(len(jobs) + 4):
                    if i < len(jobs):
                        j = jobs[i]
                        for e in range(2):
                            n = (2 * i + e) % NSM
                            b = tile(for_dve)
                            for t, a, z in both:
                                ins = dve.tensor_tensor_reduce(out=sm[:, n, a:z], in0=b[:, a:z],
                                                               in1=cst[:, j["mask"] + a:j["mask"] + z],
                                                               scale=1.0, scalar=-3e38, op0=ALU.add, op1=ALU.max,
                                                               accum_out=mx[:, n, t:t + 1])
                            link(ins)
                            dve.sem_inc(for_dve.read, 1)
                            dve.tensor_scalar(mx[:, n, :], mx[:, n, :], -j["scale"], None, ALU.mult).then_inc(s_masked, 1)
                    if 1 <= i < len(jobs) + 1:
                        j = jobs[i - 1]
                        for e in range(2):
                            n = (2 * (i - 1) + e) % NSM
                            seen.more(s_exp)
                            if j["weight"]:
                                for t, a, z in both:
                                    ins = dve.tensor_tensor_reduce(out=sm[:, n, a:z], in0=sm[:, n, a:z],
                                                                   in1=cst[:, C_DW + a:C_DW + z],
                                                                   scale=1.0, scalar=0.0, op0=ALU.mult, op1=ALU.add,
                                                                   accum_out=rs[:, n, t:t + 1])
                                link(ins)
                            link(dve.reciprocal(rs[:, n, :], rs[:, n, :]))
                            gate = j["heads"][e]["gate"]
                            if gate is not None:
                                g = gn[:, 1, :].rearrange("p (t n) -> p t n", t=T)[:, :, gate]
                                link(dve.tensor_tensor(rs[:, n, :], rs[:, n, :], g, ALU.mult))
                            for t, a, z in both:
                                ins = dve.tensor_scalar(sm[:, n, a:z], sm[:, n, a:z], rs[:, n, t:t + 1], None, ALU.mult)
                            ins.then_inc(p_ready, 1)
                    if i >= 4 and jobs[i - 4]["last"]:
                        b = tile(outputs)
                        read(outputs, dve.tensor_copy(oT[:, jobs[i - 4]["chunk"], :], b[:, 0:S]))

            def stick_heads():
                z = {}
                for i in range(NH // 2 + 3):
                    if i < NH // 2:
                        for h in (2 * i, 2 * i + 1):
                            z[h] = tile(for_dve)
                            seen.more(sb_log)
                            dve.scalar_tensor_tensor(out=sm[:, h % NSM, :], in0=z[h][:, 0:3 * P], scalar=0.0,
                                                     in1=pT[:, h % NPT, :], op0=ALU.max, op1=ALU.add).then_inc(sb_raw, 1)
                    if 1 <= i < NH // 2 + 1:
                        for h in (2 * i - 2, 2 * i - 1):
                            seen.more(sb_total)
                            link(dve.tensor_tensor(sm[:, h % NSM, :], z[h][:, 0:3 * P], cst[:, C_SMASK:C_SMASK + 3 * P], ALU.add))
                            dve.sem_inc(for_dve.read, 1)
                            dve.sem_inc(sb_masked, 1)
                    if i >= 3:
                        b = tile(outputs)
                        read(outputs, dve.tensor_copy(oT[:, 4 + i - 3, :], b[:, 0:S]))

            def late_parameters():
                b = tile(for_dve)
                link(dve.tensor_copy(posc[:, :], b[:, 0:4]))
                dve.sem_inc(for_dve.read, 1)
                for t in range(T):
                    dve.tensor_scalar(trig[:, 2, 32 * t:32 * t + 24], cst[:, C_INV:C_INV + 24], posc[:, t:t + 1], None, ALU.mult)
                    link(dve.tensor_scalar(trig[:, 2, 32 * t + 24:32 * t + 32], cst[:, C_INV + 24:C_INV + 32],
                                           posc[:, 2 + t:3 + t], None, ALU.mult))
                turnsn = tiny[:, 16:80]
                for a, ahead in ((1, 0.0), (0, 0.25)):
                    link(dve.tensor_scalar(turnsn, trig[:, 2, :], 1 / TWO_PI, ahead, ALU.mult, ALU.add))
                    link(dve.tensor_scalar(turnsn, turnsn, ROUNDER, None, ALU.add))
                    link(dve.tensor_scalar(turnsn, turnsn, -ROUNDER, None, ALU.add))
                    link(dve.scalar_tensor_tensor(out=trig[:, a, :], in0=turnsn, scalar=-PI_A, in1=trig[:, 2, :], op0=ALU.mult, op1=ALU.add))
                    for part in (PI_B, PI_C):
                        link(dve.scalar_tensor_tensor(out=trig[:, a, :], in0=turnsn, scalar=-part, in1=trig[:, a, :], op0=ALU.mult, op1=ALU.add))
                    if ahead:
                        link(dve.tensor_scalar(trig[:, a, :], trig[:, a, :], TWO_PI * ahead, None, ALU.add))
                    link(dve.tensor_scalar(trig[:, a, :], trig[:, a, :], PI_SAFE, -PI_SAFE, ALU.min, ALU.max))
                dve.sem_inc(angles, 1)
                seen.more(c_exp)
                seen.more(sines)

            def cast_positions():
                dve.wait_ge(masks_loaded, 16)
                dve.wait_ge(late_loaded, N_LATE)
                dve.wait_ge(small_loaded, N_POOL_ROWS)
                dve.tensor_copy(posf[:, :], posi[:, :]).then_inc(pos_cast, 1)

            seen.more(c_exp, 2)
            link(dve.tensor_scalar(c_tmp, c_tmp, 1.0, None, ALU.add))
            link(dve.reciprocal(c_tmp, c_tmp))
            link(dve.tensor_tensor(c_act, c_tmp, pcol[:, 0, 72:80], ALU.mult))

            for l in range(LAYERS1):
                if l == 0:
                    for u in range(4):
                        step = ada_rows(u)
                        for j in range(4):
                            step(j)
                        if u:
                            modulation_out(l, u - 1)
                    modulation_out(l, 3)
                    seen.more(c_exp)
                    dve.wait_ge(x_loaded, 16)
                first_quarters(1)
                scale_tokens()
                first_quarters(1)
                features_out(mod[:, 8:16], mod[:, 0:8], True)
                first_quarters(2)
                seen.more(bc_loaded, 32)

                def beside(u):
                    step = ada_rows(ADA_LATE[u]) if u in ADA_LATE else None
                    if u < 14:
                        split_unit(step)

                for u in range(9):
                    beside(u)
                    if l == 0 and u == LATE_AT - 1:
                        cast_positions()
                    b = tile(for_dve)
                    c0 = u * ATT_W
                    n = min(ATT_W, ATT - c0)
                    read(for_dve, dve.tensor_copy(proj[:, 1, c0:c0 + n], b[:, 0:n]))
                    if u == 8:
                        stored(for_dve)
                        dve.sem_inc(evac_dve, 1)
                    if u - 1 in ADA_LATE:
                        modulation_out(l, ADA_LATE[u - 1])
                    if l == 0 and u == LATE_AT:
                        late_parameters()
                beside(9)
                modulation_out(l, ADA_LATE[8])
                seen.more(evac_act)
                seen.more(rstd_ready, 2)
                for t in range(T):
                    dve.tensor_scalar(wide[:, t, 0:QR], proj[:, t, 0:QR], stat[:, 14 + t:15 + t], None, ALU.mult)
                    dve.tensor_scalar(wide[:, t, QR:D], proj[:, t, QR:QR + KVR], stat[:, 18 + t:19 + t], None, ALU.mult)\
                       .then_inc(scaled, 1)
                kpe = proj[:, :, QR + KVR:SB0].rearrange("p t (h e) -> p t h e", h=1)
                rope(kpe[:, :, :, 0:16], kpe[:, :, :, 16:32], 0, 16, (0, T, 1))
                qk = proj[:, :, MB0:MB0 + 2 * NH * HD].rearrange("p t (h e) -> p t h e", e=HD)
                rope(qk[:, :, :, 0:8], qk[:, :, :, 8:16], 16, 8, (0, T, 2 * NH))
                for u in range(10, 15):
                    beside(u)
                    if u - 1 in ADA_LATE:
                        modulation_out(l, ADA_LATE[u - 1])
                features_out(pcol[:, l, 16:24])
                for t in range(T):
                    dve.tensor_copy(k_mla[:, t, :, NOPE:QK],
                                    proj[:, t, QR + KVR:SB0].unsqueeze(1).to_broadcast([P, NH, ROPE]))
                for u in range(2):
                    b = tile(for_dve)
                    read(for_dve, dve.tensor_copy(qmla[:, 1, u * UQ_W:(u + 1) * UQ_W], b[:, 0:UQ_W]))
                for hf in range(2):
                    for t in range(T):
                        b = tile(for_dve)
                        kv = b[:, :].rearrange("p (h e) -> p h e", e=NOPE + HD)
                        dve.tensor_copy(k_mla[:, t, 4 * hf:4 * hf + 4, 0:NOPE], kv[:, :, 0:NOPE])
                        read(for_dve, dve.tensor_copy(
                            v_mla[:, t, 4 * hf * HD:4 * (hf + 1) * HD].rearrange("p (h e) -> p h e", e=HD), kv[:, :, NOPE:]))
                stored(for_dve)
                seen.more(evac_act)
                qh = qmla.rearrange("p t (h e) -> p t h e", e=QK)
                rope(qh[:, :, :, NOPE:NOPE + 16], qh[:, :, :, NOPE + 16:QK], 0, 16, (0, T, NH))
                dve.sem_inc(ready_dve, 1)
                turns_out(mla_turns)
                softmax_heads(mla_jobs)
                turns_out(sb_turns)
                stick_heads()
                turns_out(moba_turns)
                softmax_heads(moba_jobs)
                dve.wait_ge(outputs.read, got[id(outputs)])
                tmp = big[:, 0:D]
                k = 0
                for br in range(3):
                    if br == 2:
                        first_quarters(2)
                    for t in range(T):
                        for hf in range(2):
                            b = tile(for_dve)
                            g = gates[:, t, br * D + hf * 512:br * D + hf * 512 + 512]
                            dst = wide[:, t, hf * 512:hf * 512 + 512]
                            if br == 0:
                                read(for_dve, dve.tensor_tensor(dst, b[:, :], g, ALU.mult))
                                continue
                            tm = tmp[:, 512 * (k % 2):512 * (k % 2) + 512]
                            k += 1
                            read(for_dve, dve.tensor_tensor(tm, b[:, :], g, ALU.mult))
                            stored(for_dve)
                            link(dve.tensor_tensor(dst, dst, tm, ALU.add))
                        if br == 2:
                            dve.sem_inc(merged, 1)
                features_out(parts=True)
                first_quarters(2)
                split_unit()

                def add_gated(g, order):
                    for k, (r, t, hf) in enumerate(order):
                        b = tile(r)
                        cols = slice(hf * 512, hf * 512 + 512)
                        tm = gf[:, 512 * (k % 2):512 * (k % 2) + 512]
                        read(r, dve.tensor_tensor(tm, b[:, :], rowbc[:, g, cols], ALU.mult))
                        stored(r)
                        dve.tensor_tensor(x[:, t, cols], x[:, t, cols], tm, ALU.add).then_inc(part_ready, 1)
                    dve.wait_ge(part_ready, PARTS1 * l + 4 * g + 4)

                add_gated(0, [(for_dve, t, hf) for hf in range(2) for t in range(T)])
                first_quarters(1)
                scale_tokens()
                first_quarters(1)
                features_out(mod[:, 24:32], mod[:, 16:24], True)
                first_quarters(2)

                def hidden(g):
                    split_hidden(4 * g, FF1 // P, for_act.read, hid_tile0[l] + 2 * g + 2)

                for u in range(8):
                    step = ada_rows(u) if l + 1 < LAYERS1 and u < 4 else None
                    if u == 7:
                        hidden(0)
                    split_unit(step)
                    if l + 1 < LAYERS1 and 1 <= u < 5:
                        modulation_out(l + 1, u - 1)
                for g in range(1, 8):
                    split_unit(lambda j: hidden(g) if j == 0 else None)
                add_gated(1, [(for_dve, 0, 0), (for_dve, 0, 1), (outputs, 1, 0), (outputs, 1, 1)])
            if LAYERS1:
                seen.more(bc_loaded, 16)
                for t in range(T):
                    seen.more(rstd_ready)
                    for hf in range(2):
                        cols = slice(hf * 512, hf * 512 + 512)
                        dve.scalar_tensor_tensor(out=x[:, t, cols], in0=x[:, t, cols], scalar=stat[:, 8 + t:9 + t],
                                                 in1=rowbc[:, 0, cols], op0=ALU.mult, op1=ALU.mult).then_inc(part_ready, 1)
                dve.wait_ge(part_ready, x1)

            else:
                seen.more(c_exp)
                cast_positions()
                late_parameters()
                dve.wait_ge(x_loaded, 16)

            parts = [x1]
            for l in range(LAYERS2):
                first_quarters(1)
                scale_tokens()
                first_quarters(1)
                features_out(pcol[:, 2 + l, 88:96], parts=True)
                first_quarters(2)
                for u in range(6):
                    if u < 5:
                        split_unit()
                    b = tile(for_dve)
                    read(for_dve, dve.tensor_copy(proj2[:, 1, u * IN2_W:(u + 1) * IN2_W], b[:, 0:IN2_W]))
                stored(for_dve)
                seen.more(evac_act)
                fv = lambda a: fox[:, a, :].rearrange("p (t h) -> p t h", t=T)
                dve.tensor_tensor(fv(0), proj2[:, :, FG:FG + FOX],
                                  small[:, l, 0:FOX].unsqueeze(1).to_broadcast([P, T, FOX]), ALU.add).then_inc(fox_in, 1)
                dve.tensor_tensor(gn[:, 0, :].rearrange("p (t n) -> p t n", t=T), proj2[:, :, NG:NG + 3 * NSA],
                                  small[:, l, FOX:].unsqueeze(1).to_broadcast([P, T, 3 * NSA]), ALU.add).then_inc(nsa_in, 1)
                for base, heads in ((NQ, NSA), (DQ, 2 * DIL)):
                    v = proj2[:, :, base:base + heads * HD].rearrange("p t (h e) -> p t h e", e=HD)
                    rope(v[:, :, :, 0:8], v[:, :, :, 8:16], 24, 8, (0, T, heads))
                for t in range(T):
                    for base in (KC, KS, KW):
                        v = proj2[:, t, base:base + GRP * HD].rearrange("p (h e) -> p h e", e=HD)
                        rope(v[:, :, 0:8], v[:, :, 8:16], 24, 8, (t, t + 1, GRP))
                for t in range(T):
                    for g in range(GRP):
                        q0 = NQ + 4 * g * HD
                        ins = dve.tensor_copy(nq[:, t, :, g, :], proj2[:, t, q0:q0 + 4 * HD].rearrange("p (j d) -> p j d", d=HD))
                link(ins)
                dve.sem_inc(ready_dve, 1)
                seen.more(fox_log)
                dve.scalar_tensor_tensor(out=fox[:, 2, :], in0=fox[:, 0, :], scalar=0.0, in1=fox[:, 1, :],
                                         op0=ALU.min, op1=ALU.subtract).then_inc(fox_lf, 1)
                for t in range(T):
                    heads = lambda c0: proj2[:, t, c0:c0 + FOX * HD].rearrange("p (h e) -> p h e", e=HD)
                    dve.tensor_scalar(faug[:, t, 0, :, 0:HD], heads(FQ), 1 / math.sqrt(HD), None, ALU.mult)
                    dve.tensor_copy(faug[:, t, 1, :, 0:HD], heads(FK))
                    dve.memset(faug[:, t, 0, :, HD + 1], 1.0)
                    dve.memset(faug[:, t, 1, :, HD], 1.0)
                b = tile(for_dve)
                sums_ = b[:, 0:T * FOX].rearrange("p (t h) -> p t h", t=T)
                dve.tensor_copy(faug[:, :, 0, :, HD], sums_)
                link(dve.tensor_scalar(faug[:, :, 1, :, HD + 1], sums_, -1.0, None, ALU.mult))
                dve.sem_inc(for_dve.read, 1)
                dve.sem_inc(ready_dve, 1)
                b = tile(for_dve)
                src = b[:, :].rearrange("p (a s) -> p a s", a=2)
                for g in range(GRP):
                    rows = slice(HD * g, HD * g + HD)
                    dve.tensor_copy(U[0:HD, :, g, :], src[rows, :, :])
                    ins = dve.tensor_copy(U[HD:P, :, g, 0:S - 1], src[rows, :, 1:S])
                link(ins)
                dve.sem_inc(for_dve.read, 1)
                for a in range(2):
                    for g in range(GRP):
                        for ch in range(2):
                            win = U[:, a, g, :].rearrange("p (n r) -> p r n", r=CMP_ST)[:, 0:CMP_ST:2, ch:ch + NCMP]
                            pos = pcol[:, 4 + l, 88 + 16 * a + 8 * ch:88 + 16 * a + 8 * ch + 8]
                            ins = dve.tensor_tensor(awin[:, a, 8 * ch:8 * ch + 8, g * NCMP:(g + 1) * NCMP], win,
                                                    pos.unsqueeze(2).to_broadcast([P, 8, NCMP]), ALU.add)
                ins.then_inc(win_ready, 1)
                turns_out(nsa_turns + dil_turns)
                seen.more(nsa_exp)
                link(dve.tensor_scalar(gn[:, 1, :], gn[:, 1, :], 1.0, None, ALU.add))
                link(dve.reciprocal(gn[:, 1, :], gn[:, 1, :]))
                turns_out(fox_turns)
                for g in range(GRP):
                    b = tile(for_dve)
                    for t in range(T):
                        n = NSA // 2 * NCMP
                        ins = dve.tensor_scalar(pc[:, t, 4 * g:4 * g + 4, :].rearrange("p h n -> p (h n)"),
                                                b[:, t * n:(t + 1) * n], 1 / math.sqrt(HD), None, ALU.mult)
                    read(for_dve, ins)
                stored(for_dve)
                wide_of = lambda v: v.unsqueeze(3).to_broadcast([P, T, NSA, NCMP])
                mask_of = lambda c0: cst[:, c0:c0 + T * NCMP].rearrange("p (t n) -> p t n", t=T).unsqueeze(2)\
                    .to_broadcast([P, T, NSA, NCMP])
                link(dve.tensor_tensor(pc, pc, mask_of(C_CADD), ALU.add))
                link(dve.tensor_reduce(pcs, pc, axis=AX.X, op=ALU.max))
                dve.tensor_tensor(pc, pc, wide_of(pcs), ALU.subtract).then_inc(pc_in, 1)
                seen.more(pc_exp)
                link(dve.tensor_tensor(pc2, pc2, mask_of(C_CMASK), ALU.mult))
                link(dve.tensor_reduce(pcs, pc2, axis=AX.X, op=ALU.add))
                link(dve.tensor_scalar(pcs, pcs, 1e-30, None, ALU.max))
                link(dve.reciprocal(pcs, pcs))
                gc = gn[:, 1, :].rearrange("p (t h b) -> p t h b", t=T, b=3)[:, :, :, 0]
                link(dve.tensor_tensor(pcs, pcs, gc, ALU.mult))
                dve.tensor_tensor(pc, pc2, wide_of(pcs), ALU.mult).then_inc(pc_out, 1)
                softmax_heads(second_jobs)

                def norm_parts(order):
                    for r, t, hf in order:
                        b = tile(r)
                        dve.tensor_copy(wide[:, t, hf * 512:hf * 512 + 512], b[:, :]).then_inc(part_ready, 1)
                        parts[0] += 1
                        dve.wait_ge(part_ready, parts[0])
                        dve.sem_inc(r.read, 1)

                def add_normed(g):
                    if g == 0:
                        seen.more(bc_loaded, 32)
                    for t in range(T):
                        seen.more(rstd_ready)
                        for hf in range(2):
                            cols = slice(hf * 512, hf * 512 + 512)
                            link(dve.scalar_tensor_tensor(out=wide[:, t, cols], in0=wide[:, t, cols],
                                                          scalar=stat[:, 8 + t:9 + t],
                                                          in1=rowbc[:, g, cols], op0=ALU.mult, op1=ALU.mult))
                            dve.tensor_tensor(x[:, t, cols], x[:, t, cols], wide[:, t, cols], ALU.add).then_inc(part_ready, 1)
                            parts[0] += 1
                    dve.wait_ge(part_ready, parts[0])

                split_unit()
                norm_parts([(for_dve, t, hf) for hf in range(2) for t in range(T)])
                add_normed(0)
                scale_tokens()
                features_out(pcol[:, 2 + l, 96:104], parts=True)

                def hidden(g):
                    split_hidden(4 * g, CH, conv_done, CH // 2 * l + min(2 * g + 2, CH // 2))

                w0c, w1c = pcol[:, 2 + l, 0:44], pcol[:, 2 + l, 44:88]
                for j in range(CH // 2 + 1):
                    if j < CH // 2 - 1:
                        split_unit()
                    if j == CH // 2:
                        hidden(0)
                        split_unit()
                    if j < CH // 2:
                        for hf in range(2):
                            b = tile(for_dve)
                            seen.more(conv_base)
                            for f in range(2):
                                ch = hf * CH + 2 * j + f
                                dst = cv[:, j % 2, hf, f * S:(f + 1) * S]
                                link(dve.scalar_tensor_tensor(out=dst[:, 1:S], in0=b[:, f * S:(f + 1) * S - 1], scalar=w1c[:, ch:ch + 1],
                                                              in1=dst[:, 1:S], op0=ALU.mult, op1=ALU.add))
                                link(dve.scalar_tensor_tensor(out=dst[:, 2:S], in0=b[:, f * S:(f + 1) * S - 2], scalar=w0c[:, ch:ch + 1],
                                                              in1=dst[:, 2:S], op0=ALU.mult, op1=ALU.add))
                            dve.sem_inc(for_dve.read, 1)
                            if hf == 0:
                                dve.sem_inc(silu_in, 1)
                    if j >= 1:
                        m = (j - 1) % 2
                        seen.more(silu_out)
                        dst = hidT[:, 2 * (j - 1):2 * j, :].rearrange("p c s -> p (c s)")
                        dve.tensor_tensor(dst, cv[:, m, 0, :], cv[:, m, 1, :], ALU.mult).then_inc(conv_done, 1)
                for g in range(1, (CH + 3) // 4):
                    split_unit(lambda j: hidden(g) if j == 0 else None)
                norm_parts([(for_dve, 0, 0), (for_dve, 0, 1), (outputs, 1, 0), (outputs, 1, 1)])
                add_normed(1)

    return nc


NAMES = ["x", "c", "positions", "w_ada", "b_ada", "norm1_g", "norm2_g", "w_in", "q_norm_g", "w_uq",
         "kv_norm_g", "w_ukv", "w_o_mla", "w_o_sb", "w_o_moba", "w_out", "w_ff1", "w_ff2", "final_norm_g",
         "positions_2", "attn_pre_norm_2", "attn_post_norm_2", "ffn_pre_norm_2", "ffn_post_norm_2",
         "w_in_2", "b_forget_2", "b_nsa_gate_2", "cmp_pos_k_2", "cmp_w1_k_2", "cmp_w2_k_2", "cmp_pos_v_2",
         "cmp_w1_v_2", "cmp_w2_v_2", "w_out_2", "w_up_2", "conv_w_2", "conv_b_2", "w_down_2"]


def kernel(**inputs):
    import concourse.bacc as bacc
    from concourse.bass_utils import run_bass_kernel_spmd

    nc = bacc.Bacc("TRN2", target_bir_lowering=False, num_devices=1)
    arrays, args = {}, []
    for name in NAMES:
        a = np.ascontiguousarray(inputs[name])
        arrays[f"in_{name}"] = a
        args.append(nc.dram_tensor(f"in_{name}", a.shape, mybir.dt.from_np(a.dtype), kind="ExternalInput").ap())
    table = constants()
    arrays["table"] = table
    args.append(nc.dram_tensor("table", table.shape, F32, kind="ExternalInput").ap())
    args.append(nc.dram_tensor("out_0", (1, S, D), F32, kind="ExternalOutput").ap())
    two_blocks(nc, *args)
    r = run_bass_kernel_spmd(nc, [arrays], core_ids=[0])
    return r.results[0]["out_0"]
```
